# Optimizing a Trainium2 kernel written in Bass

```python
import jax, jax.numpy as jnp
from jax import lax
import numpy as np
import math

D_MODEL = 1024
BATCH = 1
SEQ = 512
DEPTH = 2

HEAD_DIM = 64
ROPE_THETA = 10000.0
NORM_EPS = 1e-6
BLOCK = 128

A_HEADS = 6
IDX_HEADS = 8
IDX_DIM = 64
TOPK_MAX = 256

B_GROUPS = ((128, 1), (512, 4), (2048, 16))
B_HEADS_PER_GROUP = 4
B_HEADS = B_HEADS_PER_GROUP * len(B_GROUPS)

C_HEADS = 8
C_KV_HEADS = 2
C_WINDOW = 128

N_BRANCHES = 3
D_FF = 4 * D_MODEL

IN_WIDTHS = (A_HEADS * HEAD_DIM, HEAD_DIM, HEAD_DIM,
             IDX_HEADS * IDX_DIM, IDX_DIM, IDX_HEADS,
             B_HEADS * HEAD_DIM, B_HEADS * HEAD_DIM, B_HEADS * HEAD_DIM,
             C_HEADS * HEAD_DIM, C_KV_HEADS * HEAD_DIM, C_KV_HEADS * HEAD_DIM,
             N_BRANCHES * D_MODEL)
IN_WIDTH = sum(IN_WIDTHS)


def rmsnorm(x, g):
    xf = x.astype(jnp.float32)
    y = xf * lax.rsqrt(jnp.mean(xf * xf, axis=-1, keepdims=True) + NORM_EPS)
    return (y * g.astype(jnp.float32)).astype(x.dtype)

def rope(x, pos):
    half = x.shape[-1] // 2
    inv = ROPE_THETA ** (-jnp.arange(half, dtype=jnp.float32) / half)
    ang = pos.astype(jnp.float32)[..., None] * inv
    cos = jnp.cos(ang)[:, :, None, :].astype(x.dtype)
    sin = jnp.sin(ang)[:, :, None, :].astype(x.dtype)
    x1, x2 = x[..., :half], x[..., half:]
    return jnp.concatenate([x1 * cos - x2 * sin, x2 * cos + x1 * sin], axis=-1)

def split_columns(z):
    parts, off = [], 0
    for w in IN_WIDTHS:
        parts.append(z[..., off:off + w])
        off += w
    return parts

def over_query_blocks(fn, seq_len):
    starts = jnp.arange(seq_len // BLOCK, dtype=jnp.int32) * BLOCK
    out = lax.map(fn, starts)
    out = jnp.moveaxis(out, 0, 1)
    return out.reshape(out.shape[0], seq_len, *out.shape[3:])

def dsa_attention(q, k, v, iq, ik, iw):
    L = q.shape[1]
    topk = min(TOPK_MAX, L // 4)
    scale = HEAD_DIM ** -0.5
    idx_scale = IDX_DIM ** -0.5
    s_all = jnp.arange(L)

    def block(t0):
        t = t0 + jnp.arange(BLOCK)
        qb = lax.dynamic_slice_in_dim(q, t0, BLOCK, 1)
        iqb = lax.dynamic_slice_in_dim(iq, t0, BLOCK, 1)
        iwb = lax.dynamic_slice_in_dim(iw, t0, BLOCK, 1).astype(jnp.float32)
        rel = jax.nn.relu(jnp.einsum('bqhd,bsd->bqhs', iqb, ik).astype(jnp.float32) * idx_scale)
        score = jnp.einsum('bqh,bqhs->bqs', iwb, rel)
        causal = s_all[None, :] <= t[:, None]
        score = jnp.where(causal[None], score, -jnp.inf)
        _, idx = lax.top_k(score, topk)
        ks = jax.vmap(lambda kk, ii: kk[ii])(k, idx)
        vs = jax.vmap(lambda vv, ii: vv[ii])(v, idx)
        valid = idx <= t[None, :, None]
        logits = jnp.einsum('bqhd,bqkd->bqhk', qb, ks).astype(jnp.float32) * scale
        logits = jnp.where(valid[:, :, None, :], logits, -jnp.inf)
        p = jax.nn.softmax(logits, axis=-1)
        return jnp.einsum('bqhk,bqkd->bqhd', p.astype(vs.dtype), vs)

    return over_query_blocks(block, L)

def dilated_attention(q, k, v):
    L = q.shape[1]
    scale = HEAD_DIM ** -0.5
    hg = B_HEADS_PER_GROUP
    qs = [q[:, :, g * hg:(g + 1) * hg] for g in range(len(B_GROUPS))]
    kss = [k[:, :, g * hg:(g + 1) * hg] for g in range(len(B_GROUPS))]
    vss = [v[:, :, g * hg:(g + 1) * hg] for g in range(len(B_GROUPS))]

    def block(t0):
        t = t0 + jnp.arange(BLOCK)
        outs, lses = [], []
        for g, (window, dil) in enumerate(B_GROUPS):
            qb = lax.dynamic_slice_in_dim(qs[g], t0, BLOCK, 1)
            pos = t[:, None] - dil * jnp.arange(window // dil + 1)[None, :]
            valid = pos >= 0
            pos_c = jnp.maximum(pos, 0)
            kg = kss[g][:, pos_c]
            vg = vss[g][:, pos_c]
            logits = jnp.einsum('bqhd,bqkhd->bqhk', qb, kg).astype(jnp.float32) * scale
            logits = jnp.where(valid[None, :, None, :], logits, -jnp.inf)
            m = jnp.max(logits, axis=-1, keepdims=True)
            e = jnp.exp(logits - m)
            den = jnp.sum(e, axis=-1)
            o = jnp.einsum('bqhk,bqkhd->bqhd', (e / den[..., None]).astype(vg.dtype), vg)
            outs.append(o)
            lses.append(m[..., 0] + jnp.log(den))
        alpha = jax.nn.softmax(jnp.stack(lses, 0), axis=0)
        return jnp.einsum('gbqh,gbqhd->bqhd', alpha.astype(outs[0].dtype), jnp.stack(outs, 0))

    return over_query_blocks(block, L)

def sink_window_attention(q, k, v, sinks):
    Bsz, L = q.shape[0], q.shape[1]
    grp = C_HEADS // C_KV_HEADS
    scale = HEAD_DIM ** -0.5
    pad = ((0, 0), (BLOCK, 0), (0, 0), (0, 0))
    kp = jnp.pad(k, pad)
    vp = jnp.pad(v, pad)
    qg = q.reshape(Bsz, L, C_KV_HEADS, grp, HEAD_DIM)
    sink = sinks.astype(jnp.float32).reshape(C_KV_HEADS, grp)[:, :, None, None]

    def block(t0):
        t = t0 + jnp.arange(BLOCK)
        s = t0 - BLOCK + jnp.arange(2 * BLOCK)
        qb = lax.dynamic_slice_in_dim(qg, t0, BLOCK, 1)
        kb = lax.dynamic_slice_in_dim(kp, t0, 2 * BLOCK, 1)
        vb = lax.dynamic_slice_in_dim(vp, t0, 2 * BLOCK, 1)
        mask = (s[None, :] <= t[:, None]) & (s[None, :] > t[:, None] - C_WINDOW) & (s[None, :] >= 0)
        logits = jnp.einsum('bqkgd,bskd->bkgqs', qb, kb).astype(jnp.float32) * scale
        logits = jnp.where(mask, logits, -jnp.inf)
        m = jnp.maximum(jnp.max(logits, axis=-1, keepdims=True), sink)
        e = jnp.exp(logits - m)
        den = jnp.sum(e, axis=-1, keepdims=True) + jnp.exp(sink - m)
        p = (e / den).astype(vb.dtype)
        o = jnp.einsum('bkgqs,bskd->bqkgd', p, vb)
        return o.reshape(Bsz, BLOCK, C_HEADS, HEAD_DIM)

    return over_query_blocks(block, L)

def hybrid_mixer(u, pos, w_in, idx_k_norm, sinks, w_a, w_b, w_c, w_o):
    Bsz, L, _ = u.shape
    (aq, ak, av, iq, ik, iw, bq, bk, bv, cq, ck, cv, gates) = split_columns(u @ w_in)
    qa = rope(aq.reshape(Bsz, L, A_HEADS, HEAD_DIM), pos)
    ka = rope(ak[:, :, None, :], pos)[:, :, 0]
    iqr = rope(iq.reshape(Bsz, L, IDX_HEADS, IDX_DIM), pos)
    ikr = rope(rmsnorm(ik, idx_k_norm)[:, :, None, :], pos)[:, :, 0]
    o_a = dsa_attention(qa, ka, av, iqr, ikr, iw * IDX_HEADS ** -0.5)
    o_b = dilated_attention(rope(bq.reshape(Bsz, L, B_HEADS, HEAD_DIM), pos),
                            rope(bk.reshape(Bsz, L, B_HEADS, HEAD_DIM), pos),
                            bv.reshape(Bsz, L, B_HEADS, HEAD_DIM))
    o_c = sink_window_attention(rope(cq.reshape(Bsz, L, C_HEADS, HEAD_DIM), pos),
                                rope(ck.reshape(Bsz, L, C_KV_HEADS, HEAD_DIM), pos),
                                cv.reshape(Bsz, L, C_KV_HEADS, HEAD_DIM), sinks)
    g = jax.nn.sigmoid(gates.reshape(Bsz, L, N_BRANCHES, D_MODEL))
    merged = (g[:, :, 0] * (o_a.reshape(Bsz, L, -1) @ w_a)
              + g[:, :, 1] * (o_b.reshape(Bsz, L, -1) @ w_b)
              + g[:, :, 2] * (o_c.reshape(Bsz, L, -1) @ w_c))
    return merged @ w_o

def first_inputs(seed: int = 0) -> dict:
    key = jax.random.key(seed)
    ks = jax.random.split(key, 15)

    def normal(k, shape, scale):
        return jax.random.normal(k, shape, jnp.float32) * scale

    def gain(k, shape):
        return 1.0 + 0.05 * jax.random.normal(k, shape, jnp.float32)

    x = normal(ks[0], (BATCH, SEQ, D_MODEL), 1.0)
    positions = jnp.tile(jnp.arange(SEQ, dtype=jnp.int32)[None, :], (BATCH, 1))
    return {
        "x": x,
        "positions": positions,
        "attn_norm": gain(ks[1], (DEPTH, D_MODEL)),
        "w_in": normal(ks[2], (DEPTH, D_MODEL, IN_WIDTH), D_MODEL ** -0.5),
        "idx_k_norm": gain(ks[3], (DEPTH, IDX_DIM)),
        "sinks": normal(ks[4], (DEPTH, C_HEADS), 0.5),
        "w_a": normal(ks[5], (DEPTH, A_HEADS * HEAD_DIM, D_MODEL), (A_HEADS * HEAD_DIM) ** -0.5),
        "w_b": normal(ks[6], (DEPTH, B_HEADS_PER_GROUP * HEAD_DIM, D_MODEL), (B_HEADS_PER_GROUP * HEAD_DIM) ** -0.5),
        "w_c": normal(ks[7], (DEPTH, C_HEADS * HEAD_DIM, D_MODEL), (C_HEADS * HEAD_DIM) ** -0.5),
        "w_o": normal(ks[8], (DEPTH, D_MODEL, D_MODEL), D_MODEL ** -0.5),
        "mlp_norm": gain(ks[9], (DEPTH, D_MODEL)),
        "w_up": normal(ks[10], (DEPTH, D_MODEL, D_FF), D_MODEL ** -0.5),
        "w_down": normal(ks[11], (DEPTH, D_FF, D_MODEL), D_FF ** -0.5),
        "final_norm": gain(ks[12], (D_MODEL,)),
    }

def first_block(x, positions, attn_norm, w_in, idx_k_norm, sinks, w_a, w_b, w_c, w_o,
              mlp_norm, w_up, w_down, final_norm):
    h = x
    for l in range(DEPTH):
        u = rmsnorm(h, attn_norm[l])
        h = h + hybrid_mixer(u, positions, w_in[l], idx_k_norm[l], sinks[l],
                             w_a[l], w_b[l], w_c[l], w_o[l])
        u = rmsnorm(h, mlp_norm[l])
        h = h + jnp.square(jax.nn.relu(u @ w_up[l])) @ w_down[l]
    return rmsnorm(h, final_norm)


SB_HEADS = 4
MLA_HEADS = 4
RWKV_HEADS = 8
SB_WIDTH = SB_HEADS * HEAD_DIM
MLA_WIDTH = MLA_HEADS * HEAD_DIM
RWKV_WIDTH = RWKV_HEADS * HEAD_DIM
MIX_WIDTH = SB_WIDTH + MLA_WIDTH + RWKV_WIDTH

MLA_Q_LORA = 192
MLA_KV_LORA = 128
MLA_NOPE_DIM = 64
MLA_ROPE_DIM = 32
MLA_V_DIM = HEAD_DIM

RWKV_DECAY_LORA = 64
RWKV_AAA_LORA = 64
RWKV_GATE_LORA = 128
RWKV_GN_EPS = 64e-5

SB_COLS = 3 * SB_WIDTH
MLA_COLS = MLA_Q_LORA + MLA_KV_LORA + MLA_ROPE_DIM
RWKV_COLS = 3 * RWKV_WIDTH + RWKV_DECAY_LORA + RWKV_AAA_LORA + RWKV_GATE_LORA
IN_COLS = SB_COLS + MLA_COLS + RWKV_COLS

D_FF_2 = 2816
CONV_WIDTH = 3

Q_BLOCK = 128
LN_EPS = 1e-5
RMS_EPS = 1e-6
DEEPNORM_ALPHA = (2 * DEPTH) ** 0.25
DEEPNORM_BETA = (8 * DEPTH) ** -0.25


def layer_norm(x, g, b):
    xf = x.astype(jnp.float32)
    mu = jnp.mean(xf, axis=-1, keepdims=True)
    var = jnp.mean(jnp.square(xf - mu), axis=-1, keepdims=True)
    return ((xf - mu) * lax.rsqrt(var + LN_EPS) * g + b).astype(x.dtype)

def rms_norm(x, g):
    xf = x.astype(jnp.float32)
    return (xf * lax.rsqrt(jnp.mean(jnp.square(xf), axis=-1, keepdims=True) + RMS_EPS) * g).astype(x.dtype)

def split_heads(t, n_heads):
    b, s, _ = t.shape
    return t.reshape(b, s, n_heads, -1).transpose(0, 2, 1, 3)

def merge_heads(t):
    b, h, s, d = t.shape
    return t.transpose(0, 2, 1, 3).reshape(b, s, h * d)

def query_block_map(block_fn, q):
    b, h, s, d = q.shape
    nb = s // Q_BLOCK
    qb = q.reshape(b, h, nb, Q_BLOCK, d).transpose(2, 0, 1, 3, 4)
    starts = jnp.arange(nb, dtype=jnp.int32) * Q_BLOCK
    out = lax.map(lambda a: block_fn(a[0], a[1]), (qb, starts))
    return out.transpose(1, 2, 0, 3, 4).reshape(b, h, s, -1)

def stick_breaking_attention(q, k, v):
    s_len = k.shape[2]
    scale = q.shape[-1] ** -0.5
    kpos = jnp.arange(s_len, dtype=jnp.int32)

    def block(qb, start):
        z = jnp.einsum('bhqd,bhkd->bhqk', qb, k).astype(jnp.float32) * scale
        qpos = start + jnp.arange(Q_BLOCK, dtype=jnp.int32)
        past = kpos[None, :] < qpos[:, None]
        log_keep = jnp.where(past, jax.nn.log_sigmoid(-z), 0.0)
        log_later = lax.cumsum(log_keep, axis=3, reverse=True) - log_keep
        w = jnp.where(past, jnp.exp(jax.nn.log_sigmoid(z) + log_later), 0.0)
        return jnp.einsum('bhqk,bhkd->bhqd', w.astype(v.dtype), v)

    return query_block_map(block, q)

def causal_softmax_attention(q, k, v, scale):
    s_len = k.shape[2]
    kpos = jnp.arange(s_len, dtype=jnp.int32)
    neg = jnp.finfo(jnp.float32).min

    def block(qb, start):
        s = jnp.einsum('bhqd,bhkd->bhqk', qb, k).astype(jnp.float32) * scale
        qpos = start + jnp.arange(Q_BLOCK, dtype=jnp.int32)
        s = jnp.where(kpos[None, :] <= qpos[:, None], s, neg)
        p = jax.nn.softmax(s, axis=-1)
        return jnp.einsum('bhqk,bhkd->bhqd', p.astype(v.dtype), v)

    return query_block_map(block, q)

def rope_tables(s_len, dim):
    inv_freq = 1.0 / (ROPE_THETA ** (jnp.arange(0, dim, 2, dtype=jnp.float32) / dim))
    ang = jnp.arange(s_len, dtype=jnp.float32)[:, None] * inv_freq[None, :]
    return jnp.cos(ang), jnp.sin(ang)

def apply_rope(t, cos, sin):
    t1, t2 = jnp.split(t, 2, axis=-1)
    cos = cos.astype(t.dtype)
    sin = sin.astype(t.dtype)
    return jnp.concatenate([t1 * cos - t2 * sin, t2 * cos + t1 * sin], axis=-1)

def mla_mixer(cols, q_norm, w_uq, kv_norm, w_ukv):
    c_q, c_kv, k_rope = jnp.split(cols, [MLA_Q_LORA, MLA_Q_LORA + MLA_KV_LORA], axis=-1)
    q = split_heads(rms_norm(c_q, q_norm) @ w_uq, MLA_HEADS)
    kv = split_heads(rms_norm(c_kv, kv_norm) @ w_ukv, MLA_HEADS)
    q_nope, q_rope = jnp.split(q, [MLA_NOPE_DIM], axis=-1)
    k_nope, v = jnp.split(kv, [MLA_NOPE_DIM], axis=-1)
    cos, sin = rope_tables(cols.shape[1], MLA_ROPE_DIM)
    q_rope = apply_rope(q_rope, cos, sin)
    k_rope = apply_rope(k_rope[:, None], cos, sin)
    q = jnp.concatenate([q_nope, q_rope], axis=-1)
    k = jnp.concatenate([k_nope, jnp.broadcast_to(k_rope, k_nope.shape[:-1] + (MLA_ROPE_DIM,))], axis=-1)
    out = causal_softmax_attention(q, k, v, (MLA_NOPE_DIM + MLA_ROPE_DIM) ** -0.5)
    return merge_heads(out)

def token_shift_mix(p, mu):
    prev = jnp.pad(p, ((0, 0), (1, 0), (0, 0)))[:, :-1]
    return p + (prev - p) * mu

def rwkv7_mixer(cols, mu, w0, w2, a0, a2, g2, k_k, k_a, r_k, gn_g, gn_b):
    b, s, _ = cols.shape
    p = token_shift_mix(cols, mu)
    idx = [RWKV_WIDTH, 2 * RWKV_WIDTH, 3 * RWKV_WIDTH,
           3 * RWKV_WIDTH + RWKV_DECAY_LORA, 3 * RWKV_WIDTH + RWKV_DECAY_LORA + RWKV_AAA_LORA]
    r, k, v, wd, ad, gd = jnp.split(p, idx, axis=-1)
    w = -jax.nn.softplus(-(w0 + jnp.tanh(wd) @ w2)) - 0.5
    decay = jnp.exp(-jnp.exp(w.astype(jnp.float32)))
    a = jax.nn.sigmoid(a0 + ad @ a2)
    g = jax.nn.sigmoid(gd) @ g2
    kk = (k * k_k).reshape(b, s, RWKV_HEADS, HEAD_DIM).astype(jnp.float32)
    kk = kk * lax.rsqrt(jnp.maximum(jnp.sum(jnp.square(kk), axis=-1, keepdims=True), 1e-12))
    k = k * (1.0 + (a - 1.0) * k_a)

    def heads(t):
        return t.reshape(b, s, RWKV_HEADS, HEAD_DIM).astype(jnp.float32)

    rh, kh, vh, ah, wh = heads(r), heads(k), heads(v), heads(a), heads(decay)
    tm = lambda t: jnp.swapaxes(t, 0, 1)

    def step(state, inp):
        r_t, w_t, k_t, v_t, kk_t, a_t = inp
        sa = jnp.einsum('bhvk,bhk->bhv', state, -kk_t)
        state = (state * w_t[:, :, None, :] + sa[..., None] * (kk_t * a_t)[:, :, None, :]
                 + v_t[..., None] * k_t[:, :, None, :])
        return state, jnp.einsum('bhvk,bhk->bhv', state, r_t)

    init = jnp.zeros((b, RWKV_HEADS, HEAD_DIM, HEAD_DIM), jnp.float32)
    _, ys = lax.scan(step, init, (tm(rh), tm(wh), tm(kh), tm(vh), tm(kk), tm(ah)))
    y = jnp.swapaxes(ys, 0, 1)
    mu_y = jnp.mean(y, axis=-1, keepdims=True)
    var_y = jnp.mean(jnp.square(y - mu_y), axis=-1, keepdims=True)
    y = ((y - mu_y) * lax.rsqrt(var_y + RWKV_GN_EPS)).reshape(b, s, RWKV_WIDTH) * gn_g + gn_b
    bonus = jnp.sum(rh * kh * r_k, axis=-1, keepdims=True) * vh
    y = (y + bonus.reshape(b, s, RWKV_WIDTH)) * g
    return y.astype(cols.dtype)

def causal_depthwise_conv(u, w, bias):
    out = lax.conv_general_dilated(u, w[:, None, :], window_strides=(1,),
                                   padding=[(CONV_WIDTH - 1, 0)],
                                   dimension_numbers=('NWC', 'WIO', 'NWC'),
                                   feature_group_count=u.shape[-1])
    return out + bias

def hybrid_layer(x, w_in, mla_q_norm, mla_w_uq, mla_kv_norm, mla_w_ukv,
                 rwkv_mu, rwkv_w0, rwkv_w2, rwkv_a0, rwkv_a2, rwkv_g2, rwkv_k_k, rwkv_k_a, rwkv_r_k,
                 rwkv_gn_g, rwkv_gn_b, w_o, ln1_g, ln1_b,
                 ffn_w_up, ffn_conv_w, ffn_conv_b, ffn_w_down, ln2_g, ln2_b):
    h = x @ w_in
    sb_cols, mla_cols, rwkv_cols = jnp.split(h, [SB_COLS, SB_COLS + MLA_COLS], axis=-1)
    q, k, v = (split_heads(t, SB_HEADS) for t in jnp.split(sb_cols, 3, axis=-1))
    o_sb = merge_heads(stick_breaking_attention(q, k, v))
    o_mla = mla_mixer(mla_cols, mla_q_norm, mla_w_uq, mla_kv_norm, mla_w_ukv)
    o_rwkv = rwkv7_mixer(rwkv_cols, rwkv_mu, rwkv_w0, rwkv_w2, rwkv_a0, rwkv_a2, rwkv_g2,
                         rwkv_k_k, rwkv_k_a, rwkv_r_k, rwkv_gn_g, rwkv_gn_b)
    mix = jnp.concatenate([o_sb, o_mla, o_rwkv], axis=-1) @ w_o
    x = layer_norm(DEEPNORM_ALPHA * x + mix, ln1_g, ln1_b)
    u_act, u_gate = jnp.split(x @ ffn_w_up, 2, axis=-1)
    hid = jax.nn.gelu(causal_depthwise_conv(u_act, ffn_conv_w, ffn_conv_b), approximate=False) * u_gate
    x = layer_norm(DEEPNORM_ALPHA * x + hid @ ffn_w_down, ln2_g, ln2_b)
    return x

def second_inputs(seed: int = 0) -> dict:
    key = jax.random.key(seed)
    ks = iter(jax.random.split(key, 32))
    L = DEPTH

    def nrm(shape, scale):
        return jax.random.normal(next(ks), shape, jnp.float32) * scale

    def unif(shape, lo, hi):
        return jax.random.uniform(next(ks), shape, jnp.float32, lo, hi)

    return {
        "x": nrm((BATCH, SEQ, D_MODEL), 1.0),
        "w_in": nrm((L, D_MODEL, IN_COLS), D_MODEL ** -0.5),
        "mla_q_norm": 1.0 + nrm((L, MLA_Q_LORA), 0.02),
        "mla_w_uq": nrm((L, MLA_Q_LORA, MLA_HEADS * (MLA_NOPE_DIM + MLA_ROPE_DIM)), MLA_Q_LORA ** -0.5),
        "mla_kv_norm": 1.0 + nrm((L, MLA_KV_LORA), 0.02),
        "mla_w_ukv": nrm((L, MLA_KV_LORA, MLA_HEADS * (MLA_NOPE_DIM + MLA_V_DIM)), MLA_KV_LORA ** -0.5),
        "rwkv_mu": unif((L, RWKV_COLS), 0.0, 1.0),
        "rwkv_w0": unif((L, RWKV_WIDTH), -6.5, -1.5),
        "rwkv_w2": nrm((L, RWKV_DECAY_LORA, RWKV_WIDTH), 0.1),
        "rwkv_a0": nrm((L, RWKV_WIDTH), 0.1),
        "rwkv_a2": nrm((L, RWKV_AAA_LORA, RWKV_WIDTH), RWKV_AAA_LORA ** -0.5),
        "rwkv_g2": nrm((L, RWKV_GATE_LORA, RWKV_WIDTH), RWKV_GATE_LORA ** -0.5),
        "rwkv_k_k": 0.85 + nrm((L, RWKV_WIDTH), 0.05),
        "rwkv_k_a": 1.0 + nrm((L, RWKV_WIDTH), 0.05),
        "rwkv_r_k": nrm((L, RWKV_HEADS, HEAD_DIM), 0.1),
        "rwkv_gn_g": 1.0 + nrm((L, RWKV_WIDTH), 0.02),
        "rwkv_gn_b": nrm((L, RWKV_WIDTH), 0.02),
        "w_o": nrm((L, MIX_WIDTH, D_MODEL), MIX_WIDTH ** -0.5 * DEEPNORM_BETA),
        "ln1_g": 1.0 + nrm((L, D_MODEL), 0.02),
        "ln1_b": nrm((L, D_MODEL), 0.02),
        "ffn_w_up": nrm((L, D_MODEL, 2 * D_FF_2), D_MODEL ** -0.5),
        "ffn_conv_w": nrm((L, CONV_WIDTH, D_FF_2), CONV_WIDTH ** -0.5),
        "ffn_conv_b": nrm((L, D_FF_2), 0.02),
        "ffn_w_down": nrm((L, D_FF_2, D_MODEL), D_FF_2 ** -0.5 * DEEPNORM_BETA),
        "ln2_g": 1.0 + nrm((L, D_MODEL), 0.02),
        "ln2_b": nrm((L, D_MODEL), 0.02),
    }

def second_block(x, w_in, mla_q_norm, mla_w_uq, mla_kv_norm, mla_w_ukv,
              rwkv_mu, rwkv_w0, rwkv_w2, rwkv_a0, rwkv_a2, rwkv_g2, rwkv_k_k, rwkv_k_a, rwkv_r_k,
              rwkv_gn_g, rwkv_gn_b, w_o, ln1_g, ln1_b,
              ffn_w_up, ffn_conv_w, ffn_conv_b, ffn_w_down, ln2_g, ln2_b):
    for l in range(DEPTH):
        x = hybrid_layer(x, w_in[l], mla_q_norm[l], mla_w_uq[l], mla_kv_norm[l], mla_w_ukv[l],
                         rwkv_mu[l], rwkv_w0[l], rwkv_w2[l], rwkv_a0[l], rwkv_a2[l], rwkv_g2[l],
                         rwkv_k_k[l], rwkv_k_a[l], rwkv_r_k[l], rwkv_gn_g[l], rwkv_gn_b[l],
                         w_o[l], ln1_g[l], ln1_b[l],
                         ffn_w_up[l], ffn_conv_w[l], ffn_conv_b[l], ffn_w_down[l], ln2_g[l], ln2_b[l])
    return x


def setup_inputs(seed=0):
    out = dict(first_inputs(seed))
    for name, value in second_inputs(seed + 1).items():
        if name != "x":
            out[name + "_2"] = value
    return out


def reference(
    x, positions, attn_norm, w_in, idx_k_norm, sinks, w_a, w_b, w_c, w_o, mlp_norm, w_up,
    w_down, final_norm, w_in_2, mla_q_norm_2, mla_w_uq_2, mla_kv_norm_2, mla_w_ukv_2, rwkv_mu_2,
    rwkv_w0_2, rwkv_w2_2, rwkv_a0_2, rwkv_a2_2, rwkv_g2_2, rwkv_k_k_2, rwkv_k_a_2, rwkv_r_k_2,
    rwkv_gn_g_2, rwkv_gn_b_2, w_o_2, ln1_g_2, ln1_b_2, ffn_w_up_2, ffn_conv_w_2, ffn_conv_b_2,
    ffn_w_down_2, ln2_g_2, ln2_b_2,
):
    x = first_block(
        x, positions, attn_norm, w_in, idx_k_norm, sinks, w_a, w_b, w_c, w_o, mlp_norm, w_up,
        w_down, final_norm,
    )
    return second_block(
        x, w_in_2, mla_q_norm_2, mla_w_uq_2, mla_kv_norm_2, mla_w_ukv_2, rwkv_mu_2, rwkv_w0_2,
        rwkv_w2_2, rwkv_a0_2, rwkv_a2_2, rwkv_g2_2, rwkv_k_k_2, rwkv_k_a_2, rwkv_r_k_2,
        rwkv_gn_g_2, rwkv_gn_b_2, w_o_2, ln1_g_2, ln1_b_2, ffn_w_up_2, ffn_conv_w_2,
        ffn_conv_b_2, ffn_w_down_2, ln2_g_2, ln2_b_2,
    )


_drawn_inputs = setup_inputs


def setup_inputs(seed=0):
    import zlib

    import numpy as np

    out = dict(_drawn_inputs(seed))
    spreads = {}
    factors = {'idx_k_norm': 3.262,
     'sinks': 8.0,
     'mla_q_norm_2': 8.0,
     'mla_kv_norm_2': 8.0,
     'rwkv_w2_2': 3.809,
     'rwkv_a0_2': 6.695,
     'rwkv_gn_g_2': 8.0,
     'rwkv_gn_b_2': 8.0,
     'ffn_conv_b_2': 8.0}
    for name, (base, spread) in spreads.items():
        noise = np.random.default_rng([zlib.crc32(name.encode()), seed]).standard_normal(out[name].shape)
        drawn = base * np.exp(spread * noise) if base else spread * noise
        out[name] = __import__('jax').numpy.asarray(drawn.astype(out[name].dtype))
    for name, factor in factors.items():
        out[name] = (out[name] * factor).astype(out[name].dtype)
    return out
```

```python
from contextlib import ExitStack

import numpy as np

import concourse.bass as bass
from concourse import mybir

F32 = mybir.dt.float32
I32 = mybir.dt.int32
ALU = mybir.AluOpType
ACT = mybir.ActivationFunctionType
AX_X = mybir.AxisListType.X

P = 128
L = 512
D = 1024
DC = D // P
TB = L // P
DEPTH = 2
HD = 64
A_HEADS, IDX_HEADS, B_GROUP_HEADS, C_HEADS = 6, 8, 4, 8
TOPK = 128
FF1 = 4 * D // P
FF2 = 2816 // P
NEG = -1.0e30
TAKEN = -3.0e38
ALPHA = float((2 * DEPTH) ** 0.25)

T_IK, T_AQ, T_AK, T_IQ, T_BQ, T_BK, T_CQ, T_CK = 0, 1, 4, 5, 9, 15, 21, 25
N_QK = 27
W_OFF = dict(aq=0, ak=384, av=448, iq=512, ik=1024, iw=1088, bq=1096, bk=1864, bv=2632,
             cq=3400, ck=3912, cv=4040, gates=4168)

SLOT = 2176
SLOTS = 4
MERGE_B = 1024 + 9 * P
N_PROJ1, N_V1, N_MERGE, N_WO = 14, 4, 16, 4
N_UP1, N_DOWN1 = FF1 // 2, FF1 // 2
S1_V = N_PROJ1
S1_MERGE = S1_V + N_V1
S1_WO = S1_MERGE + N_MERGE
S1_UP = S1_WO + N_WO
S1_DOWN = S1_UP + N_UP1
N_S1 = S1_DOWN + N_DOWN1

P1_ATTN, P1_MLP, P1_IK, P1_SINK, P1_FINAL, P1_NSINK = 0, 8, 16, 17, 25, 40
N_P1 = 33
C1_INV, C1_SIGN, C1_ID, C1_ONE, C1_BLK, C1_CAUSAL, C1_WIN, C1_DIL = 0, 1, 2, 130, 258, 386, 514, 770
C1_DIL16 = C1_DIL + 4 * L
N_C1 = C1_DIL16 + 2 * P

SB_HEADS, MLA_HEADS = 4, 4
Q_LORA, NOPE, RD = 192, 64, 32
QW = NOPE + RD
PAIRS, CH = 4, 64
NCH = L // CH
T2_SBQ, T2_SBK, T2_CQ, T2_CKV, T2_KRS, T2_RW = 0, 2, 4, 6, 7, 8
N_T2 = 22
N_PROJ2 = N_T2 // 2
S2_V = N_PROJ2
S2_MLA = S2_V + 1
S2_LORA = S2_MLA + 1
S2_WO = S2_LORA + 1
S2_UP = S2_WO + 4
S2_DOWN = S2_UP + FF2
N_S2 = S2_DOWN + FF2 // 2
(P2_MU, P2_W0, P2_A0, P2_KK, P2_KA, P2_RK, P2_GNG, P2_GNB, P2_QN, P2_KVN, P2_LN1G, P2_LN1B, P2_LN2G, P2_LN2B,
 P2_CW, P2_CB) = 0, 14, 18, 22, 26, 30, 34, 38, 42, 44, 45, 53, 61, 69, 77, 77 + 3 * FF2
N_P2 = P2_CB + FF2
P2_OMU = N_P2
(C2_CAUSAL, C2_SBKEEP, C2_SBNEG, C2_TRI, C2_RW, C2_ND, C2_NO, C2_NDT, C2_I4, C2_RESET, C2_COS, C2_SIN) = (
    514, 1026, 1154, 1282, 1410, 1922, 2050, 2178, 2690, 3202, 3714, 4226)
N_C2 = 4738


class Signal:

    def __init__(self, sem, base=0):
        self.sem, self.n, self.base = sem, 0, base

    def up(self, instruction, by=1):
        instruction.then_inc(self.sem, by)
        self.n += by
        return self.sem, self.base + self.n


class Banks:

    def __init__(self, start=0):
        self.fills, self.at, self.next = [start] * 8, {}, 0

    def plan(self, name):
        b = self.next
        self.next = (b + 1) % 8
        self.fills[b] += 1
        self.at[name] = (b, self.fills[b], 0)

    def plan_body(self, names, times):
        at = []
        before = list(self.fills)
        for name in names:
            b = self.next
            self.next = (b + 1) % 8
            self.fills[b] += 1
            at.append((name, b, self.fills[b]))
        for name, b, n in at:
            self.at[name] = (b, n, self.fills[b] - before[b])
        for b in range(8):
            self.fills[b] = before[b] + times * (self.fills[b] - before[b])


def build(nc, d, debug=False, stop=None):
    ctx = ExitStack()
    with ctx:
        sems = []

        def sem(name):
            s = ctx.enter_context(nc.semaphore(name))
            sems.append(s)
            return s

        def sb(name, shape, dt=F32):
            return ctx.enter_context(nc.sbuf_tensor(name, shape, dt))

        h = sb("h", [P, DC, L])
        u = sb("u", [P, DC, L])
        ring = sb("ring", [P, SLOTS, SLOT])
        cst = sb("cst", [P, 4800])
        prm = sb("prm", [P, 200])
        small = sb("small", [P, 64])
        room = sb("room", [P, 31000])
        ps = ctx.enter_context(nc.psum_tensor("ps", [P, 8, L], F32))

        full = [sem(f"bank{b}_full") for b in range(8)]
        read = [sem(f"bank{b}_read") for b in range(8)]
        landed = [sem(f"slot{s}_landed") for s in range(SLOTS)]
        loaded = sem("loaded")
        stored = sem("stored")
        act_own = sem("act_own")
        dve_own = sem("dve_own")
        pool_own = sem("pool_own")
        S = {n: sem(n) for n in (
            "rope_arg", "rope_sin", "squared", "root", "normed", "swapped", "roped", "ik_squared", "ik_normed",
            "relued", "iscored", "mask_ready", "row_min", "exped", "den_ready", "scaled", "sink_exped", "pt_kept", "o_kept",
            "gate_kept", "gated", "merged_ready", "h_ready", "hidden_kept", "slab_used",
            "mixed", "prm_ready", "roots2", "mla_normed", "mla_squared", "kr_ready", "q_ready", "k_ready",
            "sb_abs", "sb_soft", "sb_masked", "sb_arg", "sb_weight", "centered", "shifted", "act_act", "gelu", "lora_in",
            "wa_ready", "kk_sq", "kk_root", "decayed", "chunk_in", "expanded", "first_masked", "sq_plus", "nd_ready",
            "solved", "rv", "ln_out", "zeroed", "state_ready")}

        def room_at(off, *shape):
            n = int(np.prod(shape))
            v = room[:, off:off + n]
            if len(shape) == 2:
                v = v.rearrange("p (a b) -> p a b", b=shape[1])
            if len(shape) == 3:
                v = v.rearrange("p (a b c) -> p a b c", b=shape[1], c=shape[2])
            return v

        def close_block():
            nums = [s.num for s in sems]
            assert nums == list(range(nums[0], nums[0] + len(nums)))
            nc.gpsimd.sem_clear(range(nums[0], nums[-1] + 1))
            nc.all_engine_barrier()

        ident = cst[:, C1_ID:C1_ID + P]
        ones = cst[:, C1_ONE:C1_ONE + P]
        blk = cst[:, C1_BLK:C1_BLK + P]
        causal = cst[:, C1_CAUSAL:C1_CAUSAL + P]

        qk = room_at(0, N_QK, L)
        av = room_at(13824, TB, HD)
        bv = room_at(14080, TB, 12 * HD)
        cv = room_at(17152, TB, 2 * HD)
        iw = room_at(17664, TB, IDX_HEADS)
        cos = room_at(17696, L)
        sin = room_at(18208, L)
        o_t = room_at(18720, 9, L)
        WORK = 23328
        swp = room_at(WORK, 2, L)
        ikn = room_at(WORK + 1024, L)
        iksq = room_at(WORK + 1536, L)
        rstd = room_at(WORK + 2048, L)
        sc = room_at(WORK, 4, 768)
        pt = room_at(WORK + 3072, 2, 768)
        score = room_at(WORK + 4608, 3, L)
        rel = room_at(WORK + 6144, 2, L)

        def slot(k, width):
            return ring[:, k % SLOTS, 0:width].rearrange("p (k c) -> p k c", c=width // 8)

        def load_slab(sy, src, k, first=0, width=2048):
            sy.dma_start(ring[:, k % SLOTS, 0:width], src[:, 0:width]).then_inc(landed[k % SLOTS], 16)

        with nc.Block() as block:
            @block.sync
            def _(sy):
                for c in range(DC):
                    sy.dma_start(h[:, c, :], d["x"][c]).then_inc(loaded, 16)
                sy.dma_start(cst[:, 0:N_C1], d["cst1"]).then_inc(loaded, 16)
                sy.dma_start(swp[:, 0, :].bitcast(I32), d["pos"]).then_inc(loaded, 16)

            @block.vector
            def _(dve):
                own = Signal(dve_own)
                dve.wait_ge(loaded, 16 * (DC + 2))
                inv2pi, magic = float(np.float32(1 / (2 * np.pi))), 12582912.0
                c1 = 6.28125
                c2 = float(np.float32(2 * np.pi - c1))
                c3 = float(np.float32(2 * np.pi - c1 - c2))
                t = own.up(nc.vector.tensor_copy(swp[:, 1, :], swp[:, 0, :].bitcast(I32)))
                dve.wait_ge(*t)
                t = own.up(nc.vector.tensor_scalar(ikn, swp[:, 1, :], cst[:, C1_INV:C1_INV + 1], None, ALU.mult))
                dve.wait_ge(*t)
                for dst, quarter in ((sin, 0.0), (cos, 0.25)):
                    t = own.up(nc.vector.tensor_scalar(iksq, ikn, inv2pi, quarter, ALU.mult, ALU.add))
                    dve.wait_ge(*t)
                    t = own.up(nc.vector.tensor_scalar(iksq, iksq, magic, None, ALU.add))
                    dve.wait_ge(*t)
                    t = own.up(nc.vector.tensor_scalar(iksq, iksq, magic, None, ALU.subtract))
                    dve.wait_ge(*t)
                    t = own.up(nc.vector.scalar_tensor_tensor(dst, iksq, -c1, ikn, ALU.mult, ALU.add))
                    dve.wait_ge(*t)
                    t = own.up(nc.vector.scalar_tensor_tensor(dst, iksq, -c2, dst, ALU.mult, ALU.add))
                    dve.wait_ge(*t)
                    t = own.up(nc.vector.scalar_tensor_tensor(dst, iksq, -c3, dst, ALU.mult, ALU.add))
                    dve.wait_ge(*t)
                    t = own.up(nc.vector.tensor_scalar(dst, dst, float(np.float32(quarter * 2 * np.pi)), 3.1415925,
                                                       ALU.add, ALU.min))
                    dve.wait_ge(*t)
                    nc.vector.tensor_scalar(dst, dst, -3.1415925, None, ALU.max).then_inc(S["rope_arg"], 1)
                dve.wait_ge(S["rope_sin"], 2)
                nc.vector.tensor_scalar(sin, sin, cst[:, C1_SIGN:C1_SIGN + 1], None, ALU.mult).then_inc(dve_own, 1)

            @block.scalar
            def _(act):
                for n, dst in enumerate((sin, cos)):
                    act.wait_ge(S["rope_arg"], n + 1)
                    nc.scalar.activation(dst, dst, ACT.Sin).then_inc(S["rope_sin"], 1)
        close_block()

        def bank_to_fill(pe, jobs, name, it=None):
            b, n, per = jobs.at[name]
            if per:
                pe.wait_ge(read[b], it * per + (n - 1))
            elif n > 1:
                pe.wait_ge(read[b], n - 1)
            return b

        def bank_filled(eng, jobs, name, it=None):
            b, n, per = jobs.at[name]
            eng.wait_ge(full[b], it * per + n if per else n)
            return b

        def read_of(jobs, name, it=None):
            b, n, per = jobs.at[name]
            return read[b], (it * per + n if per else n)

        def norm_squares(act, wait_h):
            for c in range(DC):
                if wait_h:
                    act.wait_ge(S["h_ready"], c + 1)
                nc.scalar.activation(u[:, c, :], h[:, c, :], ACT.Square).then_inc(S["squared"], 1)

        def norm_sum(pe, jobs, name):
            b = bank_to_fill(pe, jobs, name)
            for c in range(DC):
                pe.wait_ge(S["squared"], c + 1)
                m = nc.tensor.matmul(ps[:, b, :], ones, u[:, c, :], start=(c == 0), stop=(c == DC - 1))
            m.then_inc(full[b], 1)

        def norm_root(act, jobs, name):
            act.wait_ge(*read_of(jobs, name))
            nc.scalar.activation(rstd, rstd, ACT.Sqrt).then_inc(S["root"], 1)

        def norm_apply(dve, jobs, name, gain, own, roots, dst=u, eps=1e-6):
            b = bank_filled(dve, jobs, name)
            nc.vector.tensor_scalar(rstd, ps[:, b, :], 1.0 / D, eps, ALU.mult, ALU.add).then_inc(read[b], 1)
            dve.wait_ge(S["root"], roots)
            dve.wait_ge(*own.up(nc.vector.reciprocal(rstd, rstd)))
            for c in range(DC):
                nc.vector.scalar_tensor_tensor(dst[:, c, :], h[:, c, :], prm[:, gain + c:gain + c + 1], rstd,
                                               ALU.mult, ALU.mult).then_inc(S["normed"], 1)

        def dense_tile(pe, jobs, name, k, half, src, first_wait=None, it=None):
            b = bank_to_fill(pe, jobs, name, it)
            w = slot(k, 2048)
            for c in range(DC):
                if first_wait is not None:
                    pe.wait_ge(first_wait, c + 1)
                m = nc.tensor.matmul(ps[:, b, :], w[:, c, half * P:(half + 1) * P], src[:, c, :],
                                     start=(c == 0), stop=(c == DC - 1))
            m.then_inc(full[b], 1)

        with nc.Fori(0, DEPTH) as layer:
            def w1_slab(k):
                return d["w1"][bass.ds(layer, 1), k].rearrange("a p c -> p (a c)")

            jobs = Banks()
            for name in ["sum", ("t", 0), ("t", 1), "ik_sum"] + [("t", t) for t in range(2, N_QK)]:
                jobs.plan(name)
            for s in range(N_V1):
                for tb in range(TB):
                    jobs.plan(("v", s, tb))

            with nc.Block() as block:
                @block.sync
                def _(sy, jobs=jobs):
                    sy.dma_start(prm[:, 0:N_P1], d["prm1"][bass.ds(layer, 1)].rearrange("a p c -> p (a c)"))\
                      .then_inc(loaded, 16)
                    for k in range(S1_MERGE):
                        if k >= SLOTS:
                            j = k - SLOTS
                            last = ("t", 2 * j + 1) if j < N_PROJ1 else ("v", j - S1_V, TB - 1)
                            if last == ("t", N_QK):
                                last = ("t", N_QK - 1)
                            b, n, _ = jobs.at[last]
                            sy.wait_ge(full[b], n)
                        sy.dma_start(ring[:, k % SLOTS, 0:2048], w1_slab(k)[:, 0:2048])\
                          .then_inc(landed[k % SLOTS], 16)

                @block.tensor
                def _(pe, jobs=jobs):
                    norm_sum(pe, jobs, "sum")

                    def tile(t):
                        k = t // 2
                        if t % 2 == 0:
                            pe.wait_ge(landed[k % SLOTS], 16 * (k // SLOTS + 1))
                        dense_tile(pe, jobs, ("t", t), k, t % 2, u, S["normed"] if t == 0 else None)

                    tile(0)
                    tile(1)
                    b = bank_to_fill(pe, jobs, "ik_sum")
                    pe.wait_ge(S["ik_squared"], 1)
                    nc.tensor.matmul(ps[:, b, :], blk, iksq, start=True, stop=True).then_inc(full[b], 1)
                    for t in range(2, N_QK):
                        tile(t)
                    for s in range(N_V1):
                        k = S1_V + s
                        pe.wait_ge(landed[k % SLOTS], 16 * (k // SLOTS + 1))
                        w = slot(k, 2048)
                        for tb in range(TB):
                            b = bank_to_fill(pe, jobs, ("v", s, tb))
                            tok = slice(tb, L, TB) if s in (1, 2) else slice(tb * P, (tb + 1) * P)
                            for c in range(DC):
                                m = nc.tensor.matmul(ps[:, b, 0:256], u[:, c, tok], w[:, c, :],
                                                     start=(c == 0), stop=(c == DC - 1))
                            m.then_inc(full[b], 1)

                @block.scalar
                def _(act, jobs=jobs):
                    norm_squares(act, 0)
                    norm_root(act, jobs, "sum")

                    def swap(i, src):
                        if i >= 2:
                            act.wait_ge(S["roped"], i - 1)
                        for q in range(4):
                            o = q ^ 1
                            nc.scalar.activation(swp[32 * q:32 * q + 32, i % 2, :], src[32 * o:32 * o + 32, :],
                                                 ACT.Copy).then_inc(S["swapped"], 1)

                    act.wait_ge(*read_of(jobs, ("t", 0)))
                    nc.scalar.activation(iksq, ikn, ACT.Square).then_inc(S["ik_squared"], 1)
                    b = bank_filled(act, jobs, ("t", 1))
                    swap(0, ps[:, b, :])
                    norm_root(act, jobs, "ik_sum")
                    act.wait_ge(S["ik_normed"], 1)
                    swap(1, ikn)
                    for t in range(2, N_QK):
                        b = bank_filled(act, jobs, ("t", t))
                        swap(t, ps[:, b, :])
                    for s in range(N_V1):
                        for tb in range(TB):
                            b = bank_filled(act, jobs, ("v", s, tb))
                            if s < 3:
                                nc.scalar.activation(bv[:, tb, 256 * s:256 * s + 256], ps[:, b, 0:256], ACT.Copy)\
                                  .then_inc(read[b], 1)
                            else:
                                nc.scalar.activation(av[:, tb, :], ps[:, b, 0:HD], ACT.Copy)
                                nc.scalar.activation(cv[:, tb, :], ps[:, b, HD:3 * HD], ACT.Copy)
                                nc.scalar.activation(iw[:, tb, :], ps[:, b, 3 * HD:3 * HD + IDX_HEADS], ACT.Copy,
                                                     scale=IDX_HEADS ** -0.5).then_inc(read[b], 1)

                @block.vector
                def _(dve, jobs=jobs):
                    own = Signal(dve_own)
                    dve.wait_ge(loaded, 16)
                    norm_apply(dve, jobs, "sum", P1_ATTN, own, 1)
                    b = bank_filled(dve, jobs, ("t", 0))
                    nc.vector.tensor_copy(ikn, ps[:, b, :]).then_inc(read[b], 1)

                    def rope(i, t, src, done):
                        dve.wait_ge(S["swapped"], 4 * (i + 1))
                        nc.vector.tensor_tensor(qk[:, t, :], src, cos, ALU.mult).then_inc(*done[:2])
                        dve.wait_ge(*own.up(nc.vector.tensor_tensor(swp[:, i % 2, :], swp[:, i % 2, :], sin, ALU.mult)))
                        dve.wait_ge(done[0], done[2])
                        nc.vector.tensor_tensor(qk[:, t, :], qk[:, t, :], swp[:, i % 2, :], ALU.add)\
                          .then_inc(S["roped"], 1)

                    def rope_bank(i, t):
                        b = bank_filled(dve, jobs, ("t", t))
                        rope(i, t, ps[:, b, :], (read[b], 1, jobs.at["t", t][1]))

                    rope_bank(0, 1)
                    b = bank_filled(dve, jobs, "ik_sum")
                    nc.vector.tensor_scalar(rstd, ps[:, b, :], 1.0 / HD, 1e-6, ALU.mult, ALU.add).then_inc(read[b], 1)
                    dve.wait_ge(S["root"], 2)
                    dve.wait_ge(*own.up(nc.vector.reciprocal(rstd, rstd)))
                    nc.vector.scalar_tensor_tensor(ikn, ikn, prm[:, P1_IK:P1_IK + 1], rstd, ALU.mult, ALU.mult)\
                      .then_inc(S["ik_normed"], 1)
                    dve.wait_ge(S["ik_normed"], 1)
                    own.n += 1
                    rope(1, T_IK, ikn, (dve_own, 1, own.n))
                    for t in range(2, N_QK):
                        rope_bank(t, t)
            close_block()

            units = [("B", j, r) for r in range(TB) for j in range(B_GROUP_HEADS)]
            units += [("C", hd, b) for b in range(TB) for hd in range(C_HEADS)]
            units += [("A", hd, b) for b in range(TB) for hd in range(A_HEADS)]

            def unit_width(unit):
                br, hd, b = unit
                return 6 * P if br == "B" else min(b + 1, 2) * P if br == "C" else (b + 1) * P

            def steps():
                for k in range(len(units) + 4):
                    yield [k - lag if 0 <= k - lag < len(units) else None for lag in range(5)]

            jobs = Banks()
            for b in range(1, TB):
                for hd in range(IDX_HEADS):
                    jobs.plan(("index", b, hd))
            for s0, s1, s2, s3, s4 in steps():
                if s0 is not None:
                    jobs.plan(("logits", s0, 0))
                    if units[s0][0] == "B":
                        jobs.plan(("logits", s0, 1))
                if s2 is not None:
                    jobs.plan(("pt", s2, 0))
                    if units[s2][0] == "B":
                        jobs.plan(("pt", s2, 1))
                if s3 is not None:
                    jobs.plan(("o", s3))

            def half(hd):
                return slice(HD * (hd % 2), HD * (hd % 2) + HD)

            with nc.Block() as block:
                @block.tensor
                def _(pe, jobs=jobs):
                    for b in range(1, TB):
                        for hd in range(IDX_HEADS):
                            bank = bank_to_fill(pe, jobs, ("index", b, hd))
                            nc.tensor.matmul(ps[:, bank, 0:(b + 1) * P], qk[half(hd), T_IQ + hd // 2, b * P:(b + 1) * P],
                                             qk[half(hd), T_IK, 0:(b + 1) * P], start=True, stop=True)\
                              .then_inc(full[bank], 1)

                    def logits(k):
                        br, hd, b = units[k]
                        w = unit_width(units[k])
                        bank = bank_to_fill(pe, jobs, ("logits", k, 0))
                        if br == "A":
                            nc.tensor.matmul(ps[:, bank, 0:w], qk[half(hd), T_AQ + hd // 2, b * P:(b + 1) * P],
                                             qk[half(hd), T_AK, 0:w], start=True, stop=True).then_inc(full[bank], 1)
                        elif br == "C":
                            nc.tensor.matmul(ps[:, bank, 0:w], qk[half(hd), T_CQ + hd // 2, b * P:(b + 1) * P],
                                             qk[half(hd), T_CK + hd // 4, (b + 1) * P - w:(b + 1) * P],
                                             start=True, stop=True).then_inc(full[bank], 1)
                        else:
                            rows = slice(b, L, TB)
                            q = [qk[half(hd), T_BQ + (g * 4 + hd) // 2, rows] for g in range(3)]
                            kk = [qk[half(hd), T_BK + (g * 4 + hd) // 2, :] for g in range(3)]
                            nc.tensor.matmul(ps[:, bank, :], q[0], kk[0], start=True, stop=True).then_inc(full[bank], 1)
                            bank = bank_to_fill(pe, jobs, ("logits", k, 1))
                            for g in (1, 2):
                                m = nc.tensor.matmul(ps[:, bank, (g - 1) * P:g * P], q[g], kk[g][:, rows],
                                                     start=(g == 1), stop=(g == 2), skip_group_check=True)
                            m.then_inc(full[bank], 1)

                    def turn(k):
                        n = unit_width(units[k]) // P
                        pe.wait_ge(S["scaled"], k + 1)
                        for part in range(2 if n > 4 else 1):
                            bank = bank_to_fill(pe, jobs, ("pt", k, part))
                            cs = range(4 * part, min(4 * part + 4, n))
                            for c in cs:
                                m = nc.tensor.transpose(ps[:, bank, (c % 4) * P:(c % 4 + 1) * P],
                                                        sc[:, k % 4, c * P:(c + 1) * P], ident)
                            m.then_inc(full[bank], 1)

                    def values(k):
                        br, hd, b = units[k]
                        n = unit_width(units[k]) // P
                        pe.wait_ge(*read_of(jobs, ("pt", k, 1 if n > 4 else 0)))
                        if n > 4:
                            pe.wait_ge(*read_of(jobs, ("pt", k, 0)))
                        bank = bank_to_fill(pe, jobs, ("o", k))
                        for c in range(n):
                            if br == "A":
                                v = av[:, c, :]
                            elif br == "C":
                                v = cv[:, b + 1 - n + c, hd // 4 * HD:(hd // 4 + 1) * HD]
                            elif c < 4:
                                v = bv[:, c, hd * HD:(hd + 1) * HD]
                            else:
                                v = bv[:, b, (4 * (c - 3) + hd) * HD:(4 * (c - 3) + hd + 1) * HD]
                            m = nc.tensor.matmul(ps[half(hd), bank, 0:P], v, pt[:, k % 2, c * P:(c + 1) * P],
                                                 start=(c == 0), stop=(c == n - 1))
                        m.then_inc(full[bank], 1)

                    for s0, s1, s2, s3, s4 in steps():
                        if s0 is not None:
                            logits(s0)
                        if s2 is not None:
                            turn(s2)
                        if s3 is not None:
                            values(s3)

                @block.scalar
                def _(act, jobs=jobs):
                    i = 0
                    for b in range(1, TB):
                        for hd in range(IDX_HEADS):
                            bank = bank_filled(act, jobs, ("index", b, hd))
                            if i >= 2:
                                act.wait_ge(S["iscored"], i - 1)
                            nc.scalar.activation(rel[:, i % 2, 0:(b + 1) * P], ps[:, bank, 0:(b + 1) * P], ACT.Relu,
                                                 scale=HD ** -0.5).then_inc(read[bank], 1)
                            i += 1
                    sinks = 0
                    for s0, s1, s2, s3, s4 in steps():
                        if s1 is not None:
                            k, w = s1, unit_width(units[s1])
                            if units[k][0] == "A":
                                act.wait_ge(*read_of(jobs, ("logits", k, 0)))
                            else:
                                act.wait_ge(S["row_min"], k + 1)
                            if units[k][0] == "C":
                                s = P1_SINK + units[k][1]
                                nc.scalar.activation(small[:, 16 + k % 4:17 + k % 4], small[:, k % 4:k % 4 + 1], ACT.Exp,
                                                     bias=prm[:, s:s + 1])
                            nc.scalar.activation(sc[:, k % 4, 0:w], sc[:, k % 4, 0:w], ACT.Exp,
                                                 bias=small[:, k % 4:k % 4 + 1], scale=-1.0,
                                                 accum_out=small[:, 4 + k % 4:5 + k % 4]).then_inc(S["exped"], 1)
                        if s2 is not None:
                            k, n = s2, unit_width(units[s2]) // P
                            for part in range(2 if n > 4 else 1):
                                bank = bank_filled(act, jobs, ("pt", k, part))
                                if k >= 2:
                                    b, m, _ = jobs.at["o", k - 2]
                                    act.wait_ge(full[b], m)
                                lo, hi = 512 * part, min(512 * part + 512, n * P)
                                nc.scalar.activation(pt[:, k % 2, lo:hi], ps[:, bank, 0:hi - lo], ACT.Copy)\
                                  .then_inc(read[bank], 1)

                @block.gpsimd
                def _(pool, jobs=jobs):
                    for k, unit in enumerate(units):
                        w = unit_width(unit)
                        pool.wait_ge(S["den_ready"], k + 1)
                        nc.gpsimd.tensor_scalar(sc[:, k % 4, 0:w], sc[:, k % 4, 0:w], small[:, 8 + k % 4:9 + k % 4], None,
                                                ALU.mult).then_inc(S["scaled"], 1)

                @block.vector
                def _(dve, jobs=jobs):
                    own = Signal(dve_own)
                    dve.wait_ge(*own.up(nc.vector.tensor_scalar(prm[:, P1_NSINK:P1_NSINK + C_HEADS],
                                                                prm[:, P1_SINK:P1_SINK + C_HEADS], -1.0, None, ALU.mult)))
                    i = 0
                    for b in range(1, TB):
                        w = (b + 1) * P
                        for hd in range(IDX_HEADS):
                            dve.wait_ge(*read_of(jobs, ("index", b, hd)))
                            if hd == 0:
                                nc.vector.tensor_scalar(score[:, b - 1, 0:w], rel[:, i % 2, 0:w], iw[:, b, hd:hd + 1], None,
                                                        ALU.mult).then_inc(S["iscored"], 1)
                            else:
                                dve.wait_ge(S["iscored"], i)
                                nc.vector.scalar_tensor_tensor(score[:, b - 1, 0:w], rel[:, i % 2, 0:w],
                                                               iw[:, b, hd:hd + 1], score[:, b - 1, 0:w],
                                                               ALU.mult, ALU.add).then_inc(S["iscored"], 1)
                            i += 1
                        dve.wait_ge(S["iscored"], i)
                        m = own.up(nc.vector.tensor_tensor(score[:, b - 1, b * P:w], score[:, b - 1, b * P:w], causal, ALU.add))
                        if b == TB - 1:
                            dve.wait_ge(*m)

                    def topk():
                        for b in range(1, TB):
                            row = score[:, b - 1, 0:(b + 1) * P]
                            for _ in range(TOPK // 8):
                                m = own.up(nc.vector.max(out=small[:, 32:40], in_=row))
                                yield
                                dve.wait_ge(*m)
                                m = own.up(nc.vector.match_replace(out=row, in_to_replace=small[:, 32:40], in_values=row,
                                                                   imm_value=TAKEN))
                                yield
                                dve.wait_ge(*m)
                            m = own.up(nc.vector.tensor_scalar(row, row, TAKEN / 2, NEG, ALU.is_gt, ALU.mult))
                            dve.wait_ge(*m)
                            yield

                    picks = topk()
                    for s0, s1, s2, s3, s4 in steps():
                        if s0 is not None:
                            k = s0
                            br, hd, b = units[k]
                            w = unit_width(units[k])
                            if br == "A":
                                for _ in picks:
                                    pass
                            mn = small[:, k % 4:k % 4 + 1]
                            if k >= 4:
                                bk, m, _ = jobs.at["pt", k - 4, 1 if units[k - 4][0] == "B" else 0]
                                dve.wait_ge(full[bk], m)
                            bank = bank_filled(dve, jobs, ("logits", k, 0))
                            if br == "B":
                                mask, w0 = cst[:, C1_DIL + b * L:C1_DIL + (b + 1) * L], L
                            elif br == "C":
                                mask, w0 = cst[:, C1_WIN + 256 - w:C1_WIN + 256], w
                            else:
                                mask, w0 = (causal if b == 0 else score[:, b - 1, 0:w]), w
                            part = small[:, 20 + 2 * (k % 2):22 + 2 * (k % 2)]
                            first = mn if br == "A" else part[:, 0:1]
                            t = nc.vector.tensor_tensor_reduce(out=sc[:, k % 4, 0:w0], in0=ps[:, bank, 0:w0], in1=mask,
                                                               scale=-(HD ** -0.5), scalar=-NEG, op0=ALU.add, op1=ALU.min,
                                                               accum_out=first)
                            t.then_inc(read[bank], 1)
                            dve.wait_ge(*read_of(jobs, ("logits", k, 0)))
                            if br == "B":
                                bank = bank_filled(dve, jobs, ("logits", k, 1))
                                mask = cst[:, C1_DIL16:C1_DIL16 + 256]
                                nc.vector.tensor_tensor_reduce(out=sc[:, k % 4, L:L + 256], in0=ps[:, bank, 0:256],
                                                               in1=mask, scale=-(HD ** -0.5), scalar=-NEG, op0=ALU.add,
                                                               op1=ALU.min, accum_out=part[:, 1:2]).then_inc(read[bank], 1)
                                dve.wait_ge(*read_of(jobs, ("logits", k, 1)))
                                nc.vector.tensor_tensor(mn, part[:, 0:1], part[:, 1:2], ALU.min).then_inc(S["row_min"], 1)
                            elif br == "C":
                                nc.vector.tensor_tensor(mn, part[:, 0:1], prm[:, P1_NSINK + hd:P1_NSINK + hd + 1], ALU.min)\
                                  .then_inc(S["row_min"], 1)
                        if s1 is not None:
                            k = s1
                            den = small[:, 4 + k % 4:5 + k % 4]
                            dve.wait_ge(S["exped"], k + 1)
                            if units[k][0] == "C":
                                dve.wait_ge(*own.up(nc.vector.tensor_tensor(den, den, small[:, 16 + k % 4:17 + k % 4], ALU.add)))
                            nc.vector.reciprocal(small[:, 8 + k % 4:9 + k % 4], den).then_inc(S["den_ready"], 1)
                        if s3 is not None:
                            k = s3
                            br, hd, b = units[k]
                            bank = bank_filled(dve, jobs, ("o", k))
                            tile = {"A": 0, "B": 3, "C": 5}[br] + hd // 2
                            cols = slice(b, L, TB) if br == "B" else slice(b * P, (b + 1) * P)
                            nc.vector.tensor_copy(o_t[half(hd), tile, cols], ps[half(hd), bank, 0:P]).then_inc(read[bank], 1)
                        next(picks, None)
                        next(picks, None)
            close_block()

            merged = room_at(0, DC, L)
            gate = room_at(4096, 6, L)
            gtmp = room_at(7168, 3, L)
            hid = room_at(0, FF1, L)
            BR = {0: (0, 3), 1: (3, 2), 2: (5, 4)}
            jobs = Banks(start=1)
            jobs.plan_body([(w, q, j) for q in range(2) for w in ("gate", "branch") for j in range(3)], DC // 2)
            for n in range(DC):
                jobs.plan(("wo", n))
            jobs.plan("sum")
            jobs.plan_body([("up", j) for j in range(8)], FF1 // 8)
            for n in range(DC):
                jobs.plan(("down", n))

            with nc.Block() as block:
                @block.sync
                def _(sy, jobs=jobs):
                    def load(k, width=2048):
                        sy.dma_start(ring[:, k_slot(k), 0:width], w1_slab_at(k)[:, 0:width])

                    def fetch(k, j, width):
                        sy.dma_start(ring[:, j, 0:width],
                                     d["w1"][bass.ds(layer, 1), bass.ds(k, 1), :, 0:width].rearrange("a b p c -> p (a b c)"))\
                          .then_inc(landed[j], 16)

                    def merge_width(j):
                        return 2048 if j % 2 == 0 else MERGE_B

                    def merge_last(j):
                        return ("gate", j // 2, 1) if j % 2 == 0 else ("branch", j // 2, 2)

                    for j in range(4):
                        fetch(S1_MERGE + j, j, merge_width(j))
                    with sy.Fori(1, N_MERGE // 4) as it:
                        for j in range(4):
                            b, n, per = jobs.at[merge_last(j)]
                            sy.wait_ge(full[b], (it - 1) * per + n)
                            fetch(it * 4 + (S1_MERGE + j), j, merge_width(j))
                    for j in range(4):
                        b, n, per = jobs.at[merge_last(j)]
                        sy.wait_ge(full[b], (N_MERGE // 4 - 1) * per + n)
                        fetch(S1_WO + j, j, 2048)
                    for j in range(4):
                        b, n, _ = jobs.at["wo", 2 * j + 1]
                        sy.wait_ge(full[b], n)
                        fetch(S1_UP + j, j, 2048)
                    with sy.Fori(1, N_UP1 // 4) as it:
                        for j in range(4):
                            b, n, per = jobs.at["up", 2 * j + 1]
                            sy.wait_ge(full[b], (it - 1) * per + n)
                            fetch(it * 4 + (S1_UP + j), j, 2048)
                    for j in range(4):
                        b, n, per = jobs.at["up", 2 * j + 1]
                        sy.wait_ge(full[b], (N_UP1 // 4 - 1) * per + n)
                        fetch(S1_DOWN + j, j, 2048)
                    with sy.Fori(1, N_DOWN1 // 4) as it:
                        for j in range(4):
                            sy.wait_ge(S["slab_used"], it * 4 + (j - 3))
                            fetch(it * 4 + (S1_DOWN + j), j, 2048)

                @block.tensor
                def _(pe, jobs=jobs):
                    for b in range(8):
                        pe.sem_inc(full[b], 1)
                        pe.sem_inc(read[b], 1)
                    with pe.Fori(0, DC // 2) as it:
                        for q in range(2):
                            for j in range(3):
                                if j != 1:
                                    s = 2 * q + (j == 2)
                                    pe.wait_ge(landed[s], it * 16 + 16)
                                w = ring[:, 2 * q + (j == 2), (j % 2) * 1024:(j % 2) * 1024 + 1024]\
                                    .rearrange("p (k c) -> p k c", c=P)
                                b = bank_to_fill(pe, jobs, ("gate", q, j), it)
                                for c in range(DC):
                                    m = nc.tensor.matmul(ps[:, b, :], w[:, c, :], u[:, c, :], start=(c == 0), stop=(c == DC - 1))
                                m.then_inc(full[b], 1)
                            w = ring[:, 2 * q + 1, 1024:MERGE_B].rearrange("p (k c) -> p k c", c=P)
                            for j in range(3):
                                t0, n = BR[j]
                                b = bank_to_fill(pe, jobs, ("branch", q, j), it)
                                for c in range(n):
                                    m = nc.tensor.matmul(ps[:, b, :], w[:, t0 + c, :], o_t[:, t0 + c, :],
                                                         start=(c == 0), stop=(c == n - 1))
                                m.then_inc(full[b], 1)
                    pe.wait_ge(S["gated"], DC + 2)
                    for n in range(DC):
                        if n % 2 == 0:
                            pe.wait_ge(landed[n // 2], 16 * (N_MERGE // 4 + 1))
                        dense_tile(pe, jobs, ("wo", n), n // 2, n % 2, merged)
                    norm_sum(pe, jobs, "sum")
                    pe.wait_ge(S["normed"], DC)
                    with pe.Fori(0, FF1 // 8) as it:
                        for j in range(8):
                            if j % 2 == 0:
                                pe.wait_ge(landed[j // 2], it * 16 + 16 * (N_MERGE // 4 + 2))
                            dense_tile(pe, jobs, ("up", j), j // 2, j % 2, u, it=it)
                    pe.wait_ge(S["hidden_kept"], FF1)

                    def down(it, first, last):
                        for j in range(4):
                            pe.wait_ge(landed[j], it * 16 + 16 * (N_MERGE // 4 + 2 + N_UP1 // 4))
                            w = ring[:, j, 0:2048].rearrange("p (k c) -> p k c", c=D)
                            for c in range(2):
                                for n in range(DC):
                                    b = jobs.at["down", n][0]
                                    if first and j == 0 and c == 0:
                                        bank_to_fill(pe, jobs, ("down", n))
                                    end = last and j == 3 and c == 1
                                    rhs = hid[:, 8 * it + 2 * j + c, :] if isinstance(it, int) else \
                                        hid[:, bass.ds(it * 8 + (2 * j + c), 1), :].rearrange("p a c -> p (a c)")
                                    m = nc.tensor.matmul(ps[:, b, :], w[:, c, n * P:(n + 1) * P], rhs,
                                                         start=(first and j == 0 and c == 0), stop=end)
                                    if end:
                                        m.then_inc(full[b], 1)
                            if not (last and j == 3):
                                m.then_inc(S["slab_used"], 1)

                    down(0, True, False)
                    with pe.Fori(1, N_DOWN1 // 4 - 1) as it:
                        down(it, False, False)
                    down(N_DOWN1 // 4 - 1, False, True)

                @block.scalar
                def _(act, jobs=jobs):
                    with act.Fori(0, DC // 2) as it:
                        for q in range(2):
                            act.wait_ge(S["gated"], it * 2 + (q + 1))
                            for j in range(3):
                                b = bank_filled(act, jobs, ("gate", q, j), it)
                                nc.scalar.activation(gate[:, 3 * q + j, :], ps[:, b, :], ACT.Sigmoid).then_inc(read[b], 1)
                    norm_squares(act, True)
                    norm_root(act, jobs, "sum")
                    with act.Fori(0, FF1 // 8) as it:
                        for j in range(8):
                            b = bank_filled(act, jobs, ("up", j), it)
                            nc.scalar.activation(hid[:, bass.ds(it * 8 + j, 1), :].rearrange("p a c -> p (a c)"),
                                                 ps[:, b, :], ACT.Relu).then_inc(read[b], 1)

                @block.vector
                def _(dve, jobs=jobs):
                    dve.sem_inc(S["gated"], 2)
                    with dve.Fori(0, DC // 2) as it:
                        for q in range(2):
                            dve.wait_ge(S["gated"], it * 2 + (q + 2))
                            for j in range(3):
                                dve.wait_ge(*read_of(jobs, ("gate", q, j), it))
                                b = bank_filled(dve, jobs, ("branch", q, j), it)
                                nc.vector.tensor_tensor(gtmp[:, j, :], ps[:, b, :], gate[:, 3 * q + j, :], ALU.mult)\
                                  .then_inc(read[b], 1)
                            for j in range(2):
                                dve.wait_ge(*read_of(jobs, ("branch", q, j), it))
                            nc.vector.tensor_tensor(gtmp[:, 0, :], gtmp[:, 0, :], gtmp[:, 1, :], ALU.add).then_inc(dve_own, 1)
                            dve.wait_ge(*read_of(jobs, ("branch", q, 2), it))
                            dve.wait_ge(dve_own, it * 2 + (q + 1))
                            nc.vector.tensor_tensor(merged[:, bass.ds(it * 2 + q, 1), :].rearrange("p a c -> p (a c)"),
                                                    gtmp[:, 0, :], gtmp[:, 2, :], ALU.add).then_inc(S["gated"], 1)
                    own = Signal(dve_own)
                    own.n = DC
                    for n in range(DC):
                        b = bank_filled(dve, jobs, ("wo", n))
                        nc.vector.tensor_tensor(h[:, n, :], h[:, n, :], ps[:, b, :], ALU.add).then_inc(read[b], 1)
                        dve.wait_ge(*read_of(jobs, ("wo", n)))
                        dve.sem_inc(S["h_ready"], 1)
                    norm_apply(dve, jobs, "sum", P1_MLP, own, 1)
                    with dve.Fori(0, FF1 // 8) as it:
                        for j in range(8):
                            dve.wait_ge(*read_of(jobs, ("up", j), it))
                            t = hid[:, bass.ds(it * 8 + j, 1), :].rearrange("p a c -> p (a c)")
                            nc.vector.tensor_tensor(t, t, t, ALU.mult).then_inc(S["hidden_kept"], 1)
                    for n in range(DC):
                        b = bank_filled(dve, jobs, ("down", n))
                        nc.vector.tensor_tensor(h[:, n, :], h[:, n, :], ps[:, b, :], ALU.add).then_inc(read[b], 1)
            close_block()

        jobs = Banks()
        jobs.plan("sum")
        with nc.Block() as block:
            @block.tensor
            def _(pe):
                norm_sum(pe, jobs, "sum")

            @block.scalar
            def _(act):
                norm_squares(act, False)
                norm_root(act, jobs, "sum")

            @block.vector
            def _(dve):
                norm_apply(dve, jobs, "sum", P1_FINAL, Signal(dve_own), 1, dst=h)
        close_block()

        sbqk = room_at(0, 4, L)
        sbv = room_at(2048, TB, SB_HEADS * HD)
        cq = room_at(3072, 2, L)
        ckv = room_at(4096, L)
        krs = room_at(4608, L)
        rr, rk, rv = room_at(5120, PAIRS, L), room_at(7168, PAIRS, L), room_at(9216, PAIRS, L)
        wdad, gd = room_at(11264, L), room_at(11776, L)
        rw_in = room_at(5120, 14, L)
        o2 = room_at(12288, DC, L)
        mq, mk = room_at(16384, MLA_HEADS, L), room_at(18432, MLA_HEADS, L)
        mv = room_at(20480, TB, MLA_HEADS * HD)
        sc2 = room_at(21504, 4, L)
        pt2 = room_at(23552, 2, L)
        msq = room_at(24576, 3, L)
        mrs = room_at(26112, 2, L)
        ZO = [0, 512, 896, 1152, 1280]
        uu = u[:, :, :].rearrange("p a b -> p (a b)")
        zs = [uu[:, 0:1280], room[:, 27136:28416]]
        sp = [uu[:, 1280:2560], room[:, 28416:29696]]

        with nc.Block() as block:
            @block.sync
            def _(sy):
                sy.dma_start(cst[:, 0:N_C2], d["cst2"]).then_inc(loaded, 16)
                sy.wait_ge(loaded, 16)
        close_block()

        def prm_col(c):
            return prm[:, c:c + 1]

        with nc.Fori(0, DEPTH) as layer:
            jobs = Banks()
            for t in range(N_T2):
                jobs.plan(("t", t))
            for tb in range(TB):
                jobs.plan(("v", tb))

            with nc.Block() as block:
                @block.sync
                def _(sy, jobs=jobs):
                    sy.dma_start(prm[:, 0:N_P2], d["prm2"][bass.ds(layer, 1)].rearrange("a p c -> p (a c)"))\
                      .then_inc(loaded, 16)
                    for k in range(S2_LORA):
                        if k >= SLOTS:
                            b, n, _ = jobs.at["t", 2 * (k - SLOTS) + 1]
                            sy.wait_ge(full[b], n)
                        sy.dma_start(ring[:, k % SLOTS, 0:2048],
                                     d["w2"][bass.ds(layer, 1), k, :, 0:2048].rearrange("a p c -> p (a c)"))\
                          .then_inc(landed[k % SLOTS], 16)
                    sy.wait_ge(landed[S2_MLA % SLOTS], 16 * (S2_MLA // SLOTS + 1))

                @block.tensor
                def _(pe, jobs=jobs):
                    for t in range(N_T2):
                        k = t // 2
                        if t % 2 == 0:
                            pe.wait_ge(landed[k % SLOTS], 16 * (k // SLOTS + 1))
                        dense_tile(pe, jobs, ("t", t), k, t % 2, h)
                    k = S2_V
                    pe.wait_ge(landed[k % SLOTS], 16 * (k // SLOTS + 1))
                    w = slot(k, 2048)
                    for tb in range(TB):
                        b = bank_to_fill(pe, jobs, ("v", tb))
                        for c in range(DC):
                            m = nc.tensor.matmul(ps[:, b, 0:256], h[:, c, tb * P:(tb + 1) * P], w[:, c, :],
                                                 start=(c == 0), stop=(c == DC - 1))
                        m.then_inc(full[b], 1)

                @block.scalar
                def _(act, jobs=jobs):
                    act.wait_ge(S["prm_ready"], 1)
                    for t in range(N_T2):
                        b = bank_filled(act, jobs, ("t", t))
                        if t < T2_RW:
                            dst = [sbqk[:, 0, :], sbqk[:, 1, :], sbqk[:, 2, :], sbqk[:, 3, :], cq[:, 0, :], cq[:, 1, :],
                                   ckv, krs][t]
                            nc.scalar.activation(dst, ps[:, b, :], ACT.Copy).then_inc(read[b], 1)
                        else:
                            i = t - T2_RW
                            nc.scalar.activation(rw_in[:, i, :], ps[:, b, :], ACT.Copy, scale=prm_col(P2_OMU + i))\
                              .then_inc(S["mixed"], 1)
                    for tb in range(TB):
                        b = bank_filled(act, jobs, ("v", tb))
                        nc.scalar.activation(sbv[:, tb, :], ps[:, b, 0:256], ACT.Copy).then_inc(read[b], 1)

                @block.vector
                def _(dve, jobs=jobs):
                    dve.wait_ge(loaded, 16)
                    nc.vector.tensor_scalar(prm[:, P2_OMU:P2_OMU + 14], prm[:, P2_MU:P2_MU + 14], -1.0, 1.0,
                                            ALU.mult, ALU.add).then_inc(S["prm_ready"], 1)
                    for t in range(T2_RW, N_T2):
                        i = t - T2_RW
                        b = bank_filled(dve, jobs, ("t", t))
                        dve.wait_ge(S["mixed"], i + 1)
                        nc.vector.scalar_tensor_tensor(rw_in[:, i, 1:L], ps[:, b, 0:L - 1], prm_col(P2_MU + i),
                                                       rw_in[:, i, 1:L], ALU.mult, ALU.add).then_inc(read[b], 1)
            close_block()

            mla = [(hd, b) for b in range(TB) for hd in range(MLA_HEADS)]
            NM = len(mla)

            def steps2():
                for k in range(NM + 4):
                    m = [k - lag if 0 <= k - lag < NM else None for lag in range(4)]
                    s = [(k - at) // 4 if (k - at) % 4 == 0 and 0 <= (k - at) // 4 < SB_HEADS else None for at in (0, 2, 4)]
                    yield m, s

            jobs = Banks()
            for name in ("cq_sum", "ckv_sum"):
                jobs.plan(name)
            for hd in range(MLA_HEADS):
                for name in ("qs", "q", "k"):
                    jobs.plan((name, hd))
            for tb in range(TB):
                jobs.plan(("mv", tb))
            for m, s in steps2():
                if s[0] is not None:
                    for c in range(TB):
                        jobs.plan(("z", s[0], c))
                if s[1] is not None:
                    for c in range(TB):
                        jobs.plan(("later", s[1], c))
                if s[2] is not None:
                    jobs.plan(("sb", s[2]))
                if m[0] is not None:
                    jobs.plan(("logits", m[0]))
                if m[2] is not None:
                    jobs.plan(("pt", m[2]))
                if m[3] is not None:
                    jobs.plan(("o", m[3]))

            with nc.Block() as block:
                @block.tensor
                def _(pe, jobs=jobs):
                    wm = ring[:, S2_MLA % SLOTS, 0:2048]
                    uq = wm[:, 0:1536].rearrange("p (k c) -> p k c", k=2)
                    ukv = wm[:, 1536:2048]
                    b = bank_to_fill(pe, jobs, "cq_sum")
                    pe.wait_ge(S["mla_squared"], 3)
                    nc.tensor.matmul(ps[:, b, :], ones, msq[:, 0, :], start=True, stop=False)
                    nc.tensor.matmul(ps[:, b, :], ones[0:64, :], msq[0:64, 1, :], start=False, stop=True).then_inc(full[b], 1)
                    b = bank_to_fill(pe, jobs, "ckv_sum")
                    nc.tensor.matmul(ps[:, b, :], ones, msq[:, 2, :], start=True, stop=True).then_inc(full[b], 1)
                    pe.wait_ge(S["mla_normed"], 3)
                    for hd in range(MLA_HEADS):
                        for name, c0 in (("qs", 384), ("q", 0)):
                            b = bank_to_fill(pe, jobs, (name, hd))
                            cols = slice(c0 + QW * hd, c0 + QW * hd + QW)
                            nc.tensor.matmul(ps[0:QW, b, :], uq[:, 0, cols], cq[:, 0, :], start=True, stop=False)
                            nc.tensor.matmul(ps[0:QW, b, :], uq[0:64, 1, cols], cq[0:64, 1, :], start=False, stop=True)\
                              .then_inc(full[b], 1)
                        b = bank_to_fill(pe, jobs, ("k", hd))
                        nc.tensor.matmul(ps[0:HD, b, :], ukv[:, HD * hd:HD * hd + HD], ckv, start=True, stop=True)\
                          .then_inc(full[b], 1)
                    for tb in range(TB):
                        b = bank_to_fill(pe, jobs, ("mv", tb))
                        nc.tensor.matmul(ps[:, b, 0:256], ckv[:, tb * P:(tb + 1) * P], ukv[:, 256:512], start=True, stop=True)\
                          .then_inc(full[b], 1)
                    for m, s in steps2():
                        if s[0] is not None:
                            hd = s[0]
                            for c in range(TB):
                                b = bank_to_fill(pe, jobs, ("z", hd, c))
                                nc.tensor.matmul(ps[:, b, 0:L - c * P], sbqk[half(hd), 2 + hd // 2, c * P:(c + 1) * P],
                                                 sbqk[half(hd), hd // 2, c * P:L], start=True, stop=True).then_inc(full[b], 1)
                        if s[1] is not None:
                            hd = s[1]
                            pe.wait_ge(S["sb_masked"], hd + 1)
                            x = sp[hd % 2]
                            for c in range(TB):
                                b = bank_to_fill(pe, jobs, ("later", hd, c))
                                for c2 in range(c, TB):
                                    i = nc.tensor.matmul(ps[:, b, (c2 - c) * P:L - c * P],
                                                         cst[:, C2_TRI:C2_TRI + P] if c2 == c else ones,
                                                         x[:, ZO[c2]:ZO[c2 + 1]], start=(c2 == c), stop=(c2 == TB - 1),
                                                         skip_group_check=True)
                                i.then_inc(full[b], 1)
                        if s[2] is not None:
                            hd = s[2]
                            pe.wait_ge(S["sb_weight"], hd + 1)
                            b = bank_to_fill(pe, jobs, ("sb", hd))
                            for c in range(TB):
                                i = nc.tensor.matmul(ps[half(hd), b, c * P:L], sbv[:, c, hd * HD:(hd + 1) * HD],
                                                     zs[hd % 2][:, ZO[c]:ZO[c + 1]], start=(c == 0), stop=(c == TB - 1),
                                                     skip_group_check=True)
                            i.then_inc(full[b], 1)
                        if m[0] is not None:
                            k = m[0]
                            hd, tb = mla[k]
                            if k == 0:
                                pe.wait_ge(S["q_ready"], MLA_HEADS)
                                pe.wait_ge(S["k_ready"], MLA_HEADS)
                                for q in range(MLA_HEADS):
                                    pe.wait_ge(*read_of(jobs, ("k", q)))
                            b = bank_to_fill(pe, jobs, ("logits", k))
                            nc.tensor.matmul(ps[:, b, 0:(tb + 1) * P], mq[0:QW, hd, tb * P:(tb + 1) * P],
                                             mk[0:QW, hd, 0:(tb + 1) * P], start=True, stop=True).then_inc(full[b], 1)
                        if m[2] is not None:
                            k = m[2]
                            hd, tb = mla[k]
                            pe.wait_ge(S["scaled"], k + 1)
                            b = bank_to_fill(pe, jobs, ("pt", k))
                            for c in range(tb + 1):
                                i = nc.tensor.transpose(ps[:, b, c * P:(c + 1) * P], sc2[:, k % 4, c * P:(c + 1) * P], ident)
                            i.then_inc(full[b], 1)
                        if m[3] is not None:
                            k = m[3]
                            hd, tb = mla[k]
                            pe.wait_ge(*read_of(jobs, ("pt", k)))
                            if k == 0:
                                for q in range(TB):
                                    pe.wait_ge(*read_of(jobs, ("mv", q)))
                            b = bank_to_fill(pe, jobs, ("o", k))
                            for c in range(tb + 1):
                                i = nc.tensor.matmul(ps[half(hd), b, 0:P], mv[:, c, hd * HD:(hd + 1) * HD],
                                                     pt2[:, k % 2, c * P:(c + 1) * P], start=(c == 0), stop=(c == tb))
                            i.then_inc(full[b], 1)

                @block.scalar
                def _(act, jobs=jobs):
                    nc.scalar.activation(msq[:, 0, :], cq[:, 0, :], ACT.Square).then_inc(S["mla_squared"], 1)
                    nc.scalar.activation(msq[0:64, 1, :], cq[0:64, 1, :], ACT.Square).then_inc(S["mla_squared"], 1)
                    nc.scalar.activation(msq[:, 2, :], ckv, ACT.Square).then_inc(S["mla_squared"], 1)
                    for i, name in enumerate(("cq_sum", "ckv_sum")):
                        act.wait_ge(*read_of(jobs, name))
                        nc.scalar.activation(mrs[:, i, :], mrs[:, i, :], ACT.Sqrt).then_inc(S["root"], 1)
                    for hd in range(MLA_HEADS):
                        b = bank_filled(act, jobs, ("q", hd))
                        nc.scalar.activation(mq[0:QW, hd, :], ps[0:QW, b, :], ACT.Copy).then_inc(read[b], 1)
                        b = bank_filled(act, jobs, ("k", hd))
                        nc.scalar.activation(mk[0:HD, hd, :], ps[0:HD, b, :], ACT.Copy).then_inc(read[b], 1)
                    for tb in range(TB):
                        b = bank_filled(act, jobs, ("mv", tb))
                        nc.scalar.activation(mv[:, tb, :], ps[:, b, 0:256], ACT.Copy).then_inc(read[b], 1)
                    own = Signal(act_own)
                    for m, s in steps2():
                        if s[0] is not None:
                            hd = s[0]
                            for c in range(TB):
                                act.wait_ge(*read_of(jobs, ("z", hd, c)))
                            x = sp[hd % 2]
                            act.wait_ge(*own.up(nc.scalar.activation(x, zs[hd % 2], ACT.Abs)))
                            act.wait_ge(*own.up(nc.scalar.activation(x, x, ACT.Exp, scale=-1.0)))
                            nc.scalar.activation(x, x, ACT.Ln, bias=1.0).then_inc(S["sb_abs"], 1)
                        if s[1] is not None:
                            hd = s[1]
                            act.wait_ge(S["sb_arg"], hd + 1)
                            nc.scalar.activation(zs[hd % 2], zs[hd % 2], ACT.Exp).then_inc(S["sb_weight"], 1)
                        if s[2] is not None:
                            hd = s[2]
                            b = bank_filled(act, jobs, ("sb", hd))
                            nc.scalar.activation(o2[half(hd), hd // 2, :], ps[half(hd), b, :], ACT.Copy).then_inc(read[b], 1)
                        if m[1] is not None:
                            k = m[1]
                            w = (mla[k][1] + 1) * P
                            act.wait_ge(*read_of(jobs, ("logits", k)))
                            nc.scalar.activation(sc2[:, k % 4, 0:w], sc2[:, k % 4, 0:w], ACT.Exp, bias=small[:, k % 4:k % 4 + 1],
                                                 scale=-1.0, accum_out=small[:, 4 + k % 4:5 + k % 4]).then_inc(S["exped"], 1)
                        if m[2] is not None:
                            k = m[2]
                            w = (mla[k][1] + 1) * P
                            b = bank_filled(act, jobs, ("pt", k))
                            if k >= 2:
                                b2, n2, _ = jobs.at["o", k - 2]
                                act.wait_ge(full[b2], n2)
                            nc.scalar.activation(pt2[:, k % 2, 0:w], ps[:, b, 0:w], ACT.Copy).then_inc(read[b], 1)

                @block.gpsimd
                def _(pool, jobs=jobs):
                    pool.wait_ge(S["kr_ready"], 1)
                    for hd in range(MLA_HEADS):
                        nc.gpsimd.tensor_copy(mk[64:96, hd, :], cq[64:96, 1, :]).then_inc(S["k_ready"], 1)
                    for m, s in steps2():
                        if s[0] is not None:
                            hd = s[0]
                            pool.wait_ge(S["sb_soft"], hd + 1)
                            for c in range(TB):
                                x = sp[hd % 2][:, ZO[c]:ZO[c] + P]
                                i = nc.gpsimd.tensor_tensor(x, x, cst[:, C2_SBKEEP:C2_SBKEEP + P], ALU.mult)
                            i.then_inc(S["sb_masked"], 1)
                        if s[1] is not None:
                            hd = s[1]
                            for c in range(TB):
                                pool.wait_ge(*read_of(jobs, ("later", hd, c)))
                                x = zs[hd % 2][:, ZO[c]:ZO[c] + P]
                                i = nc.gpsimd.tensor_tensor(x, x, cst[:, C2_SBNEG:C2_SBNEG + P], ALU.add)
                            i.then_inc(S["sb_arg"], 1)
                        if m[1] is not None:
                            k = m[1]
                            w = (mla[k][1] + 1) * P
                            pool.wait_ge(S["den_ready"], k + 1)
                            nc.gpsimd.tensor_scalar(sc2[:, k % 4, 0:w], sc2[:, k % 4, 0:w], small[:, 8 + k % 4:9 + k % 4],
                                                    None, ALU.mult).then_inc(S["scaled"], 1)

                @block.vector
                def _(dve, jobs=jobs):
                    own = Signal(dve_own)
                    cs = cst[64:96, C2_COS:C2_COS + L]
                    sn = cst[64:96, C2_SIN:C2_SIN + L]
                    for i, (name, n) in enumerate((("cq_sum", Q_LORA), ("ckv_sum", P))):
                        b = bank_filled(dve, jobs, name)
                        nc.vector.tensor_scalar(mrs[:, i, :], ps[:, b, :], 1.0 / n, 1e-6, ALU.mult, ALU.add).then_inc(read[b], 1)
                    dve.wait_ge(S["root"], 2)
                    dve.wait_ge(*own.up(nc.vector.reciprocal(mrs[:, :, :], mrs[:, :, :])))
                    for x, g, i in ((cq[:, 0, :], P2_QN, 0), (cq[0:64, 1, :], P2_QN + 1, 0), (ckv, P2_KVN, 1)):
                        n = x.shape[0]
                        nc.vector.scalar_tensor_tensor(x, x, prm[0:n, g:g + 1], mrs[0:n, i, :], ALU.mult, ALU.mult)\
                          .then_inc(S["mla_normed"], 1)
                    kr = cq[64:96, 1, :]
                    own.up(nc.vector.tensor_tensor(kr, kr, cs, ALU.mult))
                    dve.wait_ge(*own.up(nc.vector.tensor_tensor(krs[64:96, :], krs[64:96, :], sn, ALU.mult)))
                    nc.vector.tensor_tensor(kr, kr, krs[64:96, :], ALU.add).then_inc(S["kr_ready"], 1)
                    for hd in range(MLA_HEADS):
                        b = bank_filled(dve, jobs, ("qs", hd))
                        tmp = msq[64:96, hd % 2, :]
                        if hd == 0:
                            dve.wait_ge(S["mla_normed"], 3)
                        if hd >= 2:
                            dve.wait_ge(S["q_ready"], hd - 1)
                        nc.vector.tensor_tensor(tmp, ps[64:96, b, :], sn, ALU.mult).then_inc(read[b], 1)
                        dve.wait_ge(*read_of(jobs, ("q", hd)))
                        x = mq[64:96, hd, :]
                        dve.wait_ge(*own.up(nc.vector.tensor_tensor(x, x, cs, ALU.mult)))
                        dve.wait_ge(*read_of(jobs, ("qs", hd)))
                        nc.vector.tensor_tensor(x, x, tmp, ALU.add).then_inc(S["q_ready"], 1)
                    for m, s in steps2():
                        if s[0] is not None:
                            hd = s[0]
                            if hd >= 2:
                                b, n, _ = jobs.at["sb", hd - 2]
                                dve.wait_ge(full[b], n)
                            for c in range(TB):
                                b = bank_filled(dve, jobs, ("z", hd, c))
                                nc.vector.tensor_scalar(zs[hd % 2][:, ZO[c]:ZO[c + 1]], ps[:, b, 0:L - c * P], HD ** -0.5, None,
                                                        ALU.mult).then_inc(read[b], 1)
                        if m[0] is not None:
                            k = m[0]
                            w = (mla[k][1] + 1) * P
                            if k >= 4:
                                b, n, _ = jobs.at["pt", k - 4]
                                dve.wait_ge(full[b], n)
                            b = bank_filled(dve, jobs, ("logits", k))
                            nc.vector.tensor_tensor_reduce(out=sc2[:, k % 4, 0:w], in0=ps[:, b, 0:w],
                                                           in1=cst[:, C2_CAUSAL + L - w:C2_CAUSAL + L],
                                                           scale=-(QW ** -0.5), scalar=-NEG, op0=ALU.add, op1=ALU.min,
                                                           accum_out=small[:, k % 4:k % 4 + 1]).then_inc(read[b], 1)
                        if s[0] is not None:
                            hd = s[0]
                            dve.wait_ge(S["sb_abs"], hd + 1)
                            nc.vector.scalar_tensor_tensor(sp[hd % 2], zs[hd % 2], 0.0, sp[hd % 2], ALU.max, ALU.add)\
                              .then_inc(S["sb_soft"], 1)
                        if s[1] is not None:
                            hd = s[1]
                            for c in range(TB):
                                b = bank_filled(dve, jobs, ("later", hd, c))
                                x = zs[hd % 2][:, ZO[c]:ZO[c + 1]]
                                nc.vector.tensor_tensor(x, x, ps[:, b, 0:L - c * P], ALU.subtract).then_inc(read[b], 1)
                        if m[1] is not None:
                            k = m[1]
                            dve.wait_ge(S["exped"], k + 1)
                            nc.vector.reciprocal(small[:, 8 + k % 4:9 + k % 4], small[:, 4 + k % 4:5 + k % 4])\
                              .then_inc(S["den_ready"], 1)
                        if m[3] is not None:
                            k = m[3]
                            hd, tb = mla[k]
                            b = bank_filled(dve, jobs, ("o", k))
                            nc.vector.tensor_copy(o2[half(hd), 2 + hd // 2, tb * P:(tb + 1) * P], ps[half(hd), b, 0:P])\
                              .then_inc(read[b], 1)
            close_block()

            alpha, beta, bonus = room_at(16384, PAIRS, L), room_at(18432, PAIRS, L), room_at(20480, PAIRS, L)
            w1t, w2t, w3t, w4t = (room_at(22528 + 2048 * i, PAIRS, L) for i in range(4))
            w5t, w6t = room_at(0, PAIRS, L), room_at(2048, PAIRS, L)
            xs = [room_at(0, PAIRS, 2 * P), room_at(22528, PAIRS, 2 * P)]
            x3 = [room_at(1024, 3, PAIRS * P), room_at(23552, 3, PAIRS * P)]
            xt = [room_at(2560, PAIRS, 3 * P), room_at(25088, PAIRS, 3 * P)]
            m4 = [room_at(26624, PAIRS, 4 * P), room_at(28672, PAIRS, 4 * P)]
            inv = [uu[:, 0:512], uu[:, 512:1024]]
            state, rbuf, xbuf = uu[:, 1024:1536], uu[:, 1536:2048], uu[:, 2048:2560]
            lora = uu[:, 2560:3584]
            dend = uu[:, 3584:3616].rearrange("p (a b) -> p a b", b=NCH)
            y = room_at(14336, PAIRS, L)
            rs = ring[:, :, :].rearrange("p a b -> p (a b)")
            names = ("nd", "no", "ndt", "q1", "p2", "ip2", "p2t", "ip4", "wt", "et", "e", "m", "mt", "q2", "m2", "m2t")
            tmp = {n: rs[:, 512 * i:512 * (i + 1)] for i, n in enumerate(names)}
            tmp.update(im2=tmp["p2"], im4=tmp["p2t"], f1=tmp["ip2"], ft=tmp["ip4"])
            i4 = cst[:, C2_I4:C2_I4 + 512]

            def pr(x, p):
                return x[:, p * P:(p + 1) * P]

            SOLVE = [
                [("p2", "ndt", "nd", "act"), ("p2t", "nd", "ndt", "dve")],
                [("ip4", "p2t", "p2", "plus"), ("wt", "ip2", "q1", "act")],
                [("et", "ip4", "wt", "dve"), ("e", "wt", "ip4", "act")],
                [("m", "et", "no", "act"), ("mt", "no", "et", "dve")],
                [("m2", "mt", "m", "act"), ("m2t", "m", "mt", "dve")],
                [("im4", "m2t", "m2", "plus"), ("f1", "im2", "q2", "act")],
                [("ft", "im4", "f1", "act")],
                [("inv", "e", "ft", "dve")],
            ]
            AFTER = {"p2": ("ip2", ALU.add), "mt": ("q2", ALU.subtract), "m2": ("im2", ALU.add)}
            CHAIN = {1: "r", 2: "x", 3: "t", 4: "y"}

            jobs = Banks()
            for name in ("w", "a"):
                for p in range(PAIRS):
                    jobs.plan((name, p))
            for name in ("kk", "bonus"):
                for p in range(PAIRS):
                    jobs.plan((name, p))
            for c in range(NCH + 1):
                if c < NCH:
                    for p in range(PAIRS):
                        jobs.plan(("first", c, p))
                        jobs.plan(("second", c, p))
                for s in range(len(SOLVE)):
                    if c < NCH:
                        for res, *_ in SOLVE[s]:
                            jobs.plan((res, c))
                    if c > 0 and s in CHAIN:
                        jobs.plan((CHAIN[s], c - 1))
            for name in ("mean", "var", "g"):
                for p in range(PAIRS):
                    jobs.plan((name, p))

            def wait_operand(pe, jobs, c, x):
                if x in ("nd", "no"):
                    pe.wait_ge(*read_of(jobs, ("second", c, PAIRS - 1)))
                elif x == "ndt" or x == "q1":
                    pe.wait_ge(S["nd_ready"], 2 * c + (1 if x == "ndt" else 2))
                elif x in ("ip2", "q2", "im2"):
                    pe.wait_ge(S["sq_plus"], 3 * c + ("ip2", "q2", "im2").index(x) + 1)
                else:
                    pe.wait_ge(*read_of(jobs, (x, c)))

            def chain_pe(pe, jobs, c, what):
                q = c % 2
                b = bank_to_fill(pe, jobs, (what, c))
                if what == "r":
                    pe.wait_ge(S["state_ready"], c + 1)
                    pe.wait_ge(*read_of(jobs, ("first", c, PAIRS - 1)))
                    pe.wait_ge(*read_of(jobs, ("second", c, PAIRS - 1)))
                    pe.wait_ge(S["solved"], PAIRS * (c + 1))
                if what == "x":
                    pe.wait_ge(*read_of(jobs, ("inv", c)))
                    pe.wait_ge(*read_of(jobs, ("r", c)))
                if what == "t":
                    pe.wait_ge(*read_of(jobs, ("x", c)))
                for p in range(PAIRS):
                    out = ps[:, b, p * P:(p + 1) * P]
                    bt, kt, vt = (xt[q][:, p, i * P:(i + 1) * P] for i in range(3))
                    al, rho = xs[q][:, p, 0:P], xs[q][:, p, P:2 * P]
                    mb, gt, mk2 = (m4[q][:, p, i * P:(i + 1) * P] for i in (1, 2, 3))
                    pairs = {"r": [(al, pr(state, p)), (gt, vt)],
                             "x": [(pr(inv[q], p), pr(rbuf, p))],
                             "t": [(bt, pr(xbuf, p)), (kt, vt)],
                             "y": [(pr(state, p), rho), (pr(xbuf, p), mb), (vt, mk2)]}[what]
                    for i, (lhs, rhs) in enumerate(pairs):
                        m = nc.tensor.matmul(out, lhs, rhs, start=(p == 0 and i == 0),
                                             stop=(p == PAIRS - 1 and i == len(pairs) - 1), skip_group_check=True)
                m.then_inc(full[b], 1)

            def expand(pool, c):
                q = c % 2
                t = slice(c * CH, (c + 1) * CH)
                blocks = [x3[q][:, i, :].rearrange("p (a b) -> p a b", b=P) for i in range(3)]
                for src, dst, at in ((alpha, xs[q], 0), (rr, xs[q], P), (beta, blocks[0], 0), (rk, blocks[1], 0),
                                     (rv, blocks[2], 0)):
                    for hh in range(2):
                        nc.gpsimd.tensor_scalar(dst[:, :, at + 64 * hh:at + 64 * hh + 64], src[:, :, t],
                                                cst[:, hh:hh + 1], None, ALU.mult).then_inc(S["expanded"], 1)

            with nc.Block() as block:
                @block.sync
                def _(sy, jobs=jobs):
                    sy.dma_start(lora, d["w2"][bass.ds(layer, 1), S2_LORA, :, 0:1024].rearrange("a p c -> p (a c)"))\
                      .then_inc(loaded, 16)
                    sy.wait_ge(loaded, 16)

                @block.tensor
                def _(pe, jobs=jobs):
                    pe.wait_ge(loaded, 16)
                    pe.wait_ge(S["lora_in"], 1)
                    for name, rows, src in (("w", slice(0, 64), wdad), ("a", slice(64, 128), wdad)):
                        for p in range(PAIRS):
                            b = bank_to_fill(pe, jobs, (name, p))
                            nc.tensor.matmul(ps[:, b, :], lora[rows, p * P:(p + 1) * P], src[rows, :], start=True, stop=True)\
                              .then_inc(full[b], 1)
                    for name, src, sig in (("kk", w4t, "kk_sq"), ("bonus", bonus, "first_masked")):
                        for p in range(PAIRS):
                            b = bank_to_fill(pe, jobs, (name, p))
                            pe.wait_ge(S[sig], p + 1)
                            nc.tensor.matmul(ps[:, b, :], blk, src[:, p, :], start=True, stop=True).then_inc(full[b], 1)
                    for c in range(NCH + 1):
                        q = c % 2
                        if c < NCH:
                            pe.wait_ge(S["expanded"], 10 * (c + 1))
                            for p in range(PAIRS):
                                b = bank_to_fill(pe, jobs, ("first", c, p))
                                bt, kt, vv = (pr(x3[q][:, i, :], p) for i in range(3))
                                nc.tensor.matmul(ps[:, b, 0:256], bt, xs[q][:, p, :], start=True, stop=False,
                                                 skip_group_check=True)
                                nc.tensor.matmul(ps[:, b, 256:512], kt, xs[q][:, p, :], start=False, stop=True,
                                                 skip_group_check=True).then_inc(full[b], 1)
                                b = bank_to_fill(pe, jobs, ("second", c, p))
                                for i, v in enumerate((bt, kt, vv)):
                                    nc.tensor.transpose(ps[:, b, i * P:(i + 1) * P], v, ident)
                                nc.tensor.matmul(ps[:, b, 384:512], xs[q][:, p, 0:P], bt, start=True, stop=True,
                                                 skip_group_check=True).then_inc(full[b], 1)
                        for s in range(len(SOLVE)):
                            if c < NCH:
                                for res, lhs, rhs, _ in SOLVE[s]:
                                    for x in (lhs, rhs):
                                        wait_operand(pe, jobs, c, x)
                                    b = bank_to_fill(pe, jobs, (res, c))
                                    for p in range(PAIRS):
                                        m = nc.tensor.matmul(ps[:, b, p * P:(p + 1) * P], pr(tmp[lhs], p), pr(tmp[rhs], p),
                                                             start=(p == 0), stop=(p == PAIRS - 1), skip_group_check=True)
                                    m.then_inc(full[b], 1)
                            if c > 0 and s in CHAIN:
                                chain_pe(pe, jobs, c - 1, CHAIN[s])
                    for name, src, sig in (("mean", y, None), ("var", w2t, "squared")):
                        for p in range(PAIRS):
                            b = bank_to_fill(pe, jobs, (name, p))
                            if sig is None:
                                pe.wait_ge(*read_of(jobs, ("y", NCH - 1)))
                            else:
                                pe.wait_ge(S[sig], p + 1)
                            nc.tensor.matmul(ps[:, b, :], blk, src[:, p, :], start=True, stop=True).then_inc(full[b], 1)
                    for p in range(PAIRS):
                        b = bank_to_fill(pe, jobs, ("g", p))
                        nc.tensor.matmul(ps[:, b, :], lora[:, 512 + p * P:512 + (p + 1) * P], gd, start=True, stop=True)\
                          .then_inc(full[b], 1)

                @block.scalar
                def _(act, jobs=jobs):
                    nc.scalar.activation(gd, gd, ACT.Sigmoid)
                    nc.scalar.activation(wdad[0:64, :], wdad[0:64, :], ACT.Tanh).then_inc(S["lora_in"], 1)
                    for p in range(PAIRS):
                        b = bank_filled(act, jobs, ("w", p))
                        nc.scalar.activation(w1t[:, p, :], ps[:, b, :], ACT.Sigmoid, bias=prm_col(P2_W0 + p)).then_inc(read[b], 1)
                    for p in range(PAIRS):
                        b = bank_filled(act, jobs, ("a", p))
                        nc.scalar.activation(w5t[:, p, :], ps[:, b, :], ACT.Sigmoid, bias=prm_col(P2_A0 + p)).then_inc(read[b], 1)
                    for p in range(PAIRS):
                        nc.scalar.activation(w4t[:, p, :], rk[:, p, :], ACT.Square, scale=prm_col(P2_KK + p))\
                          .then_inc(S["kk_sq"], 1)
                    for p in range(PAIRS):
                        act.wait_ge(*read_of(jobs, ("kk", p)))
                        nc.scalar.activation(w6t[:, p, :], w6t[:, p, :], ACT.Sqrt).then_inc(S["kk_root"], 1)
                    act.wait_ge(S["decayed"], PAIRS)
                    act.wait_ge(S["decayed"], PAIRS + 1)
                    nc.scalar.activation(w2t, w3t, ACT.Exp).then_inc(S["chunk_in"], 1)
                    act.wait_ge(S["decayed"], PAIRS + 2)
                    nc.scalar.activation(w3t, w3t, ACT.Exp, scale=-1.0).then_inc(S["chunk_in"], 1)
                    nc.scalar.activation(w1t, w1t, ACT.Exp).then_inc(S["chunk_in"], 1)
                    for c in range(NCH + 1):
                        if c < NCH:
                            for p in range(PAIRS):
                                b = bank_filled(act, jobs, ("second", c, p))
                                act.wait_ge(S["solved"], PAIRS * c + p + 1)
                                nc.scalar.activation(xt[c % 2][:, p, :], ps[:, b, 0:384], ACT.Copy).then_inc(read[b], 1)
                        for s in range(len(SOLVE)):
                            if c < NCH:
                                for res, _, _, who in SOLVE[s]:
                                    if who == "act":
                                        b = bank_filled(act, jobs, (res, c))
                                        nc.scalar.activation(tmp[res], ps[:, b, :], ACT.Copy).then_inc(read[b], 1)
                            if c > 0 and s in CHAIN:
                                what = CHAIN[s]
                                if what in "rx":
                                    b = bank_filled(act, jobs, (what, c - 1))
                                    nc.scalar.activation(rbuf if what == "r" else xbuf, ps[:, b, :], ACT.Copy,
                                                         scale=-1.0 if what == "r" else 1.0).then_inc(read[b], 1)
                                if what == "y":
                                    b = bank_filled(act, jobs, (what, c - 1))
                                    src = ps[:, b, :].rearrange("p (a b) -> p a b", b=P)
                                    t = slice((c - 1) * CH, c * CH)
                                    nc.scalar.activation(y[0:64, :, t], src[0:64, :, 0:64], ACT.Copy)
                                    nc.scalar.activation(y[64:128, :, t], src[64:128, :, 64:128], ACT.Copy).then_inc(read[b], 1)
                    for p in range(PAIRS):
                        act.wait_ge(*read_of(jobs, ("mean", p)))
                        nc.scalar.activation(w2t[:, p, :], w1t[:, p, :], ACT.Square).then_inc(S["squared"], 1)
                    for p in range(PAIRS):
                        act.wait_ge(*read_of(jobs, ("var", p)))
                        nc.scalar.activation(w3t[:, p, :], w3t[:, p, :], ACT.Sqrt).then_inc(S["root"], 1)

                @block.gpsimd
                def _(pool, jobs=jobs):
                    pool.wait_ge(S["zeroed"], 1)
                    nc.gpsimd.memset(state, 0.0).then_inc(S["state_ready"], 1)
                    expand(pool, 0)
                    for c in range(NCH + 1):
                        ndt = tmp["ndt"]
                        if c < NCH:
                            pool.wait_ge(*read_of(jobs, ("second", c, PAIRS - 1)))
                            pool.wait_ge(S["solved"], PAIRS * (c + 1))
                            nc.gpsimd.tensor_tensor(ndt.rearrange("p (a b) -> p a b", b=P), m4[c % 2][:, :, 0:P],
                                                    cst[:, C2_NDT:C2_NDT + 512].rearrange("p (a b) -> p a b", b=P), ALU.mult)\
                              .then_inc(S["nd_ready"], 1)
                            pool.wait_ge(S["nd_ready"], 2 * c + 1)
                            nc.gpsimd.tensor_tensor(tmp["q1"], i4, ndt, ALU.subtract).then_inc(S["nd_ready"], 1)
                        for s in range(len(SOLVE)):
                            if c < NCH:
                                for res, *_ in SOLVE[s]:
                                    if res in AFTER:
                                        dst, op = AFTER[res]
                                        pool.wait_ge(*read_of(jobs, (res, c)))
                                        nc.gpsimd.tensor_tensor(tmp[dst], i4, tmp[res], op).then_inc(S["sq_plus"], 1)
                            if s == 5 and c + 1 < NCH:
                                if c > 0:
                                    b, n, _ = jobs.at["y", c - 1]
                                    pool.wait_ge(full[b], n)
                                expand(pool, c + 1)

                @block.vector
                def _(dve, jobs=jobs):
                    own = Signal(dve_own)
                    chain = lambda i: dve.wait_ge(*own.up(i))
                    for p in range(PAIRS):
                        b = bank_filled(dve, jobs, ("kk", p))
                        nc.vector.tensor_scalar(w6t[:, p, :], ps[:, b, :], 1e-12, None, ALU.max).then_inc(read[b], 1)
                    for p in range(PAIRS):
                        dve.wait_ge(*read_of(jobs, ("w", p)))
                    chain(nc.vector.tensor_scalar(w1t, w1t, -float(np.exp(-0.5)), None, ALU.mult))
                    for p in range(PAIRS):
                        nc.vector.tensor_tensor_scan(w3t[:, p, :], cst[:, C2_RESET:C2_RESET + L], w1t[:, p, :], 0.0,
                                                     ALU.mult, ALU.add).then_inc(S["decayed"], 1)
                    dve.wait_ge(S["decayed"], PAIRS)
                    nc.vector.tensor_tensor(w1t, w3t, w1t, ALU.subtract).then_inc(S["decayed"], 1)
                    dve.wait_ge(S["kk_root"], PAIRS)
                    chain(nc.vector.reciprocal(w6t, w6t))
                    for p in range(PAIRS):
                        i = own.up(nc.vector.scalar_tensor_tensor(alpha[:, p, :], rk[:, p, :], prm_col(P2_KK + p), w6t[:, p, :],
                                                                  ALU.mult, ALU.mult))
                    dve.wait_ge(*i)
                    for p in range(PAIRS):
                        dve.wait_ge(*read_of(jobs, ("a", p)))
                    chain(nc.vector.tensor_tensor(beta, alpha, w5t, ALU.mult))
                    for p in range(PAIRS):
                        i = own.up(nc.vector.tensor_scalar(w5t[:, p, :], w5t[:, p, :], 1.0, prm_col(P2_KA + p),
                                                           ALU.subtract, ALU.mult))
                    dve.wait_ge(*i)
                    dve.wait_ge(S["kk_sq"], PAIRS)
                    chain(nc.vector.scalar_tensor_tensor(rk, w5t, 1.0, rk, ALU.add, ALU.mult))
                    for p in range(PAIRS):
                        nc.vector.scalar_tensor_tensor(bonus[:, p, :], rr[:, p, :], prm_col(P2_RK + p), rk[:, p, :],
                                                       ALU.mult, ALU.mult).then_inc(S["first_masked"], 1)
                    dve.wait_ge(S["chunk_in"], 1)
                    dve.wait_ge(S["first_masked"], PAIRS)
                    chain(nc.vector.tensor_copy(dend, w2t[:, :, CH - 1:L:CH]))
                    nc.vector.tensor_tensor(rr, rr, w2t, ALU.mult).then_inc(S["decayed"], 1)
                    dve.wait_ge(S["chunk_in"], 2)
                    chain(nc.vector.tensor_tensor(beta, beta, w3t, ALU.mult))
                    chain(nc.vector.tensor_tensor(rk, rk, w3t, ALU.mult))
                    dve.wait_ge(S["chunk_in"], 3)
                    chain(nc.vector.tensor_tensor(alpha, alpha, w1t, ALU.mult))
                    for p in range(PAIRS):
                        b = bank_filled(dve, jobs, ("bonus", p))
                        nc.vector.tensor_tensor(bonus[:, p, :], ps[:, b, :], rv[:, p, :], ALU.mult).then_inc(read[b], 1)
                    for p in range(PAIRS):
                        dve.wait_ge(*read_of(jobs, ("bonus", p)))
                    dve.wait_ge(S["decayed"], PAIRS + 2)
                    chain(nc.vector.tensor_copy(small[:, 40:41], bonus[:, 0, 0:1]))
                    nc.vector.tensor_copy(small[:, 41:42], small[:, 40:41]).then_inc(S["zeroed"], 1)
                    for c in range(NCH + 1):
                        q = c % 2
                        if c < NCH:
                            if c > 0:
                                b, n, _ = jobs.at["inv", c - 1]
                                dve.wait_ge(full[b], n)
                            for p in range(PAIRS):
                                b = bank_filled(dve, jobs, ("first", c, p))
                                nc.vector.tensor_tensor(m4[q][:, p, :], ps[:, b, :], cst[:, C2_RW:C2_RW + 512], ALU.mult)\
                                  .then_inc(read[b], 1)
                                dve.wait_ge(*read_of(jobs, ("first", c, p)))
                                b = bank_filled(dve, jobs, ("second", c, p))
                                own.up(nc.vector.tensor_tensor(pr(tmp["nd"], p), ps[:, b, 384:512], cst[:, C2_ND:C2_ND + P], ALU.mult))
                                nc.vector.tensor_tensor(pr(tmp["no"], p), ps[:, b, 384:512], cst[:, C2_NO:C2_NO + P], ALU.mult)\
                                  .then_inc(S["solved"], 1)
                        for s in range(len(SOLVE)):
                            if c < NCH:
                                for res, _, _, who in SOLVE[s]:
                                    if who == "act":
                                        continue
                                    b = bank_filled(dve, jobs, (res, c))
                                    dst = inv[q] if res == "inv" else tmp[res]
                                    if who == "plus":
                                        i = nc.vector.tensor_tensor(dst, ps[:, b, :], i4, ALU.add)
                                    else:
                                        i = nc.vector.tensor_copy(dst, ps[:, b, :])
                                    i.then_inc(read[b], 1)
                            if c > 0 and s in CHAIN and CHAIN[s] == "y" and c < NCH:
                                pass
                            if c > 0 and s in CHAIN and CHAIN[s] == "y":
                                b, n, _ = jobs.at["y", c - 1]
                                dve.wait_ge(full[b], n)
                                b = bank_filled(dve, jobs, ("t", c - 1))
                                nc.vector.tensor_tensor(state, state, ps[:, b, :], ALU.add).then_inc(read[b], 1)
                                dve.wait_ge(*read_of(jobs, ("t", c - 1)))
                                st = state.rearrange("p (a b) -> p a b", b=P)
                                nc.vector.tensor_tensor(st, st, dend[:, :, c - 1:c].to_broadcast([P, PAIRS, P]), ALU.mult)\
                                  .then_inc(S["state_ready"], 1)
                    for p in range(PAIRS):
                        b = bank_filled(dve, jobs, ("mean", p))
                        nc.vector.scalar_tensor_tensor(w1t[:, p, :], ps[:, b, :], -1.0 / HD, y[:, p, :], ALU.mult, ALU.add)\
                          .then_inc(read[b], 1)
                    for p in range(PAIRS):
                        b = bank_filled(dve, jobs, ("var", p))
                        nc.vector.tensor_scalar(w3t[:, p, :], ps[:, b, :], 1.0 / HD, 64e-5, ALU.mult, ALU.add).then_inc(read[b], 1)
                    dve.wait_ge(S["root"], PAIRS)
                    chain(nc.vector.reciprocal(w3t, w3t))
                    for p in range(PAIRS):
                        i = own.up(nc.vector.scalar_tensor_tensor(w1t[:, p, :], w1t[:, p, :], prm_col(P2_GNG + p), w3t[:, p, :],
                                                                  ALU.mult, ALU.mult))
                    dve.wait_ge(*i)
                    for p in range(PAIRS):
                        i = own.up(nc.vector.scalar_tensor_tensor(w1t[:, p, :], w1t[:, p, :], prm_col(P2_GNB + p), bonus[:, p, :],
                                                                  ALU.add, ALU.add))
                    dve.wait_ge(*i)
                    for p in range(PAIRS):
                        b = bank_filled(dve, jobs, ("g", p))
                        nc.vector.tensor_tensor(o2[:, 4 + p, :], w1t[:, p, :], ps[:, b, :], ALU.mult).then_inc(read[b], 1)
            close_block()

            hid2 = room_at(0, FF2, L)
            cv2 = room_at(22528, 2, L)
            ge = room_at(23552, 2, L)
            nrm = room_at(24576, L)
            nx = room_at(25088, L)
            ROUNDS = 5
            jobs = Banks(start=1)
            for n in range(DC):
                jobs.plan(("wo", n))
            for name in ("mean1", "var1"):
                jobs.plan(name)
            jobs.plan_body([(w, j) for j in range(4) for w in ("conv", "up")], ROUNDS)
            for j in range(FF2 - 4 * ROUNDS):
                for w in ("conv", "up"):
                    jobs.plan((w, 4 + j))
            for n in range(DC):
                jobs.plan(("down", n))
            for name in ("mean2", "var2"):
                jobs.plan(name)

            def ln_pe(pe, name, squared):
                b = bank_to_fill(pe, jobs, name)
                for c in range(DC):
                    pe.wait_ge(S["squared" if squared else "h_ready"], (squared - 1 if squared else 0) + c + 1)
                    m = nc.tensor.matmul(ps[:, b, :], ones, (u if squared else h)[:, c, :], start=(c == 0), stop=(c == DC - 1))
                m.then_inc(full[b], 1)

            def ln_act(act, i):
                for c in range(DC):
                    act.wait_ge(S["centered"], DC * i + c + 1)
                    nc.scalar.activation(u[:, c, :], h[:, c, :], ACT.Square).then_inc(S["squared"], 1)
                act.wait_ge(*read_of(jobs, f"var{i + 1}"))
                nc.scalar.activation(nrm, nrm, ACT.Sqrt).then_inc(S["root"], 1)
                for c in range(DC):
                    act.wait_ge(S["normed"], DC * i + c + 1)
                    g = (P2_LN1B, P2_LN2B)[i] + c
                    nc.scalar.activation(h[:, c, :], h[:, c, :], ACT.Identity, bias=prm_col(g)).then_inc(S["ln_out"], 1)

            def ln_dve(dve, i, own):
                b = bank_filled(dve, jobs, f"mean{i + 1}")
                nc.vector.tensor_scalar(nx, ps[:, b, :], -1.0 / D, None, ALU.mult).then_inc(read[b], 1)
                dve.wait_ge(*read_of(jobs, f"mean{i + 1}"))
                for c in range(DC):
                    nc.vector.tensor_tensor(h[:, c, :], h[:, c, :], nx, ALU.add).then_inc(S["centered"], 1)
                b = bank_filled(dve, jobs, f"var{i + 1}")
                nc.vector.tensor_scalar(nrm, ps[:, b, :], 1.0 / D, 1e-5, ALU.mult, ALU.add).then_inc(read[b], 1)
                dve.wait_ge(S["root"], i + 1)
                dve.wait_ge(*own.up(nc.vector.reciprocal(nrm, nrm)))
                for c in range(DC):
                    g = (P2_LN1G, P2_LN2G)[i] + c
                    nc.vector.scalar_tensor_tensor(h[:, c, :], h[:, c, :], prm_col(g), nrm, ALU.mult, ALU.mult)\
                      .then_inc(S["normed"], 1)

            def at(x, k):
                if isinstance(k, int):
                    return x[:, k, :]
                return x[:, bass.ds(k, 1), :].rearrange("p a c -> p (a c)")

            def col(c, k):
                return prm[:, c + k:c + k + 1] if isinstance(k, int) else prm[:, bass.ds(k + c, 1)]

            with nc.Block() as block:
                @block.sync
                def _(sy, jobs=jobs):
                    def fetch(k, j):
                        sy.dma_start(ring[:, j, 0:2048],
                                     d["w2"][bass.ds(layer, 1), bass.ds(k, 1), :, 0:2048].rearrange("a b p c -> p (a b c)"))\
                          .then_inc(landed[j], 16)

                    for j in range(4):
                        fetch(S2_WO + j, j)
                    for j in range(4):
                        b, n, _ = jobs.at["wo", 2 * j + 1]
                        sy.wait_ge(full[b], n)
                        fetch(S2_UP + j, j)
                    with sy.Fori(1, ROUNDS) as it:
                        for j in range(4):
                            b, n, per = jobs.at["up", j]
                            sy.wait_ge(full[b], (it - 1) * per + n)
                            fetch(it * 4 + (S2_UP + j), j)
                    for j in range(4):
                        b, n, per = jobs.at["up", j]
                        sy.wait_ge(full[b], (ROUNDS - 1) * per + n)
                        fetch(S2_UP + 4 * ROUNDS + j, j)
                    for j in range(2):
                        b, n, _ = jobs.at["up", 4 + j]
                        sy.wait_ge(full[b], n)
                        fetch(S2_DOWN + 2 + j, j)
                    for k in range(4, FF2 // 2):
                        sy.wait_ge(S["slab_used"], k - 3)
                        fetch(S2_DOWN + k, (k + 2) % 4)

                @block.tensor
                def _(pe, jobs=jobs):
                    for b in range(8):
                        pe.sem_inc(full[b], 1)
                        pe.sem_inc(read[b], 1)
                    for n in range(DC):
                        if n % 2 == 0:
                            pe.wait_ge(landed[n // 2], 16)
                        dense_tile(pe, jobs, ("wo", n), n // 2, n % 2, o2)
                    ln_pe(pe, "mean1", 0)
                    ln_pe(pe, "var1", 1)
                    pe.wait_ge(S["ln_out"], DC)
                    with pe.Fori(0, ROUNDS) as it:
                        for j in range(4):
                            pe.wait_ge(landed[j], it * 16 + 32)
                            dense_tile(pe, jobs, ("conv", j), j, 0, h, it=it)
                            dense_tile(pe, jobs, ("up", j), j, 1, h, it=it)
                    for j in range(2):
                        pe.wait_ge(landed[j], 16 * (ROUNDS + 2))
                        dense_tile(pe, jobs, ("conv", 4 + j), j, 0, h)
                        dense_tile(pe, jobs, ("up", 4 + j), j, 1, h)
                    pe.wait_ge(S["hidden_kept"], FF2)
                    for k in range(FF2 // 2):
                        s = (k + 2) % 4
                        pe.wait_ge(landed[s], 16 * (ROUNDS + 2 + (k + 2) // 4))
                        w = ring[:, s, 0:2048].rearrange("p (k c) -> p k c", c=D)
                        for c in range(2):
                            for n in range(DC):
                                b = jobs.at["down", n][0]
                                if k == 0 and c == 0:
                                    bank_to_fill(pe, jobs, ("down", n))
                                end = k == FF2 // 2 - 1 and c == 1
                                m = nc.tensor.matmul(ps[:, b, :], w[:, c, n * P:(n + 1) * P], hid2[:, 2 * k + c, :],
                                                     start=(k == 0 and c == 0), stop=end)
                                if end:
                                    m.then_inc(full[b], 1)
                        if k < FF2 // 2 - 1:
                            m.then_inc(S["slab_used"], 1)
                    b = bank_to_fill(pe, jobs, "mean2")
                    for c in range(DC):
                        pe.wait_ge(*read_of(jobs, ("down", c)))
                        m = nc.tensor.matmul(ps[:, b, :], ones, h[:, c, :], start=(c == 0), stop=(c == DC - 1))
                    m.then_inc(full[b], 1)
                    ln_pe(pe, "var2", DC + 1)

                @block.scalar
                def _(act, jobs=jobs):
                    ln_act(act, 0)

                    def pair(j, k, it, seq):
                        b = bank_filled(act, jobs, ("conv", j), it)
                        act.wait_ge(S["hidden_kept"], seq + 1)
                        nc.scalar.activation(cv2[:, j % 2, :], ps[:, b, :], ACT.Identity, bias=col(P2_CB, k),
                                             scale=col(P2_CW + 2 * FF2, k)).then_inc(S["mixed"], 1)
                        act.wait_ge(S["shifted"], seq + 1)
                        nc.scalar.activation(ge[:, j % 2, :], cv2[:, j % 2, :], ACT.Gelu).then_inc(S["gelu"], 1)

                    with act.Fori(0, ROUNDS) as it:
                        for j in range(4):
                            pair(j, it * 4 + j, it, it * 4 + j)
                    for j in range(2):
                        pair(4 + j, 4 * ROUNDS + j, None, 4 * ROUNDS + j)
                    ln_act(act, 1)

                @block.vector
                def _(dve, jobs=jobs):
                    own = Signal(dve_own)
                    dve.sem_inc(S["hidden_kept"], 2)
                    for n in range(DC):
                        b = bank_filled(dve, jobs, ("wo", n))
                        nc.vector.scalar_tensor_tensor(h[:, n, :], h[:, n, :], ALPHA, ps[:, b, :], ALU.mult, ALU.add)\
                          .then_inc(read[b], 1)
                        dve.wait_ge(*read_of(jobs, ("wo", n)))
                        dve.sem_inc(S["h_ready"], 1)
                    ln_dve(dve, 0, own)

                    def pair(j, k, it, seq):
                        x = cv2[:, j % 2, :]
                        b = bank_filled(dve, jobs, ("conv", j), it)
                        dve.wait_ge(S["mixed"], seq + 1)
                        nc.vector.scalar_tensor_tensor(x[:, 1:L], ps[:, b, 0:L - 1], col(P2_CW + FF2, k), x[:, 1:L],
                                                       ALU.mult, ALU.add).then_inc(dve_own, 1)
                        dve.wait_ge(dve_own, seq + 2)
                        nc.vector.scalar_tensor_tensor(x[:, 2:L], ps[:, b, 0:L - 2], col(P2_CW, k), x[:, 2:L],
                                                       ALU.mult, ALU.add).then_inc(read[b], 1)
                        dve.wait_ge(*read_of(jobs, ("conv", j), it))
                        dve.sem_inc(S["shifted"], 1)
                        b = bank_filled(dve, jobs, ("up", j), it)
                        dve.wait_ge(S["gelu"], seq + 1)
                        nc.vector.tensor_tensor(at(hid2, k), ge[:, j % 2, :], ps[:, b, :], ALU.mult).then_inc(read[b], 1)
                        dve.wait_ge(*read_of(jobs, ("up", j), it))
                        dve.sem_inc(S["hidden_kept"], 1)

                    with dve.Fori(0, ROUNDS) as it:
                        for j in range(4):
                            pair(j, it * 4 + j, it, it * 4 + j)
                    for j in range(2):
                        pair(4 + j, 4 * ROUNDS + j, None, 4 * ROUNDS + j)
                    own.n += FF2
                    for n in range(DC):
                        b = bank_filled(dve, jobs, ("down", n))
                        nc.vector.scalar_tensor_tensor(h[:, n, :], h[:, n, :], ALPHA, ps[:, b, :], ALU.mult, ALU.add)\
                          .then_inc(read[b], 1)
                    for n in range(DC):
                        dve.wait_ge(*read_of(jobs, ("down", n)))
                    ln_dve(dve, 1, own)
            close_block()

        with nc.Block() as block:
            @block.sync
            def _(sy):
                for c in range(DC):
                    sy.dma_start(d["out"][c], h[:, c, :]).then_inc(stored, 16)
                sy.wait_ge(stored, 16 * DC)


def _slabs(w, cols):
    w = w[:, cols]
    k, n = w.shape
    w = w.reshape(k // P, P, n // 256, 256).transpose(2, 1, 0, 3)
    return w.reshape(n // 256, P, (k // P) * 256)


def _padded(x, width=SLOT):
    out = np.zeros(x.shape[:-1] + (width,), x.dtype)
    out[..., :x.shape[-1]] = x
    return out


def _down_slabs(w):
    n = w.shape[0] // 256
    return w.reshape(n, 2, P, D).transpose(0, 2, 1, 3).reshape(n, P, 2 * D)


def _first_weights(w_in, w_a, w_b, w_c, w_o, w_up, w_down):
    o = W_OFF
    r = lambda name, n, at=0: list(range(o[name] + at, o[name] + at + n))
    qk = (r("ik", 64) * 2 + r("aq", 384) + r("ak", 64) * 2 + r("iq", 512) + r("bq", 768) + r("bk", 768) + r("cq", 512)
          + r("ck", 64) * 2 + r("ck", 64, 64) * 2)
    assert len(qk) == N_QK * P
    qk += [0] * P
    v = r("bv", 768) + r("av", 64) + r("cv", 128) + r("iw", 8)
    v += [0] * (1024 - len(v))
    out = [_padded(_slabs(w_in, qk)), _padded(_slabs(w_in, v))]
    for n in range(DC):
        cut = lambda w, c0: w[:, c0 + n * P:c0 + (n + 1) * P].reshape(-1, P, P).transpose(1, 0, 2).reshape(P, -1)
        g = [cut(w_in, o["gates"] + j * D) for j in range(3)]
        out.append(_padded(np.concatenate(g[:2], axis=1))[None])
        out.append(np.concatenate([g[2], cut(w_a, 0), cut(w_b, 0), cut(w_c, 0)], axis=1)[None])
    out.append(_padded(_slabs(w_o, list(range(D)))))
    out.append(_padded(_slabs(w_up, list(range(4 * D)))))
    out.append(_padded(_down_slabs(w_down)))
    return np.concatenate(out)


def _columns(v):
    return v.reshape(-1, P).T


def _first_constants():
    c = np.zeros((P, N_C1), np.float32)
    p = np.arange(P)
    c[:, C1_INV] = np.power(np.float32(10000.0), -(p % 32).astype(np.float32) / np.float32(32)).astype(np.float32)
    c[:, C1_SIGN] = np.where(p % 64 < 32, -1.0, 1.0)
    c[:, C1_ID:C1_ID + P] = np.eye(P)
    c[:, C1_ONE:C1_ONE + P] = 1.0
    c[:, C1_BLK:C1_BLK + P] = p[:, None] // 64 == p[None] // 64
    off = lambda on: np.where(on, 0.0, NEG)
    t, s = p[:, None], p[None]
    c[:, C1_CAUSAL:C1_CAUSAL + P] = off(s <= t)
    s2 = np.arange(2 * P)[None] - P
    c[:, C1_WIN:C1_WIN + 2 * P] = off((s2 <= t) & (s2 > t - 128))
    for r in range(4):
        back = 4 * t + r - np.arange(L)[None]
        c[:, C1_DIL + r * L:C1_DIL + (r + 1) * L] = off((back >= 0) & (back <= 128))
    c[:, C1_DIL16:C1_DIL16 + P] = off(s <= t)
    c[:, C1_DIL16 + P:C1_DIL16 + 2 * P] = off((s <= t) & ((t - s) % 4 == 0))
    return c


def _second_weights(w_in, w_uq, w_ukv, w2, a2, g2, w_o, w_up, w_down):
    sb, mla, rw = 0, 3 * SB_HEADS * HD, 3 * SB_HEADS * HD + Q_LORA + P + RD
    r = lambda at, n: list(range(at, at + n))
    wz = np.concatenate([w_in, np.zeros((D, 1), w_in.dtype)], axis=1)
    z = [w_in.shape[1]]
    kr = mla + Q_LORA + P
    cols = (r(sb, 512) + r(mla, Q_LORA) + r(kr, RD) + z * 32 + r(mla + Q_LORA, P)
            + z * 64 + r(kr + RD // 2, RD // 2) + r(kr, RD // 2) + z * 32 + r(rw, 14 * P))
    assert len(cols) == N_T2 * P
    out = [_padded(_slabs(wz, cols)), _padded(_slabs(wz, r(sb + 512, 256)))]
    swapped = [QW * hd + c for hd in range(MLA_HEADS) for c in r(0, NOPE) + r(NOPE + RD // 2, RD // 2) + r(NOPE, RD // 2)]
    uq = np.concatenate([w_uq, w_uq[:, swapped]], axis=1)
    uq = np.concatenate([uq, np.zeros((2 * P - Q_LORA, uq.shape[1]), uq.dtype)])
    uq = uq.reshape(2, P, -1).transpose(1, 0, 2).reshape(P, -1)
    keys = [2 * HD * hd + c for hd in range(MLA_HEADS) for c in range(HD)]
    ukv = w_ukv[:, keys + [c + HD for c in keys]]
    out.append(_padded(np.concatenate([uq, ukv], axis=1))[None])
    out.append(_padded(np.concatenate([np.concatenate([w2, a2]), g2], axis=1))[None])
    out.append(_padded(_slabs(w_o, r(0, D))))
    ff = FF2 * P
    out.append(_padded(_slabs(w_up, [c for n in range(FF2) for c in r(n * P, P) + r(ff + n * P, P)])))
    out.append(_padded(_down_slabs(w_down)))
    return np.concatenate(out)


def _second_constants():
    c = np.zeros((P, N_C2), np.float32)
    c[:, 2:C2_CAUSAL] = _first_constants()[:, 2:C2_CAUSAL]
    a, b = np.arange(P)[:, None], np.arange(P)[None]
    c[:HD, 0] = 1.0
    c[HD:, 1] = 1.0
    c[:, C2_CAUSAL + 3 * P:C2_CAUSAL + 4 * P] = np.where(b <= a, 0.0, NEG)
    c[:, C2_SBKEEP:C2_SBKEEP + P] = a < b
    c[:, C2_SBNEG:C2_SBNEG + P] = np.where(a < b, 0.0, NEG)
    c[:, C2_TRI:C2_TRI + P] = a >= b
    same = a // CH == b // CH
    for i, on in enumerate((a < b, a <= b) * 2):
        c[:, C2_RW + i * P:C2_RW + (i + 1) * P] = on & same
    near = a // 8 == b // 8
    c[:, C2_ND:C2_ND + P] = (b < a) & near
    c[:, C2_NO:C2_NO + P] = (b < a) & same & ~near
    c[:, C2_NDT:C2_NDT + 4 * P] = np.tile((a < b) & near, (1, 4))
    c[:, C2_I4:C2_I4 + 4 * P] = np.tile(np.eye(P), (1, 4))
    c[:, C2_RESET:C2_RESET + L] = np.arange(L) % CH != 0
    freq = (np.float32(1) / np.power(np.float32(10000), np.arange(0, RD, 2, dtype=np.float32) / np.float32(RD))).astype(np.float32)
    ang = (np.arange(L, dtype=np.float32)[None] * freq[:, None]).astype(np.float32).astype(np.float64)
    c[64:96, C2_COS:C2_COS + L] = np.tile(np.cos(ang), (2, 1))
    c[64:96, C2_SIN:C2_SIN + L] = np.concatenate([-np.sin(ang), np.sin(ang)])
    return c


def layout(x):
    f = lambda n: np.ascontiguousarray(np.asarray(x[n]))
    a = {}
    a["x"] = f("x")[0].T.reshape(DC, P, L)
    a["pos"] = np.broadcast_to(f("positions").astype(np.int32), (P, L))
    a["cst1"] = _first_constants()
    a["w1"] = np.stack([_first_weights(*(f(n)[l] for n in ("w_in", "w_a", "w_b", "w_c", "w_o", "w_up", "w_down")))
                        for l in range(DEPTH)])
    assert a["w1"].shape[1] == N_S1
    prm = np.zeros((DEPTH, P, N_P1), np.float32)
    for l in range(DEPTH):
        prm[l, :, P1_ATTN:P1_ATTN + 8] = _columns(f("attn_norm")[l])
        prm[l, :, P1_MLP:P1_MLP + 8] = _columns(f("mlp_norm")[l])
        prm[l, :, P1_IK] = np.tile(f("idx_k_norm")[l], 2)
        prm[l, :, P1_SINK:P1_SINK + 8] = f("sinks")[l][None]
        prm[l, :, P1_FINAL:P1_FINAL + 8] = _columns(f("final_norm"))
    a["prm1"] = prm
    a["cst2"] = _second_constants()
    names = ("w_in", "mla_w_uq", "mla_w_ukv", "rwkv_w2", "rwkv_a2", "rwkv_g2", "w_o", "ffn_w_up", "ffn_w_down")
    a["w2"] = np.stack([_second_weights(*(f(n + "_2")[l] for n in names)) for l in range(DEPTH)])
    assert a["w2"].shape[1] == N_S2
    prm = np.zeros((DEPTH, P, N_P2), np.float32)
    for l in range(DEPTH):
        for n, at in (("rwkv_mu", P2_MU), ("rwkv_w0", P2_W0), ("rwkv_a0", P2_A0), ("rwkv_k_k", P2_KK), ("rwkv_k_a", P2_KA),
                      ("rwkv_r_k", P2_RK), ("rwkv_gn_g", P2_GNG), ("rwkv_gn_b", P2_GNB), ("mla_kv_norm", P2_KVN),
                      ("ln1_g", P2_LN1G), ("ln1_b", P2_LN1B), ("ln2_g", P2_LN2G), ("ln2_b", P2_LN2B),
                      ("ffn_conv_w", P2_CW), ("ffn_conv_b", P2_CB)):
            v = _columns(f(n + "_2")[l].reshape(-1))
            prm[l, :, at:at + v.shape[1]] = v
        prm[l, :, P2_QN] = f("mla_q_norm_2")[l][0:P]
        prm[l, 0:Q_LORA - P, P2_QN + 1] = f("mla_q_norm_2")[l][P:]
    a["prm2"] = prm
    return {n: np.ascontiguousarray(v) for n, v in a.items()}


def kernel(**inputs):
    import concourse.bacc as bacc
    from concourse.bass_utils import run_bass_kernel_spmd

    nc = bacc.Bacc("TRN2", target_bir_lowering=False, num_devices=1)
    arrays, d = {}, {}
    for name, a in layout(inputs).items():
        arrays[f"in_{name}"] = a
        d[name] = nc.dram_tensor(f"in_{name}", a.shape, mybir.dt.from_np(a.dtype), kind="ExternalInput").ap()
    d["out"] = nc.dram_tensor("out", (DC, P, L), F32, kind="ExternalOutput").ap()
    build(nc, d)
    r = run_bass_kernel_spmd(nc, [arrays], core_ids=[0])
    out = r.results[0]["out"].reshape(D, L)
    return np.ascontiguousarray(out.T)[None]
```

```python
from contextlib import ExitStack

import numpy as np

import concourse.bass as bass
from concourse import mybir

F32 = mybir.dt.float32
F32R = mybir.dt.float32r
I32 = mybir.dt.int32
ALU = mybir.AluOpType
ACT = mybir.ActivationFunctionType
AX_X = mybir.AxisListType.X

P = 128
L = 512
D = 1024
DC = D // P
TB = L // P
DEPTH = 2
HD = 64
A_HEADS, IDX_HEADS, B_GROUP_HEADS, C_HEADS = 6, 8, 4, 8
TOPK = 128
FF1 = 4 * D // P
FF2 = 2816 // P
NEG = -1.0e30
TAKEN = -3.0e38
ALPHA = float((2 * DEPTH) ** 0.25)

T_IK, T_AQ, T_AK, T_IQ, T_BQ, T_BK, T_CQ, T_CK = 0, 1, 4, 5, 9, 15, 21, 25
N_QK = 27
W_OFF = dict(aq=0, ak=384, av=448, iq=512, ik=1024, iw=1088, bq=1096, bk=1864, bv=2632,
             cq=3400, ck=3912, cv=4040, gates=4168)

SLOT = 2176
ROOM = 53208
BASE = 16512
MERGE_B = 1024 + 9 * P
N_PROJ1, N_V1, N_MERGE, N_WO = 14, 4, 16, 4
N_UP1, N_DOWN1 = FF1 // 2, FF1 // 2
S1_V = N_PROJ1
S1_MERGE = S1_V + N_V1
S1_WO = S1_MERGE + N_MERGE
S1_UP = S1_WO + N_WO
S1_DOWN = S1_UP + N_UP1
N_S1 = S1_DOWN + N_DOWN1

P1_ATTN, P1_MLP, P1_IK, P1_SINK, P1_FINAL, P1_NSINK = 0, 8, 16, 17, 25, 40
N_P1 = 33
C1_INV, C1_SIGN, C1_ID, C1_ONE, C1_BLK, C1_CAUSAL, C1_WIN, C1_DIL = 0, 1, 2, 130, 258, 386, 514, 770
C1_DIL16 = C1_DIL + 4 * L
N_C1 = C1_DIL16 + 2 * P

SB_HEADS, MLA_HEADS = 4, 4
Q_LORA, NOPE, RD = 192, 64, 32
QW = NOPE + RD
PAIRS, CH = 4, 64
NCH = L // CH
T2_SBQ, T2_SBK, T2_CQ, T2_CKV, T2_KRS, T2_RW = 0, 2, 4, 6, 7, 8
N_T2 = 22
N_PROJ2 = N_T2 // 2
S2_V = N_PROJ2
S2_MLA = S2_V + 1
S2_LORA = S2_MLA + 1
S2_WO = S2_LORA + 1
S2_UP = S2_WO + 4
S2_DOWN = S2_UP + FF2
N_S2 = S2_DOWN + FF2 // 2
(P2_MU, P2_W0, P2_A0, P2_KK, P2_KA, P2_RK, P2_GNG, P2_GNB, P2_QN, P2_KVN, P2_LN1G, P2_LN1B, P2_LN2G, P2_LN2B,
 P2_CW, P2_CB) = 0, 14, 18, 22, 26, 30, 34, 38, 42, 44, 45, 53, 61, 69, 77, 77 + 3 * FF2
N_P2 = P2_CB + FF2
P2_OMU = N_P2
(C2_CAUSAL, C2_SBKEEP, C2_SBNEG, C2_TRI, C2_RW, C2_ND, C2_NO, C2_NDT, C2_I4, C2_RESET, C2_COS, C2_SIN) = (
    514, 1026, 1154, 1282, 1410, 1922, 2050, 2178, 2690, 3202, 3714, 4226)
N_C2 = 4738


class Signal:

    def __init__(self, sem, base=0):
        self.sem, self.n, self.base = sem, 0, base

    def up(self, instruction, by=1):
        instruction.then_inc(self.sem, by)
        self.n += by
        return self.sem, self.base + self.n


class Banks:

    def __init__(self, start=0):
        self.fills, self.at, self.next = [start] * 8, {}, 0

    def plan(self, name):
        b = self.next
        self.next = (b + 1) % 8
        self.fills[b] += 1
        self.at[name] = (b, self.fills[b], 0)

    def plan_body(self, names, times):
        at = []
        before = list(self.fills)
        for name in names:
            b = self.next
            self.next = (b + 1) % 8
            self.fills[b] += 1
            at.append((name, b, self.fills[b]))
        for name, b, n in at:
            self.at[name] = (b, n, self.fills[b] - before[b])
        for b in range(8):
            self.fills[b] = before[b] + times * (self.fills[b] - before[b])


def build(nc, d, debug=False, stop=None):
    ctx = ExitStack()
    with ctx:
        sems = []

        def sem(name):
            s = ctx.enter_context(nc.semaphore(name))
            sems.append(s)
            return s

        def sb(name, shape, dt=F32):
            return ctx.enter_context(nc.sbuf_tensor(name, shape, dt))

        def place(name, at, *shape, dt=F32):
            n = int(np.prod(shape))
            assert at >= 0 and at + n <= ROOM
            return nc.alloc_sbuf_tensor_at(name, [P, *shape], dt, offset=BASE + 4 * at)

        h = place("h", 0, DC, L)
        cst = place("cst", 4096, 4800)
        prm = place("prm", 8896, 200)
        small = place("small", 9096, 64)
        ctx.enter_context(nc.sbuf_tensor("fence", [P, ROOM], F32))
        ps = ctx.enter_context(nc.psum_tensor("ps", [P, 8, L], F32))

        full = [sem(f"bank{b}_full") for b in range(8)]
        read = [sem(f"bank{b}_read") for b in range(8)]
        landed = [sem(f"raw{s}_landed") for s in range(4)]
        loaded = sem("loaded")
        stored = sem("stored")
        act_own = sem("act_own")
        dve_own = sem("dve_own")
        pool_own = sem("pool_own")
        S = {n: sem(n) for n in (
            "rope_arg", "rope_sin", "squared", "root", "normed", "swapped", "roped", "ik_squared", "ik_normed",
            "relued", "iscored", "mask_ready", "row_min", "exped", "den_ready", "scaled", "sink_exped", "pt_kept", "o_kept",
            "gate_kept", "gated", "merged_ready", "h_ready", "hidden_kept", "slab_used",
            "mixed", "w_hi", "w_lo", "sq_used", "u_hi", "u_lo", "m_hi", "m_lo", "down_read", "relu_kept", "hid_sq", "prm_ready", "roots2", "mla_normed", "mla_squared", "kr_ready", "q_ready", "k_ready",
            "sb_abs", "sb_soft", "sb_masked", "sb_arg", "sb_weight", "centered", "shifted", "act_act", "gelu", "lora_in",
            "wa_ready", "kk_sq", "kk_root", "decayed", "chunk_in", "expanded", "first_masked", "sq_plus", "nd_ready",
            "solved", "rv", "ln_out", "zeroed", "state_ready")}

        def close_block():
            nums = [s.num for s in sems]
            assert nums == list(range(nums[0], nums[0] + len(nums)))
            nc.gpsimd.sem_clear(range(nums[0], nums[-1] + 1))
            nc.all_engine_barrier()

        ident = cst[:, C1_ID:C1_ID + P]
        ones = cst[:, C1_ONE:C1_ONE + P]
        blk = cst[:, C1_BLK:C1_BLK + P]
        causal = cst[:, C1_CAUSAL:C1_CAUSAL + P]

        u_hi, u_lo = place("u_hi", 9160, DC, L, dt=F32R), place("u_lo", 13256, DC, L, dt=F32R)
        qk = place("qk", 34488, N_QK, L)
        av, bv = place("av", 48312, TB, HD), place("bv", 48568, TB, 12 * HD)
        cv, iw = place("cv", 51640, TB, 2 * HD), place("iw", 52152, TB, IDX_HEADS)
        cos, sin = place("cos", 52184, L)[:, :], place("sin", 52696, L)[:, :]
        four = place("four", 17352, 4, L)
        swp, ikn, iksq = four[:, 0:2, :], four[:, 2, :], four[:, 3, :]
        rstd = place("rstd", 19400, L)[:, :]
        o_hi, o_lo = place("o_hi", 17352, 9, L, dt=F32R), place("o_lo", 21960, 9, L, dt=F32R)
        sc = place("sc", 26568, 4, 768)
        pt = place("pt", 29640, 2, 768)
        score = place("score", 31176, 3, L)
        rel = place("rel", 32712, 2, L)

        def weight_room(tag, at, raws, width=2048):
            raw = place(f"raw_{tag}", at, raws, width)
            hi = place(f"w_hi_{tag}", at + raws * width, 2, width, dt=F32R)
            lo = place(f"w_lo_{tag}", at + (raws + 2) * width, 2, width, dt=F32R)
            return raw, hi, lo

        with nc.Block() as block:
            @block.sync
            def _(sy):
                for c in range(DC):
                    sy.dma_start(h[:, c, :], d["x"][c]).then_inc(loaded, 16)
                sy.dma_start(cst[:, 0:N_C1], d["cst1"]).then_inc(loaded, 16)
                sy.dma_start(swp[:, 0, :].bitcast(I32), d["pos"]).then_inc(loaded, 16)

            @block.vector
            def _(dve):
                own = Signal(dve_own)
                dve.wait_ge(loaded, 16 * (DC + 2))
                inv2pi, magic = float(np.float32(1 / (2 * np.pi))), 12582912.0
                c1 = 6.28125
                c2 = float(np.float32(2 * np.pi - c1))
                c3 = float(np.float32(2 * np.pi - c1 - c2))
                t = own.up(nc.vector.tensor_copy(swp[:, 1, :], swp[:, 0, :].bitcast(I32)))
                dve.wait_ge(*t)
                t = own.up(nc.vector.tensor_scalar(ikn, swp[:, 1, :], cst[:, C1_INV:C1_INV + 1], None, ALU.mult))
                dve.wait_ge(*t)
                for dst, quarter in ((sin, 0.0), (cos, 0.25)):
                    t = own.up(nc.vector.tensor_scalar(iksq, ikn, inv2pi, quarter, ALU.mult, ALU.add))
                    dve.wait_ge(*t)
                    t = own.up(nc.vector.tensor_scalar(iksq, iksq, magic, None, ALU.add))
                    dve.wait_ge(*t)
                    t = own.up(nc.vector.tensor_scalar(iksq, iksq, magic, None, ALU.subtract))
                    dve.wait_ge(*t)
                    t = own.up(nc.vector.scalar_tensor_tensor(dst, iksq, -c1, ikn, ALU.mult, ALU.add))
                    dve.wait_ge(*t)
                    t = own.up(nc.vector.scalar_tensor_tensor(dst, iksq, -c2, dst, ALU.mult, ALU.add))
                    dve.wait_ge(*t)
                    t = own.up(nc.vector.scalar_tensor_tensor(dst, iksq, -c3, dst, ALU.mult, ALU.add))
                    dve.wait_ge(*t)
                    t = own.up(nc.vector.tensor_scalar(dst, dst, float(np.float32(quarter * 2 * np.pi)), 3.1415925,
                                                       ALU.add, ALU.min))
                    dve.wait_ge(*t)
                    nc.vector.tensor_scalar(dst, dst, -3.1415925, None, ALU.max).then_inc(S["rope_arg"], 1)
                dve.wait_ge(S["rope_sin"], 2)
                nc.vector.tensor_scalar(sin, sin, cst[:, C1_SIGN:C1_SIGN + 1], None, ALU.mult).then_inc(dve_own, 1)

            @block.scalar
            def _(act):
                for n, dst in enumerate((sin, cos)):
                    act.wait_ge(S["rope_arg"], n + 1)
                    nc.scalar.activation(dst, dst, ACT.Sin).then_inc(S["rope_sin"], 1)
        close_block()

        def bank_to_fill(pe, jobs, name, it=None):
            b, n, per = jobs.at[name]
            if per:
                pe.wait_ge(read[b], it * per + (n - 1))
            elif n > 1:
                pe.wait_ge(read[b], n - 1)
            return b

        def bank_filled(eng, jobs, name, it=None):
            b, n, per = jobs.at[name]
            eng.wait_ge(full[b], it * per + n if per else n)
            return b

        def read_of(jobs, name, it=None):
            b, n, per = jobs.at[name]
            return read[b], (it * per + n if per else n)

        def norm_squares(act, wait_h, sq):
            for c in range(DC):
                if wait_h:
                    act.wait_ge(S["h_ready"], c + 1)
                if c >= 4:
                    act.wait_ge(S["sq_used"], c - 3)
                nc.scalar.activation(sq[:, c % 4, :], h[:, c, :], ACT.Square).then_inc(S["squared"], 1)

        def norm_sum(pe, jobs, name, sq):
            b = bank_to_fill(pe, jobs, name)
            for c in range(DC):
                pe.wait_ge(S["squared"], c + 1)
                m = nc.tensor.matmul(ps[:, b, :], ones, sq[:, c % 4, :], start=(c == 0), stop=(c == DC - 1))
                m.then_inc(full[b] if c == DC - 1 else S["sq_used"], 1)

        def norm_root(act, jobs, name, r):
            act.wait_ge(*read_of(jobs, name))
            nc.scalar.activation(r, r, ACT.Sqrt).then_inc(S["root"], 1)

        def norm_apply(dve, jobs, name, gain, own, roots, r, x, dst=None):
            b = bank_filled(dve, jobs, name)
            nc.vector.tensor_scalar(r, ps[:, b, :], 1.0 / D, 1e-6, ALU.mult, ALU.add).then_inc(read[b], 1)
            dve.wait_ge(S["root"], roots)
            dve.wait_ge(*own.up(nc.vector.reciprocal(r, r)))
            for c in range(DC):
                if c >= 4 and dst is None:
                    dve.wait_ge(S["u_lo"], c - 3)
                nc.vector.scalar_tensor_tensor(x[:, c % 4, :] if dst is None else dst[:, c, :], h[:, c, :],
                                               prm[:, gain + c:gain + c + 1], r, ALU.mult, ALU.mult)\
                  .then_inc(S["normed"], 1)

        def split_u_hi(act, x):
            for c in range(DC):
                act.wait_ge(S["normed"], c + 1)
                nc.scalar.activation(u_hi[:, c, :], x[:, c % 4, :], ACT.Copy).then_inc(S["u_hi"], 1)

        def split_u_lo(pool, x):
            for c in range(DC):
                pool.wait_ge(S["u_hi"], c + 1)
                nc.gpsimd.tensor_tensor(u_lo[:, c, :], x[:, c % 4, :], u_hi[:, c, :].bitcast(F32), ALU.subtract)\
                  .then_inc(S["u_lo"], 1)

        def split_w_hi(act, W, k, count, width=2048):
            raw, hi, lo = W
            nc.scalar.activation(hi[:, k % 2, 0:width], raw[:, k % raw.shape[1], 0:width], ACT.Copy).then_inc(S["w_hi"], 1)

        def split_w_lo(dve, W, k, count, width=2048):
            raw, hi, lo = W
            dve.wait_ge(S["w_hi"], count)
            nc.vector.tensor_tensor(lo[:, k % 2, 0:width], raw[:, k % raw.shape[1], 0:width],
                                    hi[:, k % 2, 0:width].bitcast(F32), ALU.subtract).then_inc(S["w_lo"], 1)

        def product3(out, w_hi, w_lo, x_hi, x_lo, start, stop):
            nc.tensor.matmul(out, w_hi, x_hi, start=start, stop=False)
            nc.tensor.matmul(out, w_hi, x_lo, start=False, stop=False)
            return nc.tensor.matmul(out, w_lo, x_hi, start=False, stop=stop)

        def dense_tile(pe, jobs, name, W, k, half, first_wait=None, it=None, x=None, first=0):
            b = bank_to_fill(pe, jobs, name, it)
            x_hi, x_lo = (u_hi, u_lo) if x is None else x
            w_hi, w_lo = (w[:, k % 2, 0:2048].rearrange("p (k c) -> p k c", c=256)[:, :, half * P:(half + 1) * P]
                          for w in W[1:])
            for c in range(DC):
                if first_wait is not None:
                    pe.wait_ge(first_wait, c + 1 + first)
                m = product3(ps[:, b, :], w_hi[:, c, :], w_lo[:, c, :], x_hi[:, c, :], x_lo[:, c, :],
                             c == 0, c == DC - 1)
            m.then_inc(full[b], 1)

        with nc.Fori(0, DEPTH) as layer:
            def w1_slab(k):
                return d["w1"][bass.ds(layer, 1), k].rearrange("a p c -> p (a c)")

            jobs = Banks()
            for name in ["sum", ("t", 0), ("t", 1), "ik_sum"] + [("t", t) for t in range(2, N_QK)]:
                jobs.plan(name)
            for s in range(N_V1):
                for tb in range(TB):
                    jobs.plan(("v", s, tb))

            WA = weight_room("a", 19912, 3)

            def last_of(k):
                return ("t", min(2 * k + 1, N_QK - 1)) if k < N_PROJ1 else ("v", k - S1_V, TB - 1)

            def split_a_hi(act, jobs, k):
                if k < S1_MERGE:
                    act.wait_ge(landed[k % 3], 16 * (k // 3 + 1))
                    if k >= 2:
                        b, n, _ = jobs.at[last_of(k - 2)]
                        act.wait_ge(full[b], n)
                    split_w_hi(act, WA, k, k + 1)

            def split_a_lo(dve, k):
                if k < S1_MERGE:
                    split_w_lo(dve, WA, k, k + 1)

            with nc.Block() as block:
                @block.sync
                def _(sy, jobs=jobs):
                    sy.dma_start(prm[:, 0:N_P1], d["prm1"][bass.ds(layer, 1)].rearrange("a p c -> p (a c)"))\
                      .then_inc(loaded, 16)
                    for k in range(S1_MERGE):
                        if k >= 3:
                            sy.wait_ge(S["w_lo"], k - 2)
                        sy.dma_start(WA[0][:, k % 3, :], w1_slab(k)[:, 0:2048]).then_inc(landed[k % 3], 16)

                @block.tensor
                def _(pe, jobs=jobs):
                    norm_sum(pe, jobs, "sum", four)

                    def tile(t):
                        if t % 2 == 0:
                            pe.wait_ge(S["w_lo"], t // 2 + 1)
                        dense_tile(pe, jobs, ("t", t), WA, t // 2, t % 2, S["u_lo"] if t == 0 else None)

                    tile(0)
                    tile(1)
                    b = bank_to_fill(pe, jobs, "ik_sum")
                    pe.wait_ge(S["ik_squared"], 1)
                    nc.tensor.matmul(ps[:, b, :], blk, iksq, start=True, stop=True).then_inc(full[b], 1)
                    for t in range(2, N_QK):
                        tile(t)
                    for s in range(N_V1):
                        k = S1_V + s
                        pe.wait_ge(S["w_lo"], k + 1)
                        w_hi, w_lo = (w[:, k % 2, :].rearrange("p (k c) -> p k c", c=256) for w in WA[1:])
                        for tb in range(TB):
                            b = bank_to_fill(pe, jobs, ("v", s, tb))
                            tok = slice(tb, L, TB) if s in (1, 2) else slice(tb * P, (tb + 1) * P)
                            for c in range(DC):
                                m = product3(ps[:, b, 0:256], u_hi[:, c, tok], u_lo[:, c, tok], w_hi[:, c, :], w_lo[:, c, :],
                                             c == 0, c == DC - 1)
                            m.then_inc(full[b], 1)

                @block.scalar
                def _(act, jobs=jobs):
                    norm_squares(act, False, four)
                    split_a_hi(act, jobs, 0)
                    split_a_hi(act, jobs, 1)
                    norm_root(act, jobs, "sum", rstd)
                    split_u_hi(act, four)

                    def swap(i, src):
                        if i < 2:
                            act.wait_ge(S["u_lo"], DC)
                        else:
                            act.wait_ge(S["roped"], i - 1)
                        for q in range(4):
                            o = q ^ 1
                            nc.scalar.activation(swp[32 * q:32 * q + 32, i % 2, :], src[32 * o:32 * o + 32, :],
                                                 ACT.Copy).then_inc(S["swapped"], 1)

                    act.wait_ge(*read_of(jobs, ("t", 0)))
                    nc.scalar.activation(iksq, ikn, ACT.Square).then_inc(S["ik_squared"], 1)
                    b = bank_filled(act, jobs, ("t", 1))
                    swap(0, ps[:, b, :])
                    split_a_hi(act, jobs, 2)
                    norm_root(act, jobs, "ik_sum", rstd)
                    act.wait_ge(S["ik_normed"], 1)
                    swap(1, ikn)
                    for t in range(2, N_QK):
                        b = bank_filled(act, jobs, ("t", t))
                        swap(t, ps[:, b, :])
                        if t % 2 == 1 or t == N_QK - 1:
                            split_a_hi(act, jobs, t // 2 + 2)
                    for s in range(N_V1):
                        for tb in range(TB):
                            b = bank_filled(act, jobs, ("v", s, tb))
                            if s < 3:
                                nc.scalar.activation(bv[:, tb, 256 * s:256 * s + 256], ps[:, b, 0:256], ACT.Copy)\
                                  .then_inc(read[b], 1)
                            else:
                                nc.scalar.activation(av[:, tb, :], ps[:, b, 0:HD], ACT.Copy)
                                nc.scalar.activation(cv[:, tb, :], ps[:, b, HD:3 * HD], ACT.Copy)
                                nc.scalar.activation(iw[:, tb, :], ps[:, b, 3 * HD:3 * HD + IDX_HEADS], ACT.Copy,
                                                     scale=IDX_HEADS ** -0.5).then_inc(read[b], 1)
                        split_a_hi(act, jobs, S1_V + s + 2)

                @block.gpsimd
                def _(pool):
                    split_u_lo(pool, four)

                @block.vector
                def _(dve, jobs=jobs):
                    own = Signal(dve_own)
                    split_a_lo(dve, 0)
                    split_a_lo(dve, 1)
                    dve.wait_ge(loaded, 16)
                    norm_apply(dve, jobs, "sum", P1_ATTN, own, 1, rstd, four)
                    b = bank_filled(dve, jobs, ("t", 0))
                    dve.wait_ge(S["u_lo"], DC)
                    nc.vector.tensor_copy(ikn, ps[:, b, :]).then_inc(read[b], 1)

                    def rope(i, t, src, done):
                        dve.wait_ge(S["swapped"], 4 * (i + 1))
                        nc.vector.tensor_tensor(qk[:, t, :], src, cos, ALU.mult).then_inc(*done[:2])
                        dve.wait_ge(*own.up(nc.vector.tensor_tensor(swp[:, i % 2, :], swp[:, i % 2, :], sin, ALU.mult)))
                        dve.wait_ge(done[0], done[2])
                        nc.vector.tensor_tensor(qk[:, t, :], qk[:, t, :], swp[:, i % 2, :], ALU.add)\
                          .then_inc(S["roped"], 1)

                    def rope_bank(i, t):
                        b = bank_filled(dve, jobs, ("t", t))
                        rope(i, t, ps[:, b, :], (read[b], 1, jobs.at["t", t][1]))

                    rope_bank(0, 1)
                    split_a_lo(dve, 2)
                    b = bank_filled(dve, jobs, "ik_sum")
                    nc.vector.tensor_scalar(rstd, ps[:, b, :], 1.0 / HD, 1e-6, ALU.mult, ALU.add).then_inc(read[b], 1)
                    dve.wait_ge(S["root"], 2)
                    dve.wait_ge(*own.up(nc.vector.reciprocal(rstd, rstd)))
                    nc.vector.scalar_tensor_tensor(ikn, ikn, prm[:, P1_IK:P1_IK + 1], rstd, ALU.mult, ALU.mult)\
                      .then_inc(S["ik_normed"], 1)
                    dve.wait_ge(S["ik_normed"], 1)
                    own.n += 1
                    rope(1, T_IK, ikn, (dve_own, 1, own.n))
                    for t in range(2, N_QK):
                        rope_bank(t, t)
                        if t % 2 == 1 or t == N_QK - 1:
                            split_a_lo(dve, t // 2 + 2)
                    for s in range(N_V1):
                        split_a_lo(dve, S1_V + s + 2)
            close_block()

            units = [("B", j, r) for r in range(TB) for j in range(B_GROUP_HEADS)]
            units += [("C", hd, b) for b in range(TB) for hd in range(C_HEADS)]
            units += [("A", hd, b) for b in range(TB) for hd in range(A_HEADS)]

            def unit_width(unit):
                br, hd, b = unit
                return 6 * P if br == "B" else min(b + 1, 2) * P if br == "C" else (b + 1) * P

            def steps():
                for k in range(len(units) + 4):
                    yield [k - lag if 0 <= k - lag < len(units) else None for lag in range(5)]

            jobs = Banks()
            for b in range(1, TB):
                for hd in range(IDX_HEADS):
                    jobs.plan(("index", b, hd))
            for s0, s1, s2, s3, s4 in steps():
                if s0 is not None:
                    jobs.plan(("logits", s0, 0))
                    if units[s0][0] == "B":
                        jobs.plan(("logits", s0, 1))
                if s2 is not None:
                    jobs.plan(("pt", s2, 0))
                    if units[s2][0] == "B":
                        jobs.plan(("pt", s2, 1))
                if s3 is not None:
                    jobs.plan(("o", s3))

            def o_place(unit):
                br, hd, b = unit
                return {"A": 0, "B": 3, "C": 5}[br] + hd // 2, (slice(b, L, TB) if br == "B" else slice(b * P, (b + 1) * P))

            def half(hd):
                return slice(HD * (hd % 2), HD * (hd % 2) + HD)

            with nc.Block() as block:
                @block.tensor
                def _(pe, jobs=jobs):
                    for b in range(1, TB):
                        for hd in range(IDX_HEADS):
                            bank = bank_to_fill(pe, jobs, ("index", b, hd))
                            nc.tensor.matmul(ps[:, bank, 0:(b + 1) * P], qk[half(hd), T_IQ + hd // 2, b * P:(b + 1) * P],
                                             qk[half(hd), T_IK, 0:(b + 1) * P], start=True, stop=True)\
                              .then_inc(full[bank], 1)

                    def logits(k):
                        br, hd, b = units[k]
                        w = unit_width(units[k])
                        bank = bank_to_fill(pe, jobs, ("logits", k, 0))
                        if br == "A":
                            nc.tensor.matmul(ps[:, bank, 0:w], qk[half(hd), T_AQ + hd // 2, b * P:(b + 1) * P],
                                             qk[half(hd), T_AK, 0:w], start=True, stop=True).then_inc(full[bank], 1)
                        elif br == "C":
                            nc.tensor.matmul(ps[:, bank, 0:w], qk[half(hd), T_CQ + hd // 2, b * P:(b + 1) * P],
                                             qk[half(hd), T_CK + hd // 4, (b + 1) * P - w:(b + 1) * P],
                                             start=True, stop=True).then_inc(full[bank], 1)
                        else:
                            rows = slice(b, L, TB)
                            q = [qk[half(hd), T_BQ + (g * 4 + hd) // 2, rows] for g in range(3)]
                            kk = [qk[half(hd), T_BK + (g * 4 + hd) // 2, :] for g in range(3)]
                            nc.tensor.matmul(ps[:, bank, :], q[0], kk[0], start=True, stop=True).then_inc(full[bank], 1)
                            bank = bank_to_fill(pe, jobs, ("logits", k, 1))
                            for g in (1, 2):
                                m = nc.tensor.matmul(ps[:, bank, (g - 1) * P:g * P], q[g], kk[g][:, rows],
                                                     start=(g == 1), stop=(g == 2), skip_group_check=True)
                            m.then_inc(full[bank], 1)

                    def turn(k):
                        n = unit_width(units[k]) // P
                        pe.wait_ge(S["scaled"], k + 1)
                        for part in range(2 if n > 4 else 1):
                            bank = bank_to_fill(pe, jobs, ("pt", k, part))
                            cs = range(4 * part, min(4 * part + 4, n))
                            for c in cs:
                                m = nc.tensor.transpose(ps[:, bank, (c % 4) * P:(c % 4 + 1) * P],
                                                        sc[:, k % 4, c * P:(c + 1) * P], ident)
                            m.then_inc(full[bank], 1)

                    def values(k):
                        br, hd, b = units[k]
                        n = unit_width(units[k]) // P
                        pe.wait_ge(*read_of(jobs, ("pt", k, 1 if n > 4 else 0)))
                        if n > 4:
                            pe.wait_ge(*read_of(jobs, ("pt", k, 0)))
                        bank = bank_to_fill(pe, jobs, ("o", k))
                        for c in range(n):
                            if br == "A":
                                v = av[:, c, :]
                            elif br == "C":
                                v = cv[:, b + 1 - n + c, hd // 4 * HD:(hd // 4 + 1) * HD]
                            elif c < 4:
                                v = bv[:, c, hd * HD:(hd + 1) * HD]
                            else:
                                v = bv[:, b, (4 * (c - 3) + hd) * HD:(4 * (c - 3) + hd + 1) * HD]
                            m = nc.tensor.matmul(ps[half(hd), bank, 0:P], v, pt[:, k % 2, c * P:(c + 1) * P],
                                                 start=(c == 0), stop=(c == n - 1))
                        m.then_inc(full[bank], 1)

                    for s0, s1, s2, s3, s4 in steps():
                        if s0 is not None:
                            logits(s0)
                        if s2 is not None:
                            turn(s2)
                        if s3 is not None:
                            values(s3)

                @block.scalar
                def _(act, jobs=jobs):
                    i = 0
                    for b in range(1, TB):
                        for hd in range(IDX_HEADS):
                            bank = bank_filled(act, jobs, ("index", b, hd))
                            if i >= 2:
                                act.wait_ge(S["iscored"], i - 1)
                            nc.scalar.activation(rel[:, i % 2, 0:(b + 1) * P], ps[:, bank, 0:(b + 1) * P], ACT.Relu,
                                                 scale=HD ** -0.5).then_inc(read[bank], 1)
                            i += 1
                    sinks = 0
                    for s0, s1, s2, s3, s4 in steps():
                        if s1 is not None:
                            k, w = s1, unit_width(units[s1])
                            if units[k][0] == "A":
                                act.wait_ge(*read_of(jobs, ("logits", k, 0)))
                            else:
                                act.wait_ge(S["row_min"], k + 1)
                            if units[k][0] == "C":
                                s = P1_SINK + units[k][1]
                                nc.scalar.activation(small[:, 16 + k % 4:17 + k % 4], small[:, k % 4:k % 4 + 1], ACT.Exp,
                                                     bias=prm[:, s:s + 1])
                            nc.scalar.activation(sc[:, k % 4, 0:w], sc[:, k % 4, 0:w], ACT.Exp,
                                                 bias=small[:, k % 4:k % 4 + 1], scale=-1.0,
                                                 accum_out=small[:, 4 + k % 4:5 + k % 4]).then_inc(S["exped"], 1)
                        if s2 is not None:
                            k, n = s2, unit_width(units[s2]) // P
                            for part in range(2 if n > 4 else 1):
                                bank = bank_filled(act, jobs, ("pt", k, part))
                                if k >= 2:
                                    b, m, _ = jobs.at["o", k - 2]
                                    act.wait_ge(full[b], m)
                                lo, hi = 512 * part, min(512 * part + 512, n * P)
                                nc.scalar.activation(pt[:, k % 2, lo:hi], ps[:, bank, 0:hi - lo], ACT.Copy)\
                                  .then_inc(read[bank], 1)
                        if s3 is not None:
                            bank = bank_filled(act, jobs, ("o", s3))
                            br, hd, b = units[s3]
                            tile, cols = o_place(units[s3])
                            nc.scalar.activation(o_hi[half(hd), tile, cols], ps[half(hd), bank, 0:P], ACT.Copy)\
                              .then_inc(S["o_kept"], 1)

                @block.gpsimd
                def _(pool, jobs=jobs):
                    for k, unit in enumerate(units):
                        w = unit_width(unit)
                        pool.wait_ge(S["den_ready"], k + 1)
                        nc.gpsimd.tensor_scalar(sc[:, k % 4, 0:w], sc[:, k % 4, 0:w], small[:, 8 + k % 4:9 + k % 4], None,
                                                ALU.mult).then_inc(S["scaled"], 1)

                @block.vector
                def _(dve, jobs=jobs):
                    own = Signal(dve_own)
                    dve.wait_ge(*own.up(nc.vector.tensor_scalar(prm[:, P1_NSINK:P1_NSINK + C_HEADS],
                                                                prm[:, P1_SINK:P1_SINK + C_HEADS], -1.0, None, ALU.mult)))
                    i = 0
                    for b in range(1, TB):
                        w = (b + 1) * P
                        for hd in range(IDX_HEADS):
                            dve.wait_ge(*read_of(jobs, ("index", b, hd)))
                            if hd == 0:
                                nc.vector.tensor_scalar(score[:, b - 1, 0:w], rel[:, i % 2, 0:w], iw[:, b, hd:hd + 1], None,
                                                        ALU.mult).then_inc(S["iscored"], 1)
                            else:
                                dve.wait_ge(S["iscored"], i)
                                nc.vector.scalar_tensor_tensor(score[:, b - 1, 0:w], rel[:, i % 2, 0:w],
                                                               iw[:, b, hd:hd + 1], score[:, b - 1, 0:w],
                                                               ALU.mult, ALU.add).then_inc(S["iscored"], 1)
                            i += 1
                        dve.wait_ge(S["iscored"], i)
                        m = own.up(nc.vector.tensor_tensor(score[:, b - 1, b * P:w], score[:, b - 1, b * P:w], causal, ALU.add))
                        if b == TB - 1:
                            dve.wait_ge(*m)

                    def topk():
                        for b in range(1, TB):
                            row = score[:, b - 1, 0:(b + 1) * P]
                            for _ in range(TOPK // 8):
                                m = own.up(nc.vector.max(out=small[:, 32:40], in_=row))
                                yield
                                dve.wait_ge(*m)
                                m = own.up(nc.vector.match_replace(out=row, in_to_replace=small[:, 32:40], in_values=row,
                                                                   imm_value=TAKEN))
                                yield
                                dve.wait_ge(*m)
                            m = own.up(nc.vector.tensor_scalar(row, row, TAKEN / 2, NEG, ALU.is_gt, ALU.mult))
                            dve.wait_ge(*m)
                            yield

                    picks = topk()
                    for s0, s1, s2, s3, s4 in steps():
                        if s0 is not None:
                            k = s0
                            br, hd, b = units[k]
                            w = unit_width(units[k])
                            if br == "A":
                                for _ in picks:
                                    pass
                            mn = small[:, k % 4:k % 4 + 1]
                            if k >= 4:
                                bk, m, _ = jobs.at["pt", k - 4, 1 if units[k - 4][0] == "B" else 0]
                                dve.wait_ge(full[bk], m)
                            bank = bank_filled(dve, jobs, ("logits", k, 0))
                            if br == "B":
                                mask, w0 = cst[:, C1_DIL + b * L:C1_DIL + (b + 1) * L], L
                            elif br == "C":
                                mask, w0 = cst[:, C1_WIN + 256 - w:C1_WIN + 256], w
                            else:
                                mask, w0 = (causal if b == 0 else score[:, b - 1, 0:w]), w
                            part = small[:, 20 + 2 * (k % 2):22 + 2 * (k % 2)]
                            first = mn if br == "A" else part[:, 0:1]
                            t = nc.vector.tensor_tensor_reduce(out=sc[:, k % 4, 0:w0], in0=ps[:, bank, 0:w0], in1=mask,
                                                               scale=-(HD ** -0.5), scalar=-NEG, op0=ALU.add, op1=ALU.min,
                                                               accum_out=first)
                            t.then_inc(read[bank], 1)
                            dve.wait_ge(*read_of(jobs, ("logits", k, 0)))
                            if br == "B":
                                bank = bank_filled(dve, jobs, ("logits", k, 1))
                                mask = cst[:, C1_DIL16:C1_DIL16 + 256]
                                nc.vector.tensor_tensor_reduce(out=sc[:, k % 4, L:L + 256], in0=ps[:, bank, 0:256],
                                                               in1=mask, scale=-(HD ** -0.5), scalar=-NEG, op0=ALU.add,
                                                               op1=ALU.min, accum_out=part[:, 1:2]).then_inc(read[bank], 1)
                                dve.wait_ge(*read_of(jobs, ("logits", k, 1)))
                                nc.vector.tensor_tensor(mn, part[:, 0:1], part[:, 1:2], ALU.min).then_inc(S["row_min"], 1)
                            elif br == "C":
                                nc.vector.tensor_tensor(mn, part[:, 0:1], prm[:, P1_NSINK + hd:P1_NSINK + hd + 1], ALU.min)\
                                  .then_inc(S["row_min"], 1)
                        if s1 is not None:
                            k = s1
                            den = small[:, 4 + k % 4:5 + k % 4]
                            dve.wait_ge(S["exped"], k + 1)
                            if units[k][0] == "C":
                                dve.wait_ge(*own.up(nc.vector.tensor_tensor(den, den, small[:, 16 + k % 4:17 + k % 4], ALU.add)))
                            nc.vector.reciprocal(small[:, 8 + k % 4:9 + k % 4], den).then_inc(S["den_ready"], 1)
                        if s3 is not None:
                            k = s3
                            br, hd, b = units[k]
                            bank = bank_filled(dve, jobs, ("o", k))
                            tile, cols = o_place(units[k])
                            dve.wait_ge(S["o_kept"], k + 1)
                            nc.vector.tensor_tensor(o_lo[half(hd), tile, cols], ps[half(hd), bank, 0:P],
                                                    o_hi[half(hd), tile, cols].bitcast(F32), ALU.subtract).then_inc(read[bank], 1)
                        next(picks, None)
                        next(picks, None)
            close_block()

            m_hi, m_lo = place("m_hi", 26568, DC, L, dt=F32R), place("m_lo", 30664, DC, L, dt=F32R)
            gate, gtmp = place("gate", 34760, 3, L), place("gtmp", 36296, 3, L)
            gsq = place("gsq", 34760, 4, L)
            grs = place("grs", 37832, L)[:, :]
            WC = weight_room("c", 38344, 2, SLOT)
            BR = {0: (0, 3), 1: (3, 2), 2: (5, 4)}
            jobs = Banks(start=1)
            jobs.plan_body([(w, q, j) for q in range(2) for w in ("gate", "branch") for j in range(3)], DC // 2)
            for n in range(DC):
                jobs.plan(("wo", n))
            jobs.plan("sum")
            N_C = N_MERGE + N_WO

            def merge_last(j):
                return ("gate", j // 2, 1) if j % 2 == 0 else ("branch", j // 2, 2)

            with nc.Block() as block:
                @block.sync
                def _(sy, jobs=jobs):
                    def fetch(k, j):
                        sy.dma_start(WC[0][:, j, :], d["w1"][bass.ds(layer, 1), bass.ds(k, 1)].rearrange("a b p c -> p (a b c)"))\
                          .then_inc(landed[j], 16)

                    fetch(S1_MERGE, 0)
                    fetch(S1_MERGE + 1, 1)
                    with sy.Fori(1, N_C // 2) as it:
                        for j in range(2):
                            sy.wait_ge(S["w_lo"], it * 2 + (j - 1))
                            fetch(it * 2 + (S1_MERGE + j), j)

                @block.tensor
                def _(pe, jobs=jobs):
                    for b in range(8):
                        pe.sem_inc(full[b], 1)
                        pe.sem_inc(read[b], 1)
                    with pe.Fori(0, DC // 2) as it:
                        for q in range(2):
                            for j in range(3):
                                if j != 1:
                                    pe.wait_ge(S["w_lo"], it * 4 + (2 * q + (j == 2) + 1))
                                w_hi, w_lo = (w[:, int(j == 2), (j % 2) * 1024:(j % 2) * 1024 + 1024]
                                              .rearrange("p (k c) -> p k c", c=P) for w in WC[1:])
                                b = bank_to_fill(pe, jobs, ("gate", q, j), it)
                                for c in range(DC):
                                    m = product3(ps[:, b, :], w_hi[:, c, :], w_lo[:, c, :], u_hi[:, c, :], u_lo[:, c, :],
                                                 c == 0, c == DC - 1)
                                m.then_inc(full[b], 1)
                            w_hi, w_lo = (w[:, 1, 1024:MERGE_B].rearrange("p (k c) -> p k c", c=P) for w in WC[1:])
                            for j in range(3):
                                t0, n = BR[j]
                                b = bank_to_fill(pe, jobs, ("branch", q, j), it)
                                for c in range(n):
                                    m = product3(ps[:, b, :], w_hi[:, t0 + c, :], w_lo[:, t0 + c, :], o_hi[:, t0 + c, :],
                                                 o_lo[:, t0 + c, :], c == 0, c == n - 1)
                                m.then_inc(full[b], 1)
                    for n in range(DC):
                        if n % 2 == 0:
                            pe.wait_ge(S["w_lo"], N_MERGE + n // 2 + 1)
                        dense_tile(pe, jobs, ("wo", n), WC, n // 2, n % 2, S["m_lo"] if n == 0 else None, x=(m_hi, m_lo), first=1)
                    norm_sum(pe, jobs, "sum", gsq)

                @block.scalar
                def _(act, jobs=jobs):
                    for k in range(2):
                        act.wait_ge(landed[k], 16)
                        split_w_hi(act, WC, k, k + 1, SLOT)
                    with act.Fori(0, DC // 2) as it:
                        for q in range(2):
                            act.wait_ge(S["gated"], it * 2 + (q + 1))
                            for j in range(3):
                                b = bank_filled(act, jobs, ("gate", q, j), it)
                                nc.scalar.activation(gate[:, j, :], ps[:, b, :], ACT.Sigmoid).then_inc(read[b], 1)
                                if j == 1:
                                    act.wait_ge(landed[0], it * 32 + 16 * (q + 2))
                                    split_w_hi(act, WC, 0, None, SLOT)
                            act.wait_ge(S["gated"], it * 2 + (q + 2))
                            nc.scalar.activation(m_hi[:, bass.ds(it * 2 + q, 1), :].rearrange("p a c -> p (a c)"), gtmp[:, 0, :],
                                                 ACT.Copy).then_inc(S["m_hi"], 1)
                            act.wait_ge(landed[1], it * 32 + 16 * (q + 2))
                            split_w_hi(act, WC, 1, None, SLOT)
                    for k in range(2, N_WO):
                        act.wait_ge(landed[k % 2], 16 * ((N_MERGE + k) // 2 + 1))
                        b, n, _ = jobs.at["wo", 2 * (k - 2) + 1]
                        act.wait_ge(full[b], n)
                        split_w_hi(act, WC, k, None, SLOT)
                    norm_squares(act, True, gsq)
                    norm_root(act, jobs, "sum", grs)
                    split_u_hi(act, gsq)

                @block.gpsimd
                def _(pool):
                    split_u_lo(pool, gsq)

                @block.vector
                def _(dve, jobs=jobs):
                    dve.sem_inc(S["gated"], 1)
                    dve.sem_inc(S["m_lo"], 1)
                    for k in range(2):
                        split_w_lo(dve, WC, k, k + 1, SLOT)
                    with dve.Fori(0, DC // 2) as it:
                        for q in range(2):
                            for j in range(3):
                                if j == 1:
                                    b, n, per = jobs.at["gate", q, 1]
                                    split_w_lo(dve, WC, 0, it * 4 + (2 * q + 3), SLOT)
                                dve.wait_ge(*read_of(jobs, ("gate", q, j), it))
                                b = bank_filled(dve, jobs, ("branch", q, j), it)
                                if j == 0:
                                    dve.wait_ge(S["m_lo"], it * 2 + (q + 1))
                                nc.vector.tensor_tensor(gtmp[:, j, :], ps[:, b, :], gate[:, j, :], ALU.mult).then_inc(read[b], 1)
                            for j in range(2):
                                dve.wait_ge(*read_of(jobs, ("branch", q, j), it))
                            nc.vector.tensor_tensor(gtmp[:, 0, :], gtmp[:, 0, :], gtmp[:, 1, :], ALU.add).then_inc(dve_own, 1)
                            dve.wait_ge(*read_of(jobs, ("branch", q, 2), it))
                            dve.wait_ge(dve_own, it * 2 + (q + 1))
                            nc.vector.tensor_tensor(gtmp[:, 0, :], gtmp[:, 0, :], gtmp[:, 2, :], ALU.add).then_inc(S["gated"], 1)
                            n = it * 2 + (q + 1)
                            dve.wait_ge(S["m_hi"], n)
                            t = bass.ds(it * 2 + q, 1)
                            nc.vector.tensor_tensor(m_lo[:, t, :].rearrange("p a c -> p (a c)"), gtmp[:, 0, :],
                                                    m_hi[:, t, :].rearrange("p a c -> p (a c)").bitcast(F32), ALU.subtract)\
                              .then_inc(S["m_lo"], 1)
                            split_w_lo(dve, WC, 1, it * 4 + (2 * q + 4), SLOT)
                    own = Signal(dve_own)
                    own.n = DC
                    for n in range(DC):
                        b = bank_filled(dve, jobs, ("wo", n))
                        nc.vector.tensor_tensor(h[:, n, :], h[:, n, :], ps[:, b, :], ALU.add).then_inc(read[b], 1)
                        dve.wait_ge(*read_of(jobs, ("wo", n)))
                        dve.sem_inc(S["h_ready"], 1)
                        if n in (1, 3):
                            split_w_lo(dve, WC, n // 2, N_MERGE + n // 2 + 3, SLOT)
                    norm_apply(dve, jobs, "sum", P1_MLP, own, 1, grs, gsq)
            close_block()

            HF = FF1 // 2
            hid_hi, hid_lo = place("hid_hi", 17352, HF, L, dt=F32R), place("hid_lo", 25544, HF, L, dt=F32R)
            hid = place("hid", 33736, 2, L)
            WF = weight_room("f", 34760, 4)
            NS = HF
            jobs = Banks(start=1)
            before = list(jobs.fills)
            jobs.plan_body([("up", t) for t in range(HF)] + [("down", n) for n in range(DC)], 2)
            per_half = [(jobs.fills[b] - before[b]) // 2 for b in range(8)]

            with nc.Block() as block:
                @block.sync
                def _(sy, jobs=jobs):
                    def fetch(k, j):
                        sy.dma_start(WF[0][:, j, :], d["w1"][bass.ds(layer, 1), bass.ds(k, 1), :, 0:2048]
                                     .rearrange("a b p c -> p (a b c)")).then_inc(landed[j], 16)

                    for j in range(4):
                        fetch(S1_UP + j, j)
                    with sy.Fori(1, 2 * NS // 4) as it:
                        for j in range(4):
                            sy.wait_ge(S["w_lo"], it * 4 + (j - 3))
                            fetch(it * 4 + (S1_UP + j), j)

                @block.tensor
                def _(pe, jobs=jobs):
                    for b in range(8):
                        pe.sem_inc(full[b], 1)
                        pe.sem_inc(read[b], 1)
                    with pe.Fori(0, 2) as hf:
                        for t in range(HF):
                            if t % 2 == 0:
                                pe.wait_ge(S["w_lo"], hf * NS + (t // 2 + 1))
                            dense_tile(pe, jobs, ("up", t), WF, t // 2, t % 2, it=hf)
                        for k in range(HF // 2):
                            pe.wait_ge(S["w_lo"], hf * NS + (HF // 2 + k + 1))
                            w_hi, w_lo = (w[:, k % 2, :].rearrange("p (k c) -> p k c", c=D) for w in WF[1:])
                            for c in range(2):
                                t = 2 * k + c
                                pe.wait_ge(S["hidden_kept"], hf * HF + (t + 1))
                                for n in range(DC):
                                    b = jobs.at["down", n][0]
                                    if t == 0:
                                        bank_to_fill(pe, jobs, ("down", n), hf)
                                    f = slice(n * P, (n + 1) * P)
                                    m = product3(ps[:, b, :], w_hi[:, c, f], w_lo[:, c, f], hid_hi[:, t, :], hid_lo[:, t, :],
                                                 t == 0, t == HF - 1)
                                    if t == HF - 1:
                                        m.then_inc(full[b], 1)
                            if k < HF // 2 - 1:
                                m.then_inc(S["slab_used"], 1)

                def slab_done(eng, jobs, k, hf):
                    if k < 0:
                        for b in range(8):
                            eng.wait_ge(full[b], hf * per_half[b] + before[b])
                    elif k < HF // 2:
                        b, n, per = jobs.at["up", 2 * k + 1]
                        eng.wait_ge(full[b], hf * per + n)
                    else:
                        eng.wait_ge(S["slab_used"], hf * (HF // 2 - 1) + (k - HF // 2 + 1))

                @block.scalar
                def _(act, jobs=jobs):
                    with act.Fori(0, 2) as hf:
                        def split(k):
                            if k < NS:
                                act.wait_ge(landed[k % 4], hf * (4 * NS) + 16 * (k // 4 + 1))
                                slab_done(act, jobs, k - 2, hf)
                                split_w_hi(act, WF, k, None)

                        split(0)
                        split(1)
                        for t in range(HF):
                            b = bank_filled(act, jobs, ("up", t), hf)
                            act.wait_ge(S["hid_sq"], hf * HF + (t + 1))
                            nc.scalar.activation(hid[:, t % 2, :], ps[:, b, :], ACT.Relu).then_inc(read[b], 1)
                            act.wait_ge(S["relu_kept"], hf * HF + (t + 1))
                            nc.scalar.activation(hid_hi[:, t, :], hid[:, t % 2, :], ACT.Copy).then_inc(S["m_hi"], 1)
                            if t % 2 == 1:
                                split(t // 2 + 2)
                        for k in range(HF // 2 + 2, NS):
                            split(k)

                @block.gpsimd
                def _(pool):
                    pool.sem_inc(S["hid_sq"], 2)
                    with pool.Fori(0, 2) as hf:
                        for t in range(HF):
                            pool.wait_ge(S["m_hi"], hf * HF + (t + 1))
                            nc.gpsimd.tensor_tensor(hid_lo[:, t, :], hid[:, t % 2, :], hid_hi[:, t, :].bitcast(F32),
                                                    ALU.subtract).then_inc(S["hidden_kept"], 1)
                            pool.wait_ge(S["hidden_kept"], hf * HF + (t + 1))
                            pool.sem_inc(S["hid_sq"], 1)

                @block.vector
                def _(dve, jobs=jobs):
                    with dve.Fori(0, 2) as hf:
                        def split(k):
                            if k < NS:
                                split_w_lo(dve, WF, k, hf * NS + (k + 1))

                        split(0)
                        split(1)
                        for t in range(HF):
                            dve.wait_ge(*read_of(jobs, ("up", t), hf))
                            x = hid[:, t % 2, :]
                            nc.vector.tensor_tensor(x, x, x, ALU.mult).then_inc(S["relu_kept"], 1)
                            if t % 2 == 1:
                                split(t // 2 + 2)
                        for k in range(HF // 2 + 2, NS):
                            split(k)
                        for n in range(DC):
                            b = bank_filled(dve, jobs, ("down", n), hf)
                            nc.vector.tensor_tensor(h[:, n, :], h[:, n, :], ps[:, b, :], ALU.add).then_inc(read[b], 1)
            close_block()

        jobs = Banks()
        jobs.plan("sum")
        with nc.Block() as block:
            @block.tensor
            def _(pe):
                norm_sum(pe, jobs, "sum", four)

            @block.scalar
            def _(act):
                norm_squares(act, False, four)
                norm_root(act, jobs, "sum", rstd)

            @block.vector
            def _(dve):
                norm_apply(dve, jobs, "sum", P1_FINAL, Signal(dve_own), 1, rstd, None, dst=h)
        close_block()

        IN2 = ROOM - 12288
        sbqk, sbv = place("sbqk", IN2, 4, L), place("sbv", IN2 + 2048, TB, SB_HEADS * HD)
        cq = place("cq", IN2 + 3072, 2, L)
        ckv = place("ckv", IN2 + 4096, L)[:, :]
        krs = place("krs", IN2 + 4608, L)[:, :]
        rw_in = place("rw_in", IN2 + 5120, 14, L)
        rr, rk, rv = (rw_in[:, PAIRS * i:PAIRS * (i + 1), :] for i in range(3))
        wdad, gd = rw_in[:, 12, :], rw_in[:, 13, :]
        mla_w = place("mla_w", IN2 - 2048, 2048)
        o2_hi, o2_lo = u_hi, u_lo
        WP = weight_room("p", 17352, 3)
        mq, mk = place("mq", 17352, MLA_HEADS, L), place("mk", 19400, MLA_HEADS, L)
        mv = place("mv", 21448, TB, MLA_HEADS * HD)
        sc2 = place("sc2", 22472, 4, L)
        pt2 = place("pt2", 24520, 2, L)
        msq = place("msq", 25544, 3, L)
        mrs = place("mrs", 27080, 2, L)
        ZO = [0, 512, 896, 1152, 1280]
        zs = [place(f"zs{i}", 28104 + 1280 * i, 1280)[:, :] for i in range(2)]
        sp = [place(f"sp{i}", 30664 + 1280 * i, 1280)[:, :] for i in range(2)]

        with nc.Block() as block:
            @block.sync
            def _(sy):
                sy.dma_start(cst[:, 0:N_C2], d["cst2"]).then_inc(loaded, 16)
                sy.wait_ge(loaded, 16)
        close_block()

        def prm_col(c):
            return prm[:, c:c + 1]

        with nc.Fori(0, DEPTH) as layer:
            jobs = Banks()
            for t in range(N_T2):
                jobs.plan(("t", t))
            for tb in range(TB):
                jobs.plan(("v", tb))

            with nc.Block() as block:
                @block.sync
                def _(sy, jobs=jobs):
                    sy.dma_start(prm[:, 0:N_P2], d["prm2"][bass.ds(layer, 1)].rearrange("a p c -> p (a c)"))\
                      .then_inc(loaded, 16)
                    for k in range(S2_MLA):
                        if k >= 3:
                            sy.wait_ge(S["w_lo"], k - 2)
                        sy.dma_start(WP[0][:, k % 3, :],
                                     d["w2"][bass.ds(layer, 1), k, :, 0:2048].rearrange("a p c -> p (a c)"))\
                          .then_inc(landed[k % 3], 16)
                    sy.dma_start(mla_w[:, :], d["w2"][bass.ds(layer, 1), S2_MLA, :, 0:2048].rearrange("a p c -> p (a c)"))\
                      .then_inc(landed[3], 16)
                    sy.wait_ge(landed[3], 16)

                @block.tensor
                def _(pe, jobs=jobs):
                    for t in range(N_T2):
                        k = t // 2
                        if t % 2 == 0:
                            pe.wait_ge(S["w_lo"], k + 1)
                        dense_tile(pe, jobs, ("t", t), WP, k, t % 2, S["u_lo"] if t == 0 else None)
                    k = S2_V
                    pe.wait_ge(S["w_lo"], k + 1)
                    w_hi, w_lo = (w[:, k % 2, :].rearrange("p (k c) -> p k c", c=256) for w in WP[1:])
                    for tb in range(TB):
                        b = bank_to_fill(pe, jobs, ("v", tb))
                        for c in range(DC):
                            tok = slice(tb * P, (tb + 1) * P)
                            m = product3(ps[:, b, 0:256], u_hi[:, c, tok], u_lo[:, c, tok], w_hi[:, c, :], w_lo[:, c, :],
                                         c == 0, c == DC - 1)
                        m.then_inc(full[b], 1)

                @block.scalar
                def _(act, jobs=jobs):
                    def split(k):
                        if k < S2_MLA:
                            act.wait_ge(landed[k % 3], 16 * (k // 3 + 1))
                            if k >= 2:
                                b, n, _ = jobs.at["t", 2 * (k - 2) + 1]
                                act.wait_ge(full[b], n)
                            split_w_hi(act, WP, k, None)

                    for c in range(DC):
                        nc.scalar.activation(u_hi[:, c, :], h[:, c, :], ACT.Copy).then_inc(S["u_hi"], 1)
                        if c in (0, 3):
                            split(int(c == 3))
                    act.wait_ge(S["prm_ready"], 1)
                    for t in range(N_T2):
                        b = bank_filled(act, jobs, ("t", t))
                        if t < T2_RW:
                            dst = [sbqk[:, 0, :], sbqk[:, 1, :], sbqk[:, 2, :], sbqk[:, 3, :], cq[:, 0, :], cq[:, 1, :],
                                   ckv, krs][t]
                            nc.scalar.activation(dst, ps[:, b, :], ACT.Copy).then_inc(read[b], 1)
                        else:
                            i = t - T2_RW
                            nc.scalar.activation(rw_in[:, i, :], ps[:, b, :], ACT.Copy, scale=prm_col(P2_OMU + i))\
                              .then_inc(S["mixed"], 1)
                        if t % 2 == 1:
                            split(t // 2 + 2)
                    for tb in range(TB):
                        b = bank_filled(act, jobs, ("v", tb))
                        nc.scalar.activation(sbv[:, tb, :], ps[:, b, 0:256], ACT.Copy).then_inc(read[b], 1)

                @block.gpsimd
                def _(pool):
                    for c in range(DC):
                        pool.wait_ge(S["u_hi"], c + 1)
                        nc.gpsimd.tensor_tensor(u_lo[:, c, :], h[:, c, :], u_hi[:, c, :].bitcast(F32), ALU.subtract)\
                          .then_inc(S["u_lo"], 1)

                @block.vector
                def _(dve, jobs=jobs):
                    split_w_lo(dve, WP, 0, 1)
                    split_w_lo(dve, WP, 1, 2)
                    dve.wait_ge(loaded, 16)
                    nc.vector.tensor_scalar(prm[:, P2_OMU:P2_OMU + 14], prm[:, P2_MU:P2_MU + 14], -1.0, 1.0,
                                            ALU.mult, ALU.add).then_inc(S["prm_ready"], 1)
                    for k in range(2, T2_RW // 2 + 2):
                        split_w_lo(dve, WP, k, k + 1)
                    for t in range(T2_RW, N_T2):
                        i = t - T2_RW
                        b = bank_filled(dve, jobs, ("t", t))
                        dve.wait_ge(S["mixed"], i + 1)
                        nc.vector.scalar_tensor_tensor(rw_in[:, i, 1:L], ps[:, b, 0:L - 1], prm_col(P2_MU + i),
                                                       rw_in[:, i, 1:L], ALU.mult, ALU.add).then_inc(read[b], 1)
                        k = t // 2 + 2
                        if t % 2 == 1 and k < S2_MLA:
                            split_w_lo(dve, WP, k, k + 1)
            close_block()

            mla = [(hd, b) for b in range(TB) for hd in range(MLA_HEADS)]
            NM = len(mla)

            def steps2():
                for k in range(NM + 4):
                    m = [k - lag if 0 <= k - lag < NM else None for lag in range(4)]
                    s = [(k - at) // 4 if (k - at) % 4 == 0 and 0 <= (k - at) // 4 < SB_HEADS else None for at in (0, 2, 4)]
                    yield m, s

            jobs = Banks()
            for name in ("cq_sum", "ckv_sum"):
                jobs.plan(name)
            for hd in range(MLA_HEADS):
                for name in ("qs", "q", "k"):
                    jobs.plan((name, hd))
            for tb in range(TB):
                jobs.plan(("mv", tb))
            for m, s in steps2():
                if s[0] is not None:
                    for c in range(TB):
                        jobs.plan(("z", s[0], c))
                if s[1] is not None:
                    for c in range(TB):
                        jobs.plan(("later", s[1], c))
                if s[2] is not None:
                    jobs.plan(("sb", s[2]))
                if m[0] is not None:
                    jobs.plan(("logits", m[0]))
                if m[2] is not None:
                    jobs.plan(("pt", m[2]))
                if m[3] is not None:
                    jobs.plan(("o", m[3]))

            with nc.Block() as block:
                @block.tensor
                def _(pe, jobs=jobs):
                    uq = mla_w[:, 0:1536].rearrange("p (k c) -> p k c", k=2)
                    ukv = mla_w[:, 1536:2048]
                    b = bank_to_fill(pe, jobs, "cq_sum")
                    pe.wait_ge(S["mla_squared"], 3)
                    nc.tensor.matmul(ps[:, b, :], ones, msq[:, 0, :], start=True, stop=False)
                    nc.tensor.matmul(ps[:, b, :], ones[0:64, :], msq[0:64, 1, :], start=False, stop=True).then_inc(full[b], 1)
                    b = bank_to_fill(pe, jobs, "ckv_sum")
                    nc.tensor.matmul(ps[:, b, :], ones, msq[:, 2, :], start=True, stop=True).then_inc(full[b], 1)
                    pe.wait_ge(S["mla_normed"], 3)
                    for hd in range(MLA_HEADS):
                        for name, c0 in (("qs", 384), ("q", 0)):
                            b = bank_to_fill(pe, jobs, (name, hd))
                            cols = slice(c0 + QW * hd, c0 + QW * hd + QW)
                            nc.tensor.matmul(ps[0:QW, b, :], uq[:, 0, cols], cq[:, 0, :], start=True, stop=False)
                            nc.tensor.matmul(ps[0:QW, b, :], uq[0:64, 1, cols], cq[0:64, 1, :], start=False, stop=True)\
                              .then_inc(full[b], 1)
                        b = bank_to_fill(pe, jobs, ("k", hd))
                        nc.tensor.matmul(ps[0:HD, b, :], ukv[:, HD * hd:HD * hd + HD], ckv, start=True, stop=True)\
                          .then_inc(full[b], 1)
                    for tb in range(TB):
                        b = bank_to_fill(pe, jobs, ("mv", tb))
                        nc.tensor.matmul(ps[:, b, 0:256], ckv[:, tb * P:(tb + 1) * P], ukv[:, 256:512], start=True, stop=True)\
                          .then_inc(full[b], 1)
                    for m, s in steps2():
                        if s[0] is not None:
                            hd = s[0]
                            for c in range(TB):
                                b = bank_to_fill(pe, jobs, ("z", hd, c))
                                nc.tensor.matmul(ps[:, b, 0:L - c * P], sbqk[half(hd), 2 + hd // 2, c * P:(c + 1) * P],
                                                 sbqk[half(hd), hd // 2, c * P:L], start=True, stop=True).then_inc(full[b], 1)
                        if s[1] is not None:
                            hd = s[1]
                            pe.wait_ge(S["sb_masked"], hd + 1)
                            x = sp[hd % 2]
                            for c in range(TB):
                                b = bank_to_fill(pe, jobs, ("later", hd, c))
                                for c2 in range(c, TB):
                                    i = nc.tensor.matmul(ps[:, b, (c2 - c) * P:L - c * P],
                                                         cst[:, C2_TRI:C2_TRI + P] if c2 == c else ones,
                                                         x[:, ZO[c2]:ZO[c2 + 1]], start=(c2 == c), stop=(c2 == TB - 1),
                                                         skip_group_check=True)
                                i.then_inc(full[b], 1)
                        if s[2] is not None:
                            hd = s[2]
                            pe.wait_ge(S["sb_weight"], hd + 1)
                            b = bank_to_fill(pe, jobs, ("sb", hd))
                            for c in range(TB):
                                i = nc.tensor.matmul(ps[half(hd), b, c * P:L], sbv[:, c, hd * HD:(hd + 1) * HD],
                                                     zs[hd % 2][:, ZO[c]:ZO[c + 1]], start=(c == 0), stop=(c == TB - 1),
                                                     skip_group_check=True)
                            i.then_inc(full[b], 1)
                        if m[0] is not None:
                            k = m[0]
                            hd, tb = mla[k]
                            if k == 0:
                                pe.wait_ge(S["q_ready"], MLA_HEADS)
                                pe.wait_ge(S["k_ready"], MLA_HEADS)
                                for q in range(MLA_HEADS):
                                    pe.wait_ge(*read_of(jobs, ("k", q)))
                            b = bank_to_fill(pe, jobs, ("logits", k))
                            nc.tensor.matmul(ps[:, b, 0:(tb + 1) * P], mq[0:QW, hd, tb * P:(tb + 1) * P],
                                             mk[0:QW, hd, 0:(tb + 1) * P], start=True, stop=True).then_inc(full[b], 1)
                        if m[2] is not None:
                            k = m[2]
                            hd, tb = mla[k]
                            pe.wait_ge(S["scaled"], k + 1)
                            b = bank_to_fill(pe, jobs, ("pt", k))
                            for c in range(tb + 1):
                                i = nc.tensor.transpose(ps[:, b, c * P:(c + 1) * P], sc2[:, k % 4, c * P:(c + 1) * P], ident)
                            i.then_inc(full[b], 1)
                        if m[3] is not None:
                            k = m[3]
                            hd, tb = mla[k]
                            pe.wait_ge(*read_of(jobs, ("pt", k)))
                            if k == 0:
                                for q in range(TB):
                                    pe.wait_ge(*read_of(jobs, ("mv", q)))
                            b = bank_to_fill(pe, jobs, ("o", k))
                            for c in range(tb + 1):
                                i = nc.tensor.matmul(ps[half(hd), b, 0:P], mv[:, c, hd * HD:(hd + 1) * HD],
                                                     pt2[:, k % 2, c * P:(c + 1) * P], start=(c == 0), stop=(c == tb))
                            i.then_inc(full[b], 1)

                @block.scalar
                def _(act, jobs=jobs):
                    nc.scalar.activation(msq[:, 0, :], cq[:, 0, :], ACT.Square).then_inc(S["mla_squared"], 1)
                    nc.scalar.activation(msq[0:64, 1, :], cq[0:64, 1, :], ACT.Square).then_inc(S["mla_squared"], 1)
                    nc.scalar.activation(msq[:, 2, :], ckv, ACT.Square).then_inc(S["mla_squared"], 1)
                    for i, name in enumerate(("cq_sum", "ckv_sum")):
                        act.wait_ge(*read_of(jobs, name))
                        nc.scalar.activation(mrs[:, i, :], mrs[:, i, :], ACT.Sqrt).then_inc(S["root"], 1)
                    for hd in range(MLA_HEADS):
                        b = bank_filled(act, jobs, ("q", hd))
                        nc.scalar.activation(mq[0:QW, hd, :], ps[0:QW, b, :], ACT.Copy).then_inc(read[b], 1)
                        b = bank_filled(act, jobs, ("k", hd))
                        nc.scalar.activation(mk[0:HD, hd, :], ps[0:HD, b, :], ACT.Copy).then_inc(read[b], 1)
                    for tb in range(TB):
                        b = bank_filled(act, jobs, ("mv", tb))
                        nc.scalar.activation(mv[:, tb, :], ps[:, b, 0:256], ACT.Copy).then_inc(read[b], 1)
                    own = Signal(act_own)
                    for m, s in steps2():
                        if s[0] is not None:
                            hd = s[0]
                            for c in range(TB):
                                act.wait_ge(*read_of(jobs, ("z", hd, c)))
                            x = sp[hd % 2]
                            act.wait_ge(*own.up(nc.scalar.activation(x, zs[hd % 2], ACT.Abs)))
                            act.wait_ge(*own.up(nc.scalar.activation(x, x, ACT.Exp, scale=-1.0)))
                            nc.scalar.activation(x, x, ACT.Ln, bias=1.0).then_inc(S["sb_abs"], 1)
                        if s[1] is not None:
                            hd = s[1]
                            act.wait_ge(S["sb_arg"], hd + 1)
                            nc.scalar.activation(zs[hd % 2], zs[hd % 2], ACT.Exp).then_inc(S["sb_weight"], 1)
                        if s[2] is not None:
                            hd = s[2]
                            b = bank_filled(act, jobs, ("sb", hd))
                            nc.scalar.activation(o2_hi[half(hd), hd // 2, :], ps[half(hd), b, :], ACT.Copy)\
                              .then_inc(S["o_kept"], 1)
                        if m[1] is not None:
                            k = m[1]
                            w = (mla[k][1] + 1) * P
                            act.wait_ge(*read_of(jobs, ("logits", k)))
                            nc.scalar.activation(sc2[:, k % 4, 0:w], sc2[:, k % 4, 0:w], ACT.Exp, bias=small[:, k % 4:k % 4 + 1],
                                                 scale=-1.0, accum_out=small[:, 4 + k % 4:5 + k % 4]).then_inc(S["exped"], 1)
                        if m[2] is not None:
                            k = m[2]
                            w = (mla[k][1] + 1) * P
                            b = bank_filled(act, jobs, ("pt", k))
                            if k >= 2:
                                b2, n2, _ = jobs.at["o", k - 2]
                                act.wait_ge(full[b2], n2)
                            nc.scalar.activation(pt2[:, k % 2, 0:w], ps[:, b, 0:w], ACT.Copy).then_inc(read[b], 1)
                        if m[3] is not None:
                            k = m[3]
                            hd, tb = mla[k]
                            b = bank_filled(act, jobs, ("o", k))
                            nc.scalar.activation(o2_hi[half(hd), 2 + hd // 2, tb * P:(tb + 1) * P], ps[half(hd), b, 0:P],
                                                 ACT.Copy).then_inc(S["o_kept"], 1)

                @block.gpsimd
                def _(pool, jobs=jobs):
                    pool.wait_ge(S["kr_ready"], 1)
                    for hd in range(MLA_HEADS):
                        nc.gpsimd.tensor_copy(mk[64:96, hd, :], cq[64:96, 1, :]).then_inc(S["k_ready"], 1)
                    for m, s in steps2():
                        if s[0] is not None:
                            hd = s[0]
                            pool.wait_ge(S["sb_soft"], hd + 1)
                            for c in range(TB):
                                x = sp[hd % 2][:, ZO[c]:ZO[c] + P]
                                i = nc.gpsimd.tensor_tensor(x, x, cst[:, C2_SBKEEP:C2_SBKEEP + P], ALU.mult)
                            i.then_inc(S["sb_masked"], 1)
                        if s[1] is not None:
                            hd = s[1]
                            for c in range(TB):
                                pool.wait_ge(*read_of(jobs, ("later", hd, c)))
                                x = zs[hd % 2][:, ZO[c]:ZO[c] + P]
                                i = nc.gpsimd.tensor_tensor(x, x, cst[:, C2_SBNEG:C2_SBNEG + P], ALU.add)
                            i.then_inc(S["sb_arg"], 1)
                        if m[1] is not None:
                            k = m[1]
                            w = (mla[k][1] + 1) * P
                            pool.wait_ge(S["den_ready"], k + 1)
                            nc.gpsimd.tensor_scalar(sc2[:, k % 4, 0:w], sc2[:, k % 4, 0:w], small[:, 8 + k % 4:9 + k % 4],
                                                    None, ALU.mult).then_inc(S["scaled"], 1)

                @block.vector
                def _(dve, jobs=jobs):
                    own = Signal(dve_own)
                    outs = 0
                    cs = cst[64:96, C2_COS:C2_COS + L]
                    sn = cst[64:96, C2_SIN:C2_SIN + L]
                    for i, (name, n) in enumerate((("cq_sum", Q_LORA), ("ckv_sum", P))):
                        b = bank_filled(dve, jobs, name)
                        nc.vector.tensor_scalar(mrs[:, i, :], ps[:, b, :], 1.0 / n, 1e-6, ALU.mult, ALU.add).then_inc(read[b], 1)
                    dve.wait_ge(S["root"], 2)
                    dve.wait_ge(*own.up(nc.vector.reciprocal(mrs[:, :, :], mrs[:, :, :])))
                    for x, g, i in ((cq[:, 0, :], P2_QN, 0), (cq[0:64, 1, :], P2_QN + 1, 0), (ckv, P2_KVN, 1)):
                        n = x.shape[0]
                        nc.vector.scalar_tensor_tensor(x, x, prm[0:n, g:g + 1], mrs[0:n, i, :], ALU.mult, ALU.mult)\
                          .then_inc(S["mla_normed"], 1)
                    kr = cq[64:96, 1, :]
                    own.up(nc.vector.tensor_tensor(kr, kr, cs, ALU.mult))
                    dve.wait_ge(*own.up(nc.vector.tensor_tensor(krs[64:96, :], krs[64:96, :], sn, ALU.mult)))
                    nc.vector.tensor_tensor(kr, kr, krs[64:96, :], ALU.add).then_inc(S["kr_ready"], 1)
                    for hd in range(MLA_HEADS):
                        b = bank_filled(dve, jobs, ("qs", hd))
                        tmp = msq[64:96, hd % 2, :]
                        if hd == 0:
                            dve.wait_ge(S["mla_normed"], 3)
                        if hd >= 2:
                            dve.wait_ge(S["q_ready"], hd - 1)
                        nc.vector.tensor_tensor(tmp, ps[64:96, b, :], sn, ALU.mult).then_inc(read[b], 1)
                        dve.wait_ge(*read_of(jobs, ("q", hd)))
                        x = mq[64:96, hd, :]
                        dve.wait_ge(*own.up(nc.vector.tensor_tensor(x, x, cs, ALU.mult)))
                        dve.wait_ge(*read_of(jobs, ("qs", hd)))
                        nc.vector.tensor_tensor(x, x, tmp, ALU.add).then_inc(S["q_ready"], 1)
                    for m, s in steps2():
                        if s[0] is not None:
                            hd = s[0]
                            if hd >= 2:
                                b, n, _ = jobs.at["sb", hd - 2]
                                dve.wait_ge(full[b], n)
                            for c in range(TB):
                                b = bank_filled(dve, jobs, ("z", hd, c))
                                nc.vector.tensor_scalar(zs[hd % 2][:, ZO[c]:ZO[c + 1]], ps[:, b, 0:L - c * P], HD ** -0.5, None,
                                                        ALU.mult).then_inc(read[b], 1)
                        if m[0] is not None:
                            k = m[0]
                            w = (mla[k][1] + 1) * P
                            if k >= 4:
                                b, n, _ = jobs.at["pt", k - 4]
                                dve.wait_ge(full[b], n)
                            b = bank_filled(dve, jobs, ("logits", k))
                            nc.vector.tensor_tensor_reduce(out=sc2[:, k % 4, 0:w], in0=ps[:, b, 0:w],
                                                           in1=cst[:, C2_CAUSAL + L - w:C2_CAUSAL + L],
                                                           scale=-(QW ** -0.5), scalar=-NEG, op0=ALU.add, op1=ALU.min,
                                                           accum_out=small[:, k % 4:k % 4 + 1]).then_inc(read[b], 1)
                        if s[0] is not None:
                            hd = s[0]
                            dve.wait_ge(S["sb_abs"], hd + 1)
                            nc.vector.scalar_tensor_tensor(sp[hd % 2], zs[hd % 2], 0.0, sp[hd % 2], ALU.max, ALU.add)\
                              .then_inc(S["sb_soft"], 1)
                        if s[1] is not None:
                            hd = s[1]
                            for c in range(TB):
                                b = bank_filled(dve, jobs, ("later", hd, c))
                                x = zs[hd % 2][:, ZO[c]:ZO[c + 1]]
                                nc.vector.tensor_tensor(x, x, ps[:, b, 0:L - c * P], ALU.subtract).then_inc(read[b], 1)
                        if m[1] is not None:
                            k = m[1]
                            dve.wait_ge(S["exped"], k + 1)
                            nc.vector.reciprocal(small[:, 8 + k % 4:9 + k % 4], small[:, 4 + k % 4:5 + k % 4])\
                              .then_inc(S["den_ready"], 1)
                        if s[2] is not None:
                            hd = s[2]
                            outs += 1
                            dve.wait_ge(S["o_kept"], outs)
                            b = bank_filled(dve, jobs, ("sb", hd))
                            nc.vector.tensor_tensor(o2_lo[half(hd), hd // 2, :], ps[half(hd), b, :],
                                                    o2_hi[half(hd), hd // 2, :].bitcast(F32), ALU.subtract).then_inc(read[b], 1)
                        if m[3] is not None:
                            k = m[3]
                            hd, tb = mla[k]
                            outs += 1
                            dve.wait_ge(S["o_kept"], outs)
                            b = bank_filled(dve, jobs, ("o", k))
                            x = (half(hd), 2 + hd // 2, slice(tb * P, (tb + 1) * P))
                            nc.vector.tensor_tensor(o2_lo[x], ps[half(hd), b, 0:P], o2_hi[x].bitcast(F32), ALU.subtract)\
                              .then_inc(read[b], 1)
            close_block()

            alpha, beta = place("alpha", 17352, PAIRS, L)[:, :, :], place("beta", 19400, PAIRS, L)[:, :, :]
            y, bonus = place("y", 11208, PAIRS, L), place("bonus", 15304, PAIRS, L)
            w1t, w2t, w3t, w4t = (place(f"w{i + 1}t", 21448 + 2048 * i, PAIRS, L)[:, :, :] for i in range(4))
            w5t, w6t = place("w5t", IN2, PAIRS, L)[:, :, :], place("w6t", IN2 + 2048, PAIRS, L)[:, :, :]
            both = lambda name, at0, at1, *shape: [place(f"{name}{i}", at, *shape) for i, at in enumerate((at0, at1))]
            xs = both("xs", IN2, 21448, PAIRS, 2 * P)
            x3 = both("x3", IN2 + 1024, 22472, 3, PAIRS * P)
            xt = both("xt", IN2 + 2560, 24008, PAIRS, 3 * P)
            m4 = both("m4", 25544, 27592, PAIRS, 4 * P)
            inv = [place(f"inv{i}", 29640 + 512 * i, L)[:, :] for i in range(2)]
            state, rbuf, xbuf = (place(n, 30664 + 512 * i, L)[:, :] for i, n in enumerate(("state", "rbuf", "xbuf")))
            dend = place("dend", 32200, PAIRS, NCH)[:, :, :]
            lora = place("lora", IN2 + 4096, 1024)[:, :]
            rs = place("rs", 32232, 16 * 512)[:, :]
            names = ("nd", "no", "ndt", "q1", "p2", "ip2", "p2t", "ip4", "wt", "et", "e", "m", "mt", "q2", "m2", "m2t")
            tmp = {n: rs[:, 512 * i:512 * (i + 1)] for i, n in enumerate(names)}
            tmp.update(im2=tmp["p2"], im4=tmp["p2t"], f1=tmp["ip2"], ft=tmp["ip4"])
            i4 = cst[:, C2_I4:C2_I4 + 512]

            def pr(x, p):
                return x[:, p * P:(p + 1) * P]

            SOLVE = [
                [("p2", "ndt", "nd", "act"), ("p2t", "nd", "ndt", "dve")],
                [("ip4", "p2t", "p2", "plus"), ("wt", "ip2", "q1", "act")],
                [("et", "ip4", "wt", "dve"), ("e", "wt", "ip4", "act")],
                [("m", "et", "no", "act"), ("mt", "no", "et", "dve")],
                [("m2", "mt", "m", "act"), ("m2t", "m", "mt", "dve")],
                [("im4", "m2t", "m2", "plus"), ("f1", "im2", "q2", "act")],
                [("ft", "im4", "f1", "act")],
                [("inv", "e", "ft", "dve")],
            ]
            AFTER = {"p2": ("ip2", ALU.add), "mt": ("q2", ALU.subtract), "m2": ("im2", ALU.add)}
            CHAIN = {1: "r", 2: "x", 3: "t", 4: "y"}

            jobs = Banks()
            for name in ("w", "a"):
                for p in range(PAIRS):
                    jobs.plan((name, p))
            for name in ("kk", "bonus"):
                for p in range(PAIRS):
                    jobs.plan((name, p))
            for c in range(NCH + 1):
                if c < NCH:
                    for p in range(PAIRS):
                        jobs.plan(("first", c, p))
                        jobs.plan(("second", c, p))
                for s in range(len(SOLVE)):
                    if c < NCH:
                        for res, *_ in SOLVE[s]:
                            jobs.plan((res, c))
                    if c > 0 and s in CHAIN:
                        jobs.plan((CHAIN[s], c - 1))
            for name in ("mean", "var", "g"):
                for p in range(PAIRS):
                    jobs.plan((name, p))

            def wait_operand(pe, jobs, c, x):
                if x in ("nd", "no"):
                    pe.wait_ge(*read_of(jobs, ("second", c, PAIRS - 1)))
                elif x == "ndt" or x == "q1":
                    pe.wait_ge(S["nd_ready"], 2 * c + (1 if x == "ndt" else 2))
                elif x in ("ip2", "q2", "im2"):
                    pe.wait_ge(S["sq_plus"], 3 * c + ("ip2", "q2", "im2").index(x) + 1)
                else:
                    pe.wait_ge(*read_of(jobs, (x, c)))

            def chain_pe(pe, jobs, c, what):
                q = c % 2
                b = bank_to_fill(pe, jobs, (what, c))
                if what == "r":
                    pe.wait_ge(S["state_ready"], c + 1)
                    pe.wait_ge(*read_of(jobs, ("first", c, PAIRS - 1)))
                    pe.wait_ge(*read_of(jobs, ("second", c, PAIRS - 1)))
                    pe.wait_ge(S["solved"], PAIRS * (c + 1))
                if what == "x":
                    pe.wait_ge(*read_of(jobs, ("inv", c)))
                    pe.wait_ge(*read_of(jobs, ("r", c)))
                if what == "t":
                    pe.wait_ge(*read_of(jobs, ("x", c)))
                for p in range(PAIRS):
                    out = ps[:, b, p * P:(p + 1) * P]
                    bt, kt, vt = (xt[q][:, p, i * P:(i + 1) * P] for i in range(3))
                    al, rho = xs[q][:, p, 0:P], xs[q][:, p, P:2 * P]
                    mb, gt, mk2 = (m4[q][:, p, i * P:(i + 1) * P] for i in (1, 2, 3))
                    pairs = {"r": [(al, pr(state, p)), (gt, vt)],
                             "x": [(pr(inv[q], p), pr(rbuf, p))],
                             "t": [(bt, pr(xbuf, p)), (kt, vt)],
                             "y": [(pr(state, p), rho), (pr(xbuf, p), mb), (vt, mk2)]}[what]
                    for i, (lhs, rhs) in enumerate(pairs):
                        m = nc.tensor.matmul(out, lhs, rhs, start=(p == 0 and i == 0),
                                             stop=(p == PAIRS - 1 and i == len(pairs) - 1), skip_group_check=True)
                m.then_inc(full[b], 1)

            def expand(pool, c):
                q = c % 2
                t = slice(c * CH, (c + 1) * CH)
                blocks = [x3[q][:, i, :].rearrange("p (a b) -> p a b", b=P) for i in range(3)]
                for src, dst, at in ((alpha, xs[q], 0), (rr, xs[q], P), (beta, blocks[0], 0), (rk, blocks[1], 0),
                                     (rv, blocks[2], 0)):
                    for hh in range(2):
                        nc.gpsimd.tensor_scalar(dst[:, :, at + 64 * hh:at + 64 * hh + 64], src[:, :, t],
                                                cst[:, hh:hh + 1], None, ALU.mult).then_inc(S["expanded"], 1)

            with nc.Block() as block:
                @block.sync
                def _(sy, jobs=jobs):
                    sy.dma_start(lora, d["w2"][bass.ds(layer, 1), S2_LORA, :, 0:1024].rearrange("a p c -> p (a c)"))\
                      .then_inc(loaded, 16)
                    sy.wait_ge(loaded, 16)

                @block.tensor
                def _(pe, jobs=jobs):
                    pe.wait_ge(loaded, 16)
                    pe.wait_ge(S["lora_in"], 1)
                    for name, rows, src in (("w", slice(0, 64), wdad), ("a", slice(64, 128), wdad)):
                        for p in range(PAIRS):
                            b = bank_to_fill(pe, jobs, (name, p))
                            nc.tensor.matmul(ps[:, b, :], lora[rows, p * P:(p + 1) * P], src[rows, :], start=True, stop=True)\
                              .then_inc(full[b], 1)
                    for name, src, sig in (("kk", w4t, "kk_sq"), ("bonus", bonus, "first_masked")):
                        for p in range(PAIRS):
                            b = bank_to_fill(pe, jobs, (name, p))
                            pe.wait_ge(S[sig], p + 1)
                            nc.tensor.matmul(ps[:, b, :], blk, src[:, p, :], start=True, stop=True).then_inc(full[b], 1)
                    for c in range(NCH + 1):
                        q = c % 2
                        if c < NCH:
                            pe.wait_ge(S["expanded"], 10 * (c + 1))
                            for p in range(PAIRS):
                                b = bank_to_fill(pe, jobs, ("first", c, p))
                                bt, kt, vv = (pr(x3[q][:, i, :], p) for i in range(3))
                                nc.tensor.matmul(ps[:, b, 0:256], bt, xs[q][:, p, :], start=True, stop=False,
                                                 skip_group_check=True)
                                nc.tensor.matmul(ps[:, b, 256:512], kt, xs[q][:, p, :], start=False, stop=True,
                                                 skip_group_check=True).then_inc(full[b], 1)
                                b = bank_to_fill(pe, jobs, ("second", c, p))
                                for i, v in enumerate((bt, kt, vv)):
                                    nc.tensor.transpose(ps[:, b, i * P:(i + 1) * P], v, ident)
                                nc.tensor.matmul(ps[:, b, 384:512], xs[q][:, p, 0:P], bt, start=True, stop=True,
                                                 skip_group_check=True).then_inc(full[b], 1)
                        for s in range(len(SOLVE)):
                            if c < NCH:
                                for res, lhs, rhs, _ in SOLVE[s]:
                                    for x in (lhs, rhs):
                                        wait_operand(pe, jobs, c, x)
                                    b = bank_to_fill(pe, jobs, (res, c))
                                    for p in range(PAIRS):
                                        m = nc.tensor.matmul(ps[:, b, p * P:(p + 1) * P], pr(tmp[lhs], p), pr(tmp[rhs], p),
                                                             start=(p == 0), stop=(p == PAIRS - 1), skip_group_check=True)
                                    m.then_inc(full[b], 1)
                            if c > 0 and s in CHAIN:
                                chain_pe(pe, jobs, c - 1, CHAIN[s])
                    for name, src, sig in (("mean", y, None), ("var", w2t, "squared")):
                        for p in range(PAIRS):
                            b = bank_to_fill(pe, jobs, (name, p))
                            if sig is None:
                                pe.wait_ge(*read_of(jobs, ("y", NCH - 1)))
                            else:
                                pe.wait_ge(S[sig], p + 1)
                            nc.tensor.matmul(ps[:, b, :], blk, src[:, p, :], start=True, stop=True).then_inc(full[b], 1)
                    for p in range(PAIRS):
                        b = bank_to_fill(pe, jobs, ("g", p))
                        nc.tensor.matmul(ps[:, b, :], lora[:, 512 + p * P:512 + (p + 1) * P], gd, start=True, stop=True)\
                          .then_inc(full[b], 1)

                @block.scalar
                def _(act, jobs=jobs):
                    nc.scalar.activation(gd, gd, ACT.Sigmoid)
                    nc.scalar.activation(wdad[0:64, :], wdad[0:64, :], ACT.Tanh).then_inc(S["lora_in"], 1)
                    for p in range(PAIRS):
                        b = bank_filled(act, jobs, ("w", p))
                        nc.scalar.activation(w1t[:, p, :], ps[:, b, :], ACT.Sigmoid, bias=prm_col(P2_W0 + p)).then_inc(read[b], 1)
                    for p in range(PAIRS):
                        b = bank_filled(act, jobs, ("a", p))
                        nc.scalar.activation(w5t[:, p, :], ps[:, b, :], ACT.Sigmoid, bias=prm_col(P2_A0 + p)).then_inc(read[b], 1)
                    for p in range(PAIRS):
                        nc.scalar.activation(w4t[:, p, :], rk[:, p, :], ACT.Square, scale=prm_col(P2_KK + p))\
                          .then_inc(S["kk_sq"], 1)
                    for p in range(PAIRS):
                        act.wait_ge(*read_of(jobs, ("kk", p)))
                        nc.scalar.activation(w6t[:, p, :], w6t[:, p, :], ACT.Sqrt).then_inc(S["kk_root"], 1)
                    act.wait_ge(S["decayed"], PAIRS)
                    act.wait_ge(S["decayed"], PAIRS + 1)
                    nc.scalar.activation(w2t, w3t, ACT.Exp).then_inc(S["chunk_in"], 1)
                    act.wait_ge(S["decayed"], PAIRS + 2)
                    nc.scalar.activation(w3t, w3t, ACT.Exp, scale=-1.0).then_inc(S["chunk_in"], 1)
                    nc.scalar.activation(w1t, w1t, ACT.Exp).then_inc(S["chunk_in"], 1)
                    for c in range(NCH + 1):
                        if c < NCH:
                            for p in range(PAIRS):
                                b = bank_filled(act, jobs, ("second", c, p))
                                act.wait_ge(S["solved"], PAIRS * c + p + 1)
                                nc.scalar.activation(xt[c % 2][:, p, :], ps[:, b, 0:384], ACT.Copy).then_inc(read[b], 1)
                        for s in range(len(SOLVE)):
                            if c < NCH:
                                for res, _, _, who in SOLVE[s]:
                                    if who == "act":
                                        b = bank_filled(act, jobs, (res, c))
                                        nc.scalar.activation(tmp[res], ps[:, b, :], ACT.Copy).then_inc(read[b], 1)
                            if c > 0 and s in CHAIN:
                                what = CHAIN[s]
                                if what in "rx":
                                    b = bank_filled(act, jobs, (what, c - 1))
                                    nc.scalar.activation(rbuf if what == "r" else xbuf, ps[:, b, :], ACT.Copy,
                                                         scale=-1.0 if what == "r" else 1.0).then_inc(read[b], 1)
                                if what == "y":
                                    b = bank_filled(act, jobs, (what, c - 1))
                                    src = ps[:, b, :].rearrange("p (a b) -> p a b", b=P)
                                    t = slice((c - 1) * CH, c * CH)
                                    nc.scalar.activation(y[0:64, :, t], src[0:64, :, 0:64], ACT.Copy)
                                    nc.scalar.activation(y[64:128, :, t], src[64:128, :, 64:128], ACT.Copy).then_inc(read[b], 1)
                    for p in range(PAIRS):
                        act.wait_ge(*read_of(jobs, ("mean", p)))
                        nc.scalar.activation(w2t[:, p, :], w1t[:, p, :], ACT.Square).then_inc(S["squared"], 1)
                    for p in range(PAIRS):
                        act.wait_ge(*read_of(jobs, ("var", p)))
                        nc.scalar.activation(w3t[:, p, :], w3t[:, p, :], ACT.Sqrt).then_inc(S["root"], 1)
                    for p in range(PAIRS):
                        act.wait_ge(*read_of(jobs, ("g", p)))
                        nc.scalar.activation(o2_hi[:, 4 + p, :], w1t[:, p, :], ACT.Copy).then_inc(S["o_kept"], 1)

                @block.gpsimd
                def _(pool, jobs=jobs):
                    pool.wait_ge(S["zeroed"], 1)
                    nc.gpsimd.memset(state, 0.0).then_inc(S["state_ready"], 1)
                    expand(pool, 0)
                    for c in range(NCH + 1):
                        ndt = tmp["ndt"]
                        if c < NCH:
                            pool.wait_ge(*read_of(jobs, ("second", c, PAIRS - 1)))
                            pool.wait_ge(S["solved"], PAIRS * (c + 1))
                            nc.gpsimd.tensor_tensor(ndt.rearrange("p (a b) -> p a b", b=P), m4[c % 2][:, :, 0:P],
                                                    cst[:, C2_NDT:C2_NDT + 512].rearrange("p (a b) -> p a b", b=P), ALU.mult)\
                              .then_inc(S["nd_ready"], 1)
                            pool.wait_ge(S["nd_ready"], 2 * c + 1)
                            nc.gpsimd.tensor_tensor(tmp["q1"], i4, ndt, ALU.subtract).then_inc(S["nd_ready"], 1)
                        for s in range(len(SOLVE)):
                            if c < NCH:
                                for res, *_ in SOLVE[s]:
                                    if res in AFTER:
                                        dst, op = AFTER[res]
                                        pool.wait_ge(*read_of(jobs, (res, c)))
                                        nc.gpsimd.tensor_tensor(tmp[dst], i4, tmp[res], op).then_inc(S["sq_plus"], 1)
                            if s == 5 and c + 1 < NCH:
                                if c > 0:
                                    b, n, _ = jobs.at["y", c - 1]
                                    pool.wait_ge(full[b], n)
                                expand(pool, c + 1)

                @block.vector
                def _(dve, jobs=jobs):
                    own = Signal(dve_own)
                    chain = lambda i: dve.wait_ge(*own.up(i))
                    for p in range(PAIRS):
                        b = bank_filled(dve, jobs, ("kk", p))
                        nc.vector.tensor_scalar(w6t[:, p, :], ps[:, b, :], 1e-12, None, ALU.max).then_inc(read[b], 1)
                    for p in range(PAIRS):
                        dve.wait_ge(*read_of(jobs, ("w", p)))
                    chain(nc.vector.tensor_scalar(w1t, w1t, -float(np.exp(-0.5)), None, ALU.mult))
                    for p in range(PAIRS):
                        nc.vector.tensor_tensor_scan(w3t[:, p, :], cst[:, C2_RESET:C2_RESET + L], w1t[:, p, :], 0.0,
                                                     ALU.mult, ALU.add).then_inc(S["decayed"], 1)
                    dve.wait_ge(S["decayed"], PAIRS)
                    nc.vector.tensor_tensor(w1t, w3t, w1t, ALU.subtract).then_inc(S["decayed"], 1)
                    dve.wait_ge(S["kk_root"], PAIRS)
                    chain(nc.vector.reciprocal(w6t, w6t))
                    for p in range(PAIRS):
                        i = own.up(nc.vector.scalar_tensor_tensor(alpha[:, p, :], rk[:, p, :], prm_col(P2_KK + p), w6t[:, p, :],
                                                                  ALU.mult, ALU.mult))
                    dve.wait_ge(*i)
                    for p in range(PAIRS):
                        dve.wait_ge(*read_of(jobs, ("a", p)))
                    chain(nc.vector.tensor_tensor(beta, alpha, w5t, ALU.mult))
                    for p in range(PAIRS):
                        i = own.up(nc.vector.tensor_scalar(w5t[:, p, :], w5t[:, p, :], 1.0, prm_col(P2_KA + p),
                                                           ALU.subtract, ALU.mult))
                    dve.wait_ge(*i)
                    dve.wait_ge(S["kk_sq"], PAIRS)
                    chain(nc.vector.scalar_tensor_tensor(rk, w5t, 1.0, rk, ALU.add, ALU.mult))
                    for p in range(PAIRS):
                        nc.vector.scalar_tensor_tensor(bonus[:, p, :], rr[:, p, :], prm_col(P2_RK + p), rk[:, p, :],
                                                       ALU.mult, ALU.mult).then_inc(S["first_masked"], 1)
                    dve.wait_ge(S["chunk_in"], 1)
                    dve.wait_ge(S["first_masked"], PAIRS)
                    chain(nc.vector.tensor_copy(dend, w2t[:, :, CH - 1:L:CH]))
                    nc.vector.tensor_tensor(rr, rr, w2t, ALU.mult).then_inc(S["decayed"], 1)
                    dve.wait_ge(S["chunk_in"], 2)
                    chain(nc.vector.tensor_tensor(beta, beta, w3t, ALU.mult))
                    chain(nc.vector.tensor_tensor(rk, rk, w3t, ALU.mult))
                    dve.wait_ge(S["chunk_in"], 3)
                    chain(nc.vector.tensor_tensor(alpha, alpha, w1t, ALU.mult))
                    for p in range(PAIRS):
                        b = bank_filled(dve, jobs, ("bonus", p))
                        nc.vector.tensor_tensor(bonus[:, p, :], ps[:, b, :], rv[:, p, :], ALU.mult).then_inc(read[b], 1)
                    for p in range(PAIRS):
                        dve.wait_ge(*read_of(jobs, ("bonus", p)))
                    dve.wait_ge(S["decayed"], PAIRS + 2)
                    chain(nc.vector.tensor_copy(small[:, 40:41], bonus[:, 0, 0:1]))
                    nc.vector.tensor_copy(small[:, 41:42], small[:, 40:41]).then_inc(S["zeroed"], 1)
                    for c in range(NCH + 1):
                        q = c % 2
                        if c < NCH:
                            if c > 0:
                                b, n, _ = jobs.at["inv", c - 1]
                                dve.wait_ge(full[b], n)
                            for p in range(PAIRS):
                                b = bank_filled(dve, jobs, ("first", c, p))
                                nc.vector.tensor_tensor(m4[q][:, p, :], ps[:, b, :], cst[:, C2_RW:C2_RW + 512], ALU.mult)\
                                  .then_inc(read[b], 1)
                                dve.wait_ge(*read_of(jobs, ("first", c, p)))
                                b = bank_filled(dve, jobs, ("second", c, p))
                                own.up(nc.vector.tensor_tensor(pr(tmp["nd"], p), ps[:, b, 384:512], cst[:, C2_ND:C2_ND + P], ALU.mult))
                                nc.vector.tensor_tensor(pr(tmp["no"], p), ps[:, b, 384:512], cst[:, C2_NO:C2_NO + P], ALU.mult)\
                                  .then_inc(S["solved"], 1)
                        for s in range(len(SOLVE)):
                            if c < NCH:
                                for res, _, _, who in SOLVE[s]:
                                    if who == "act":
                                        continue
                                    b = bank_filled(dve, jobs, (res, c))
                                    dst = inv[q] if res == "inv" else tmp[res]
                                    if who == "plus":
                                        i = nc.vector.tensor_tensor(dst, ps[:, b, :], i4, ALU.add)
                                    else:
                                        i = nc.vector.tensor_copy(dst, ps[:, b, :])
                                    i.then_inc(read[b], 1)
                            if c > 0 and s in CHAIN and CHAIN[s] == "y" and c < NCH:
                                pass
                            if c > 0 and s in CHAIN and CHAIN[s] == "y":
                                b, n, _ = jobs.at["y", c - 1]
                                dve.wait_ge(full[b], n)
                                b = bank_filled(dve, jobs, ("t", c - 1))
                                nc.vector.tensor_tensor(state, state, ps[:, b, :], ALU.add).then_inc(read[b], 1)
                                dve.wait_ge(*read_of(jobs, ("t", c - 1)))
                                st = state.rearrange("p (a b) -> p a b", b=P)
                                nc.vector.tensor_tensor(st, st, dend[:, :, c - 1:c].to_broadcast([P, PAIRS, P]), ALU.mult)\
                                  .then_inc(S["state_ready"], 1)
                    for p in range(PAIRS):
                        b = bank_filled(dve, jobs, ("mean", p))
                        nc.vector.scalar_tensor_tensor(w1t[:, p, :], ps[:, b, :], -1.0 / HD, y[:, p, :], ALU.mult, ALU.add)\
                          .then_inc(read[b], 1)
                    for p in range(PAIRS):
                        b = bank_filled(dve, jobs, ("var", p))
                        nc.vector.tensor_scalar(w3t[:, p, :], ps[:, b, :], 1.0 / HD, 64e-5, ALU.mult, ALU.add).then_inc(read[b], 1)
                    dve.wait_ge(S["root"], PAIRS)
                    chain(nc.vector.reciprocal(w3t, w3t))
                    for p in range(PAIRS):
                        i = own.up(nc.vector.scalar_tensor_tensor(w1t[:, p, :], w1t[:, p, :], prm_col(P2_GNG + p), w3t[:, p, :],
                                                                  ALU.mult, ALU.mult))
                    dve.wait_ge(*i)
                    for p in range(PAIRS):
                        i = own.up(nc.vector.scalar_tensor_tensor(w1t[:, p, :], w1t[:, p, :], prm_col(P2_GNB + p), bonus[:, p, :],
                                                                  ALU.add, ALU.add))
                    dve.wait_ge(*i)
                    for p in range(PAIRS):
                        b = bank_filled(dve, jobs, ("g", p))
                        nc.vector.tensor_tensor(w1t[:, p, :], w1t[:, p, :], ps[:, b, :], ALU.mult).then_inc(read[b], 1)
                    for p in range(PAIRS):
                        dve.wait_ge(S["o_kept"], p + 1)
                        nc.vector.tensor_tensor(o2_lo[:, 4 + p, :], w1t[:, p, :], o2_hi[:, 4 + p, :].bitcast(F32), ALU.subtract)\
                          .then_inc(S["ln_out"], 1)
            close_block()

            hid2_hi, hid2_lo = place("hid2_hi", 17352, FF2, L, dt=F32R), place("hid2_lo", 28616, FF2, L, dt=F32R)
            W2 = weight_room("d", 39880, 2)
            cv2, ge = place("cv2", 52168, L)[:, :], place("ge", 52680, L)[:, :]
            nrm, nx = place("nrm", 17352, L)[:, :], place("nx", 17864, L)[:, :]
            lsq = place("lsq", 18376, DC, L)
            N_ALL = 4 + FF2 + FF2 // 2
            GU, GD = 4, 4 + FF2
            ROUNDS = 5
            jobs = Banks(start=1)
            for n in range(DC):
                jobs.plan(("wo", n))
            for name in ("mean1", "var1"):
                jobs.plan(name)
            jobs.plan_body([(w, j) for j in range(4) for w in ("conv", "up")], ROUNDS)
            for j in range(FF2 - 4 * ROUNDS):
                for w in ("conv", "up"):
                    jobs.plan((w, 4 + j))
            for n in range(DC):
                jobs.plan(("down", n))
            for name in ("mean2", "var2"):
                jobs.plan(name)

            def ln_pe(pe, name, squared):
                b = bank_to_fill(pe, jobs, name)
                for c in range(DC):
                    pe.wait_ge(S["squared" if squared else "h_ready"], (squared - 1 if squared else 0) + c + 1)
                    m = nc.tensor.matmul(ps[:, b, :], ones, (lsq if squared else h)[:, c, :], start=(c == 0), stop=(c == DC - 1))
                m.then_inc(full[b], 1)

            def ln_act(act, i):
                for c in range(DC):
                    act.wait_ge(S["centered"], DC * i + c + 1)
                    nc.scalar.activation(lsq[:, c, :], h[:, c, :], ACT.Square).then_inc(S["squared"], 1)
                act.wait_ge(*read_of(jobs, f"var{i + 1}"))
                nc.scalar.activation(nrm, nrm, ACT.Sqrt).then_inc(S["root"], 1)
                for c in range(DC):
                    act.wait_ge(S["normed"], DC * i + c + 1)
                    g = (P2_LN1B, P2_LN2B)[i] + c
                    nc.scalar.activation(h[:, c, :], h[:, c, :], ACT.Identity, bias=prm_col(g)).then_inc(S["ln_out"], 1)
                    if i == 0 and c > 0:
                        act.wait_ge(S["ln_out"], c)
                        nc.scalar.activation(u_hi[:, c - 1, :], h[:, c - 1, :], ACT.Copy).then_inc(S["u_hi"], 1)
                if i == 0:
                    act.wait_ge(S["ln_out"], DC)
                    nc.scalar.activation(u_hi[:, DC - 1, :], h[:, DC - 1, :], ACT.Copy).then_inc(S["u_hi"], 1)

            def ln_dve(dve, i, own):
                b = bank_filled(dve, jobs, f"mean{i + 1}")
                nc.vector.tensor_scalar(nx, ps[:, b, :], -1.0 / D, None, ALU.mult).then_inc(read[b], 1)
                dve.wait_ge(*read_of(jobs, f"mean{i + 1}"))
                for c in range(DC):
                    nc.vector.tensor_tensor(h[:, c, :], h[:, c, :], nx, ALU.add).then_inc(S["centered"], 1)
                b = bank_filled(dve, jobs, f"var{i + 1}")
                nc.vector.tensor_scalar(nrm, ps[:, b, :], 1.0 / D, 1e-5, ALU.mult, ALU.add).then_inc(read[b], 1)
                dve.wait_ge(S["root"], i + 1)
                dve.wait_ge(*own.up(nc.vector.reciprocal(nrm, nrm)))
                for c in range(DC):
                    g = (P2_LN1G, P2_LN2G)[i] + c
                    nc.vector.scalar_tensor_tensor(h[:, c, :], h[:, c, :], prm_col(g), nrm, ALU.mult, ALU.mult)\
                      .then_inc(S["normed"], 1)

            def at(x, k):
                if isinstance(k, int):
                    return x[:, k, :]
                return x[:, bass.ds(k, 1), :].rearrange("p a c -> p (a c)")

            def col(c, k):
                return prm[:, c + k:c + k + 1] if isinstance(k, int) else prm[:, bass.ds(k + c, 1)]

            with nc.Block() as block:
                @block.sync
                def _(sy, jobs=jobs):
                    def fetch(g, j):
                        sy.dma_start(W2[0][:, j, :],
                                     d["w2"][bass.ds(layer, 1), bass.ds(g, 1), :, 0:2048].rearrange("a b p c -> p (a b c)"))\
                          .then_inc(landed[j], 16)

                    fetch(S2_WO, 0)
                    fetch(S2_WO + 1, 1)
                    with sy.Fori(1, N_ALL // 2) as it:
                        for j in range(2):
                            sy.wait_ge(S["w_lo"], it * 2 + (j - 1))
                            fetch(it * 2 + (S2_WO + j), j)
                    sy.wait_ge(S["w_lo"], N_ALL - 2)
                    fetch(S2_WO + N_ALL - 1, 0)

                @block.tensor
                def _(pe, jobs=jobs):
                    for b in range(8):
                        pe.sem_inc(full[b], 1)
                        pe.sem_inc(read[b], 1)
                    for n in range(DC):
                        if n % 2 == 0:
                            pe.wait_ge(S["w_lo"], n // 2 + 1)
                        dense_tile(pe, jobs, ("wo", n), W2, n // 2, n % 2, x=(o2_hi, o2_lo))
                    ln_pe(pe, "mean1", 0)
                    ln_pe(pe, "var1", 1)
                    pe.wait_ge(S["u_lo"], DC)
                    with pe.Fori(0, ROUNDS) as it:
                        for j in range(4):
                            pe.wait_ge(S["w_lo"], it * 4 + (GU + j + 1))
                            dense_tile(pe, jobs, ("conv", j), W2, j, 0, it=it)
                            dense_tile(pe, jobs, ("up", j), W2, j, 1, it=it)
                    for j in range(2):
                        pe.wait_ge(S["w_lo"], GU + 4 * ROUNDS + j + 1)
                        dense_tile(pe, jobs, ("conv", 4 + j), W2, j, 0)
                        dense_tile(pe, jobs, ("up", 4 + j), W2, j, 1)
                    for k in range(FF2 // 2):
                        pe.wait_ge(S["w_lo"], GD + k + 1)
                        w_hi, w_lo = (w[:, k % 2, :].rearrange("p (k c) -> p k c", c=D) for w in W2[1:])
                        for c in range(2):
                            t = 2 * k + c
                            pe.wait_ge(S["hidden_kept"], t + 2)
                            for n in range(DC):
                                b = jobs.at["down", n][0]
                                if t == 0:
                                    bank_to_fill(pe, jobs, ("down", n))
                                f = slice(n * P, (n + 1) * P)
                                m = product3(ps[:, b, :], w_hi[:, c, f], w_lo[:, c, f], hid2_hi[:, t, :], hid2_lo[:, t, :],
                                             t == 0, t == FF2 - 1)
                                if t == FF2 - 1:
                                    m.then_inc(full[b], 1)
                        if k < FF2 // 2 - 1:
                            m.then_inc(S["slab_used"], 1)
                    b = bank_to_fill(pe, jobs, "mean2")
                    for c in range(DC):
                        pe.wait_ge(*read_of(jobs, ("down", c)))
                        m = nc.tensor.matmul(ps[:, b, :], ones, h[:, c, :], start=(c == 0), stop=(c == DC - 1))
                    m.then_inc(full[b], 1)
                    ln_pe(pe, "var2", DC + 1)

                @block.scalar
                def _(act, jobs=jobs):
                    act.sem_inc(S["gelu"], 1)
                    for g in range(GU + 2):
                        act.wait_ge(landed[g % 2], 16 * (g // 2 + 1))
                        if g >= 2:
                            b, n, _ = jobs.at["wo", 2 * (g - 2) + 1]
                            act.wait_ge(full[b], n)
                        split_w_hi(act, W2, g, None)
                    ln_act(act, 0)

                    def pair(j, k, it, seq):
                        b = bank_filled(act, jobs, ("conv", j), it)
                        act.wait_ge(S["gelu"], seq + 1)
                        nc.scalar.activation(cv2, ps[:, b, :], ACT.Identity, bias=col(P2_CB, k),
                                             scale=col(P2_CW + 2 * FF2, k)).then_inc(S["mixed"], 1)
                        act.wait_ge(S["shifted"], seq + 1)
                        act.wait_ge(S["hidden_kept"], seq + 1)
                        nc.scalar.activation(ge, cv2, ACT.Gelu).then_inc(S["gelu"], 1)
                        act.wait_ge(*read_of(jobs, ("up", j), it))
                        nc.scalar.activation(at(hid2_hi, k), ge, ACT.Copy).then_inc(S["m_hi"], 1)
                        landings = (GU + j + 2) // 2 + 1
                        act.wait_ge(landed[j % 2], 16 * (2 * ROUNDS + landings - 2) if it is None else it * 32 + 16 * landings)
                        split_w_hi(act, W2, j, None)

                    with act.Fori(0, ROUNDS) as it:
                        for j in range(4):
                            pair(j, it * 4 + j, it, it * 4 + j)
                    for j in range(2):
                        pair(4 + j, 4 * ROUNDS + j, None, 4 * ROUNDS + j)
                    for g in range(GD + 2, N_ALL):
                        act.wait_ge(landed[g % 2], 16 * (g // 2 + 1))
                        act.wait_ge(S["slab_used"], g - GD - 1)
                        split_w_hi(act, W2, g, None)
                    ln_act(act, 1)

                @block.gpsimd
                def _(pool, jobs=jobs):
                    pool.sem_inc(S["hidden_kept"], 1)
                    for c in range(DC):
                        pool.wait_ge(S["u_hi"], c + 1)
                        nc.gpsimd.tensor_tensor(u_lo[:, c, :], h[:, c, :], u_hi[:, c, :].bitcast(F32), ALU.subtract)\
                          .then_inc(S["u_lo"], 1)
                    with pool.Fori(0, ROUNDS) as it:
                        for j in range(4):
                            k = it * 4 + j
                            pool.wait_ge(S["m_hi"], it * 4 + (j + 1))
                            nc.gpsimd.tensor_tensor(at(hid2_lo, k), ge, at(hid2_hi, k).bitcast(F32), ALU.subtract)\
                              .then_inc(S["hidden_kept"], 1)
                    for k in range(4 * ROUNDS, FF2):
                        pool.wait_ge(S["m_hi"], k + 1)
                        nc.gpsimd.tensor_tensor(hid2_lo[:, k, :], ge, hid2_hi[:, k, :].bitcast(F32), ALU.subtract)\
                          .then_inc(S["hidden_kept"], 1)

                @block.vector
                def _(dve, jobs=jobs):
                    own = Signal(dve_own)
                    split_w_lo(dve, W2, 0, 1)
                    split_w_lo(dve, W2, 1, 2)
                    for n in range(DC):
                        b = bank_filled(dve, jobs, ("wo", n))
                        nc.vector.scalar_tensor_tensor(h[:, n, :], h[:, n, :], ALPHA, ps[:, b, :], ALU.mult, ALU.add)\
                          .then_inc(read[b], 1)
                        dve.wait_ge(*read_of(jobs, ("wo", n)))
                        dve.sem_inc(S["h_ready"], 1)
                        if n % 2 == 1:
                            split_w_lo(dve, W2, n // 2, n // 2 + 3)
                    ln_dve(dve, 0, own)

                    def pair(j, k, it, seq):
                        x = cv2
                        b = bank_filled(dve, jobs, ("conv", j), it)
                        dve.wait_ge(S["mixed"], seq + 1)
                        nc.vector.scalar_tensor_tensor(x[:, 1:L], ps[:, b, 0:L - 1], col(P2_CW + FF2, k), x[:, 1:L],
                                                       ALU.mult, ALU.add).then_inc(dve_own, 1)
                        dve.wait_ge(dve_own, seq + 2)
                        nc.vector.scalar_tensor_tensor(x[:, 2:L], ps[:, b, 0:L - 2], col(P2_CW, k), x[:, 2:L],
                                                       ALU.mult, ALU.add).then_inc(read[b], 1)
                        dve.wait_ge(*read_of(jobs, ("conv", j), it))
                        dve.sem_inc(S["shifted"], 1)
                        b = bank_filled(dve, jobs, ("up", j), it)
                        dve.wait_ge(S["gelu"], seq + 2)
                        nc.vector.tensor_tensor(ge, ge, ps[:, b, :], ALU.mult).then_inc(read[b], 1)
                        split_w_lo(dve, W2, j, seq + GU + 3)

                    with dve.Fori(0, ROUNDS) as it:
                        for j in range(4):
                            pair(j, it * 4 + j, it, it * 4 + j)
                    for j in range(2):
                        pair(4 + j, 4 * ROUNDS + j, None, 4 * ROUNDS + j)
                    own.n += FF2
                    for g in range(GD + 2, N_ALL):
                        split_w_lo(dve, W2, g, g + 1)
                    for n in range(DC):
                        b = bank_filled(dve, jobs, ("down", n))
                        nc.vector.scalar_tensor_tensor(h[:, n, :], h[:, n, :], ALPHA, ps[:, b, :], ALU.mult, ALU.add)\
                          .then_inc(read[b], 1)
                    for n in range(DC):
                        dve.wait_ge(*read_of(jobs, ("down", n)))
                    ln_dve(dve, 1, own)
            close_block()

        with nc.Block() as block:
            @block.sync
            def _(sy):
                for c in range(DC):
                    sy.dma_start(d["out"][c], h[:, c, :]).then_inc(stored, 16)
                sy.wait_ge(stored, 16 * DC)


def _slabs(w, cols):
    w = w[:, cols]
    k, n = w.shape
    w = w.reshape(k // P, P, n // 256, 256).transpose(2, 1, 0, 3)
    return w.reshape(n // 256, P, (k // P) * 256)


def _padded(x, width=SLOT):
    out = np.zeros(x.shape[:-1] + (width,), x.dtype)
    out[..., :x.shape[-1]] = x
    return out


def _down_slabs(w):
    n = w.shape[0] // 256
    return w.reshape(n, 2, P, D).transpose(0, 2, 1, 3).reshape(n, P, 2 * D)


def _first_weights(w_in, w_a, w_b, w_c, w_o, w_up, w_down):
    o = W_OFF
    r = lambda name, n, at=0: list(range(o[name] + at, o[name] + at + n))
    qk = (r("ik", 64) * 2 + r("aq", 384) + r("ak", 64) * 2 + r("iq", 512) + r("bq", 768) + r("bk", 768) + r("cq", 512)
          + r("ck", 64) * 2 + r("ck", 64, 64) * 2)
    assert len(qk) == N_QK * P
    qk += [0] * P
    v = r("bv", 768) + r("av", 64) + r("cv", 128) + r("iw", 8)
    v += [0] * (1024 - len(v))
    out = [_padded(_slabs(w_in, qk)), _padded(_slabs(w_in, v))]
    for n in range(DC):
        cut = lambda w, c0: w[:, c0 + n * P:c0 + (n + 1) * P].reshape(-1, P, P).transpose(1, 0, 2).reshape(P, -1)
        g = [cut(w_in, o["gates"] + j * D) for j in range(3)]
        out.append(_padded(np.concatenate(g[:2], axis=1))[None])
        out.append(np.concatenate([g[2], cut(w_a, 0), cut(w_b, 0), cut(w_c, 0)], axis=1)[None])
    out.append(_padded(_slabs(w_o, list(range(D)))))
    for half in range(2):
        ff = range(half * 2 * D, (half + 1) * 2 * D)
        out.append(_padded(_slabs(w_up, list(ff))))
        out.append(_padded(_down_slabs(w_down[ff[0]:ff[-1] + 1])))
    return np.concatenate(out)


def _columns(v):
    return v.reshape(-1, P).T


def _first_constants():
    c = np.zeros((P, N_C1), np.float32)
    p = np.arange(P)
    c[:, C1_INV] = np.power(np.float32(10000.0), -(p % 32).astype(np.float32) / np.float32(32)).astype(np.float32)
    c[:, C1_SIGN] = np.where(p % 64 < 32, -1.0, 1.0)
    c[:, C1_ID:C1_ID + P] = np.eye(P)
    c[:, C1_ONE:C1_ONE + P] = 1.0
    c[:, C1_BLK:C1_BLK + P] = p[:, None] // 64 == p[None] // 64
    off = lambda on: np.where(on, 0.0, NEG)
    t, s = p[:, None], p[None]
    c[:, C1_CAUSAL:C1_CAUSAL + P] = off(s <= t)
    s2 = np.arange(2 * P)[None] - P
    c[:, C1_WIN:C1_WIN + 2 * P] = off((s2 <= t) & (s2 > t - 128))
    for r in range(4):
        back = 4 * t + r - np.arange(L)[None]
        c[:, C1_DIL + r * L:C1_DIL + (r + 1) * L] = off((back >= 0) & (back <= 128))
    c[:, C1_DIL16:C1_DIL16 + P] = off(s <= t)
    c[:, C1_DIL16 + P:C1_DIL16 + 2 * P] = off((s <= t) & ((t - s) % 4 == 0))
    return c


def _second_weights(w_in, w_uq, w_ukv, w2, a2, g2, w_o, w_up, w_down):
    sb, mla, rw = 0, 3 * SB_HEADS * HD, 3 * SB_HEADS * HD + Q_LORA + P + RD
    r = lambda at, n: list(range(at, at + n))
    wz = np.concatenate([w_in, np.zeros((D, 1), w_in.dtype)], axis=1)
    z = [w_in.shape[1]]
    kr = mla + Q_LORA + P
    cols = (r(sb, 512) + r(mla, Q_LORA) + r(kr, RD) + z * 32 + r(mla + Q_LORA, P)
            + z * 64 + r(kr + RD // 2, RD // 2) + r(kr, RD // 2) + z * 32 + r(rw, 14 * P))
    assert len(cols) == N_T2 * P
    out = [_padded(_slabs(wz, cols)), _padded(_slabs(wz, r(sb + 512, 256)))]
    swapped = [QW * hd + c for hd in range(MLA_HEADS) for c in r(0, NOPE) + r(NOPE + RD // 2, RD // 2) + r(NOPE, RD // 2)]
    uq = np.concatenate([w_uq, w_uq[:, swapped]], axis=1)
    uq = np.concatenate([uq, np.zeros((2 * P - Q_LORA, uq.shape[1]), uq.dtype)])
    uq = uq.reshape(2, P, -1).transpose(1, 0, 2).reshape(P, -1)
    keys = [2 * HD * hd + c for hd in range(MLA_HEADS) for c in range(HD)]
    ukv = w_ukv[:, keys + [c + HD for c in keys]]
    out.append(_padded(np.concatenate([uq, ukv], axis=1))[None])
    out.append(_padded(np.concatenate([np.concatenate([w2, a2]), g2], axis=1))[None])
    out.append(_padded(_slabs(w_o, r(0, D))))
    ff = FF2 * P
    out.append(_padded(_slabs(w_up, [c for n in range(FF2) for c in r(n * P, P) + r(ff + n * P, P)])))
    out.append(_padded(_down_slabs(w_down)))
    return np.concatenate(out)


def _second_constants():
    c = np.zeros((P, N_C2), np.float32)
    c[:, 2:C2_CAUSAL] = _first_constants()[:, 2:C2_CAUSAL]
    a, b = np.arange(P)[:, None], np.arange(P)[None]
    c[:HD, 0] = 1.0
    c[HD:, 1] = 1.0
    c[:, C2_CAUSAL + 3 * P:C2_CAUSAL + 4 * P] = np.where(b <= a, 0.0, NEG)
    c[:, C2_SBKEEP:C2_SBKEEP + P] = a < b
    c[:, C2_SBNEG:C2_SBNEG + P] = np.where(a < b, 0.0, NEG)
    c[:, C2_TRI:C2_TRI + P] = a >= b
    same = a // CH == b // CH
    for i, on in enumerate((a < b, a <= b) * 2):
        c[:, C2_RW + i * P:C2_RW + (i + 1) * P] = on & same
    near = a // 8 == b // 8
    c[:, C2_ND:C2_ND + P] = (b < a) & near
    c[:, C2_NO:C2_NO + P] = (b < a) & same & ~near
    c[:, C2_NDT:C2_NDT + 4 * P] = np.tile((a < b) & near, (1, 4))
    c[:, C2_I4:C2_I4 + 4 * P] = np.tile(np.eye(P), (1, 4))
    c[:, C2_RESET:C2_RESET + L] = np.arange(L) % CH != 0
    freq = (np.float32(1) / np.power(np.float32(10000), np.arange(0, RD, 2, dtype=np.float32) / np.float32(RD))).astype(np.float32)
    ang = (np.arange(L, dtype=np.float32)[None] * freq[:, None]).astype(np.float32).astype(np.float64)
    c[64:96, C2_COS:C2_COS + L] = np.tile(np.cos(ang), (2, 1))
    c[64:96, C2_SIN:C2_SIN + L] = np.concatenate([-np.sin(ang), np.sin(ang)])
    return c


def layout(x):
    f = lambda n: np.ascontiguousarray(np.asarray(x[n]))
    a = {}
    a["x"] = f("x")[0].T.reshape(DC, P, L)
    a["pos"] = np.broadcast_to(f("positions").astype(np.int32), (P, L))
    a["cst1"] = _first_constants()
    a["w1"] = np.stack([_first_weights(*(f(n)[l] for n in ("w_in", "w_a", "w_b", "w_c", "w_o", "w_up", "w_down")))
                        for l in range(DEPTH)])
    assert a["w1"].shape[1] == N_S1
    prm = np.zeros((DEPTH, P, N_P1), np.float32)
    for l in range(DEPTH):
        prm[l, :, P1_ATTN:P1_ATTN + 8] = _columns(f("attn_norm")[l])
        prm[l, :, P1_MLP:P1_MLP + 8] = _columns(f("mlp_norm")[l])
        prm[l, :, P1_IK] = np.tile(f("idx_k_norm")[l], 2)
        prm[l, :, P1_SINK:P1_SINK + 8] = f("sinks")[l][None]
        prm[l, :, P1_FINAL:P1_FINAL + 8] = _columns(f("final_norm"))
    a["prm1"] = prm
    a["cst2"] = _second_constants()
    names = ("w_in", "mla_w_uq", "mla_w_ukv", "rwkv_w2", "rwkv_a2", "rwkv_g2", "w_o", "ffn_w_up", "ffn_w_down")
    a["w2"] = np.stack([_second_weights(*(f(n + "_2")[l] for n in names)) for l in range(DEPTH)])
    assert a["w2"].shape[1] == N_S2
    prm = np.zeros((DEPTH, P, N_P2), np.float32)
    for l in range(DEPTH):
        for n, at in (("rwkv_mu", P2_MU), ("rwkv_w0", P2_W0), ("rwkv_a0", P2_A0), ("rwkv_k_k", P2_KK), ("rwkv_k_a", P2_KA),
                      ("rwkv_r_k", P2_RK), ("rwkv_gn_g", P2_GNG), ("rwkv_gn_b", P2_GNB), ("mla_kv_norm", P2_KVN),
                      ("ln1_g", P2_LN1G), ("ln1_b", P2_LN1B), ("ln2_g", P2_LN2G), ("ln2_b", P2_LN2B),
                      ("ffn_conv_w", P2_CW), ("ffn_conv_b", P2_CB)):
            v = _columns(f(n + "_2")[l].reshape(-1))
            prm[l, :, at:at + v.shape[1]] = v
        prm[l, :, P2_QN] = f("mla_q_norm_2")[l][0:P]
        prm[l, 0:Q_LORA - P, P2_QN + 1] = f("mla_q_norm_2")[l][P:]
    a["prm2"] = prm
    return {n: np.ascontiguousarray(v) for n, v in a.items()}


def kernel(**inputs):
    import concourse.bacc as bacc
    from concourse.bass_utils import run_bass_kernel_spmd

    nc = bacc.Bacc("TRN2", target_bir_lowering=False, num_devices=1)
    arrays, d = {}, {}
    for name, a in layout(inputs).items():
        arrays[f"in_{name}"] = a
        d[name] = nc.dram_tensor(f"in_{name}", a.shape, mybir.dt.from_np(a.dtype), kind="ExternalInput").ap()
    d["out"] = nc.dram_tensor("out", (DC, P, L), F32, kind="ExternalOutput").ap()
    build(nc, d)
    r = run_bass_kernel_spmd(nc, [arrays], core_ids=[0])
    out = r.results[0]["out"].reshape(D, L)
    return np.ascontiguousarray(out.T)[None]
```

```python
from contextlib import ExitStack

import numpy as np

import concourse.bass as bass
from concourse import mybir

F32 = mybir.dt.float32
F32R = mybir.dt.float32r
I32 = mybir.dt.int32
ALU = mybir.AluOpType
ACT = mybir.ActivationFunctionType
AX_X = mybir.AxisListType.X

P = 128
L = 512
D = 1024
DC = D // P
TB = L // P
DEPTH = 2
HD = 64
A_HEADS, IDX_HEADS, B_GROUP_HEADS, C_HEADS = 6, 8, 4, 8
TOPK = 128
FF1 = 4 * D // P
FF2 = 2816 // P
NEG = -1.0e30
TAKEN = -3.0e38
ALPHA = float((2 * DEPTH) ** 0.25)

T_IK, T_AQ, T_AK, T_IQ, T_BQ, T_BK, T_CQ, T_CK = 0, 1, 4, 5, 9, 15, 21, 25
N_QK = 27
W_OFF = dict(aq=0, ak=384, av=448, iq=512, ik=1024, iw=1088, bq=1096, bk=1864, bv=2632,
             cq=3400, ck=3912, cv=4040, gates=4168)

SLOT = 2176
ROOM = 53208
BASE = 16512
MERGE_B = 1024 + 9 * P
N_PROJ1, N_V1, N_MERGE, N_WO = 14, 4, 16, 4
N_UP1, N_DOWN1 = FF1 // 2, FF1 // 2
S1_V = N_PROJ1
S1_MERGE = S1_V + N_V1
S1_WO = S1_MERGE + N_MERGE
S1_UP = S1_WO + N_WO
S1_DOWN = S1_UP + N_UP1
N_S1 = S1_DOWN + N_DOWN1

P1_ATTN, P1_MLP, P1_IK, P1_SINK, P1_FINAL, P1_NSINK = 0, 8, 16, 17, 25, 40
N_P1 = 33
C1_INV, C1_SIGN, C1_ID, C1_ONE, C1_BLK, C1_CAUSAL, C1_WIN, C1_DIL = 0, 1, 2, 130, 258, 386, 514, 770
C1_DIL16 = C1_DIL + 4 * L
N_C1 = C1_DIL16 + 2 * P

SB_HEADS, MLA_HEADS = 4, 4
Q_LORA, NOPE, RD = 192, 64, 32
QW = NOPE + RD
PAIRS, CH = 4, 64
NCH = L // CH
T2_SBQ, T2_SBK, T2_CQ, T2_CKV, T2_KRS, T2_RW = 0, 2, 4, 6, 7, 8
N_T2 = 22
N_PROJ2 = N_T2 // 2
S2_V = N_PROJ2
S2_MLA = S2_V + 1
S2_LORA = S2_MLA + 1
S2_WO = S2_LORA + 1
S2_UP = S2_WO + 4
S2_DOWN = S2_UP + FF2
N_S2 = S2_DOWN + FF2 // 2
(P2_MU, P2_W0, P2_A0, P2_KK, P2_KA, P2_RK, P2_GNG, P2_GNB, P2_QN, P2_KVN, P2_LN1G, P2_LN1B, P2_LN2G, P2_LN2B,
 P2_CW, P2_CB) = 0, 14, 18, 22, 26, 30, 34, 38, 42, 44, 45, 53, 61, 69, 77, 77 + 3 * FF2
N_P2 = P2_CB + FF2
P2_OMU = N_P2
(C2_CAUSAL, C2_SBKEEP, C2_SBNEG, C2_TRI, C2_RW, C2_ND, C2_NO, C2_NDT, C2_I4, C2_RESET, C2_COS, C2_SIN) = (
    514, 1026, 1154, 1282, 1410, 1922, 2050, 2178, 2690, 3202, 3714, 4226)
N_C2 = 4738


class Signal:

    def __init__(self, sem, base=0):
        self.sem, self.n, self.base = sem, 0, base

    def up(self, instruction, by=1):
        instruction.then_inc(self.sem, by)
        self.n += by
        return self.sem, self.base + self.n


class Banks:

    def __init__(self, start=0):
        self.fills, self.at, self.next = [start] * 8, {}, 0

    def plan(self, name):
        b = self.next
        self.next = (b + 1) % 8
        self.fills[b] += 1
        self.at[name] = (b, self.fills[b], 0)

    def plan_body(self, names, times):
        at = []
        before = list(self.fills)
        for name in names:
            b = self.next
            self.next = (b + 1) % 8
            self.fills[b] += 1
            at.append((name, b, self.fills[b]))
        for name, b, n in at:
            self.at[name] = (b, n, self.fills[b] - before[b])
        for b in range(8):
            self.fills[b] = before[b] + times * (self.fills[b] - before[b])


def build(nc, d, debug=False, stop=None):
    ctx = ExitStack()
    with ctx:
        sems = []

        def sem(name):
            s = ctx.enter_context(nc.semaphore(name))
            sems.append(s)
            return s

        def sb(name, shape, dt=F32):
            return ctx.enter_context(nc.sbuf_tensor(name, shape, dt))

        def place(name, at, *shape, dt=F32):
            n = int(np.prod(shape))
            assert at >= 0 and at + n <= ROOM
            return nc.alloc_sbuf_tensor_at(name, [P, *shape], dt, offset=BASE + 4 * at)

        h = place("h", 0, DC, L)
        cst = place("cst", 4096, 4800)
        prm = place("prm", 8896, 200)
        small = place("small", 9096, 64)
        ctx.enter_context(nc.sbuf_tensor("fence", [P, ROOM], F32))
        ps = ctx.enter_context(nc.psum_tensor("ps", [P, 8, L], F32))

        full = [sem(f"bank{b}_full") for b in range(8)]
        read = [sem(f"bank{b}_read") for b in range(8)]
        landed = [sem(f"raw{s}_landed") for s in range(4)]
        loaded = sem("loaded")
        stored = sem("stored")
        act_own = sem("act_own")
        dve_own = sem("dve_own")
        pool_own = sem("pool_own")
        S = {n: sem(n) for n in (
            "rope_arg", "rope_sin", "squared", "root", "normed", "swapped", "roped", "ik_squared", "ik_normed",
            "relued", "iscored", "mask_ready", "row_min", "exped", "den_ready", "scaled", "sink_exped", "pt_kept", "o_kept",
            "gate_kept", "gated", "merged_ready", "h_ready", "hidden_kept", "slab_used",
            "mixed", "w_hi", "w_lo", "sq_used", "u_hi", "u_lo", "m_hi", "m_lo", "down_read", "relu_kept", "hid_sq", "prm_ready", "roots2", "mla_normed", "mla_squared", "kr_ready", "q_ready", "k_ready",
            "sb_abs", "sb_soft", "sb_masked", "sb_arg", "sb_weight", "centered", "shifted", "act_act", "gelu", "lora_in",
            "wa_ready", "kk_sq", "kk_root", "decayed", "chunk_in", "expanded", "first_masked", "sq_plus", "nd_ready",
            "solved", "alpha_in", "ahead", "rv", "ln_out", "scaled_in", "state_ready")}

        def close_block():
            nums = [s.num for s in sems]
            assert nums == list(range(nums[0], nums[0] + len(nums)))
            nc.gpsimd.sem_clear(range(nums[0], nums[-1] + 1))
            nc.all_engine_barrier()

        ident = cst[:, C1_ID:C1_ID + P]
        ones = cst[:, C1_ONE:C1_ONE + P]
        blk = cst[:, C1_BLK:C1_BLK + P]
        causal = cst[:, C1_CAUSAL:C1_CAUSAL + P]

        u_hi, u_lo = place("u_hi", 9160, DC, L, dt=F32R), place("u_lo", 13256, DC, L, dt=F32R)
        qk = place("qk", 34488, N_QK, L)
        av, bv = place("av", 48312, TB, HD), place("bv", 48568, TB, 12 * HD)
        cv, iw = place("cv", 51640, TB, 2 * HD), place("iw", 52152, TB, IDX_HEADS)
        cos, sin = place("cos", 52184, L)[:, :], place("sin", 52696, L)[:, :]
        four = place("four", 17352, 4, L)
        swp, ikn, iksq = four[:, 0:2, :], four[:, 2, :], four[:, 3, :]
        rstd = place("rstd", 19400, L)[:, :]
        o_hi, o_lo = place("o_hi", 17352, 9, L, dt=F32R), place("o_lo", 21960, 9, L, dt=F32R)
        sc = place("sc", 26568, 4, 768)
        pt = place("pt", 29640, 2, 768)
        score = place("score", 31176, 3, L)
        rel = place("rel", 32712, 2, L)
        diag = place("diag", 33736, 4, P)

        def weight_room(tag, at, raws, width=2048, split_at=None):
            raw = place(f"raw_{tag}", at, raws, width)
            hi_at, lo_at = split_at or (at + raws * width, at + (raws + 2) * width)
            hi, lo = place(f"w_hi_{tag}", hi_at, 2, width, dt=F32R), place(f"w_lo_{tag}", lo_at, 2, width, dt=F32R)
            return raw, hi, lo

        WC = weight_room("c", 39096, 2, SLOT)
        WF = weight_room("f", 39096, 2, split_at=(34760, 43192))
        W2 = weight_room("d", 39880, 2)

        def fetch_ahead(sy, raw, w, k, width):
            for j in range(2):
                sy.dma_start(raw[:, j, 0:width], w[bass.ds(layer, 1), k + j, :, 0:width].rearrange("a p c -> p (a c)"))\
                  .then_inc(S["ahead"], 16)
            sy.wait_ge(S["ahead"], 32)

        def come_ahead(sy):
            for j in range(2):
                sy.sem_inc(landed[j], 16)

        with nc.Block() as block:
            @block.sync
            def _(sy):
                sy.dma_start(swp[:, 0, :].bitcast(I32), d["pos"]).then_inc(landed[0], 16)
                sy.dma_start(cst[:, 0:C1_ID], d["cst1"][:, 0:C1_ID]).then_inc(landed[0], 16)
                for c in range(DC):
                    sy.dma_start(h[:, c, :], d["x"][c]).then_inc(loaded, 16)
                sy.dma_start(cst[:, C1_ID:N_C1], d["cst1"][:, C1_ID:N_C1]).then_inc(loaded, 16)
                sy.wait_ge(loaded, 16 * (DC + 1))

            @block.vector
            def _(dve):
                own = Signal(dve_own)
                dve.wait_ge(landed[0], 32)
                inv2pi, magic = float(np.float32(1 / (2 * np.pi))), 12582912.0
                c1 = 6.28125
                c2 = float(np.float32(2 * np.pi - c1))
                c3 = float(np.float32(2 * np.pi - c1 - c2))
                t = own.up(nc.vector.tensor_copy(swp[:, 1, :], swp[:, 0, :].bitcast(I32)))
                dve.wait_ge(*t)
                t = own.up(nc.vector.tensor_scalar(ikn, swp[:, 1, :], cst[:, C1_INV:C1_INV + 1], None, ALU.mult))
                dve.wait_ge(*t)
                for dst, quarter in ((sin, 0.0), (cos, 0.25)):
                    t = own.up(nc.vector.tensor_scalar(iksq, ikn, inv2pi, quarter, ALU.mult, ALU.add))
                    dve.wait_ge(*t)
                    t = own.up(nc.vector.tensor_scalar(iksq, iksq, magic, None, ALU.add))
                    dve.wait_ge(*t)
                    t = own.up(nc.vector.tensor_scalar(iksq, iksq, magic, None, ALU.subtract))
                    dve.wait_ge(*t)
                    t = own.up(nc.vector.scalar_tensor_tensor(dst, iksq, -c1, ikn, ALU.mult, ALU.add))
                    dve.wait_ge(*t)
                    t = own.up(nc.vector.scalar_tensor_tensor(dst, iksq, -c2, dst, ALU.mult, ALU.add))
                    dve.wait_ge(*t)
                    t = own.up(nc.vector.scalar_tensor_tensor(dst, iksq, -c3, dst, ALU.mult, ALU.add))
                    dve.wait_ge(*t)
                    t = own.up(nc.vector.tensor_scalar(dst, dst, float(np.float32(quarter * 2 * np.pi)), 3.1415925,
                                                       ALU.add, ALU.min))
                    dve.wait_ge(*t)
                    nc.vector.tensor_scalar(dst, dst, -3.1415925, None, ALU.max).then_inc(S["rope_arg"], 1)
                dve.wait_ge(S["rope_sin"], 2)
                nc.vector.tensor_scalar(sin, sin, cst[:, C1_SIGN:C1_SIGN + 1], None, ALU.mult).then_inc(dve_own, 1)

            @block.scalar
            def _(act):
                for n, dst in enumerate((sin, cos)):
                    act.wait_ge(S["rope_arg"], n + 1)
                    nc.scalar.activation(dst, dst, ACT.Sin).then_inc(S["rope_sin"], 1)
        close_block()

        def bank_to_fill(pe, jobs, name, it=None):
            b, n, per = jobs.at[name]
            if per:
                pe.wait_ge(read[b], it * per + (n - 1))
            elif n > 1:
                pe.wait_ge(read[b], n - 1)
            return b

        def bank_filled(eng, jobs, name, it=None):
            b, n, per = jobs.at[name]
            eng.wait_ge(full[b], it * per + n if per else n)
            return b

        def read_of(jobs, name, it=None):
            b, n, per = jobs.at[name]
            return read[b], (it * per + n if per else n)

        def norm_squares(act, wait_h, sq):
            for c in range(DC):
                if wait_h:
                    act.wait_ge(S["h_ready"], c + 1)
                if c >= 4:
                    act.wait_ge(S["sq_used"], c - 3)
                nc.scalar.activation(sq[:, c % 4, :], h[:, c, :], ACT.Square).then_inc(S["squared"], 1)

        def norm_sum(pe, jobs, name, sq):
            b = bank_to_fill(pe, jobs, name)
            for c in range(DC):
                pe.wait_ge(S["squared"], c + 1)
                m = nc.tensor.matmul(ps[:, b, :], ones, sq[:, c % 4, :], start=(c == 0), stop=(c == DC - 1))
                m.then_inc(full[b] if c == DC - 1 else S["sq_used"], 1)

        def norm_root(act, jobs, name, r):
            act.wait_ge(*read_of(jobs, name))
            nc.scalar.activation(r, r, ACT.Sqrt).then_inc(S["root"], 1)

        def norm_inverse(dve, jobs, name, own, roots, r):
            b = bank_filled(dve, jobs, name)
            nc.vector.tensor_scalar(r, ps[:, b, :], 1.0 / D, 1e-6, ALU.mult, ALU.add).then_inc(read[b], 1)
            dve.wait_ge(S["root"], roots)
            dve.wait_ge(*own.up(nc.vector.reciprocal(r, r)))

        def norm_apply(dve, gain, r, x, dst=None, lo=False):
            for c in range(DC):
                if c >= 4 and dst is None:
                    dve.wait_ge(S["u_lo"], c - 3)
                nc.vector.scalar_tensor_tensor(x[:, c % 4, :] if dst is None else dst[:, c, :], h[:, c, :],
                                               prm[:, gain + c:gain + c + 1], r, ALU.mult, ALU.mult)\
                  .then_inc(S["normed"], 1)
                if lo and c > 0:
                    lo_chunk(dve, x, c - 1)
            if lo:
                lo_chunk(dve, x, DC - 1)

        def split_u_hi(act, x):
            for c in range(DC):
                act.wait_ge(S["normed"], c + 1)
                nc.scalar.activation(u_hi[:, c, :], x[:, c % 4, :], ACT.Copy).then_inc(S["u_hi"], 1)

        def lo_chunk(eng, x, c):
            eng.wait_ge(S["u_hi"], c + 1)
            eng.tensor_tensor(u_lo[:, c, :], x[:, c % 4, :], u_hi[:, c, :].bitcast(F32), ALU.subtract).then_inc(S["u_lo"], 1)

        def split_u_lo(pool, x):
            for c in range(DC):
                lo_chunk(pool, x, c)

        def split_w_hi(act, W, k, count, width=2048):
            raw, hi, lo = W
            nc.scalar.activation(hi[:, k % 2, 0:width], raw[:, k % raw.shape[1], 0:width], ACT.Copy).then_inc(S["w_hi"], 1)

        def split_w_lo(dve, W, k, count, width=2048):
            raw, hi, lo = W
            dve.wait_ge(S["w_hi"], count)
            nc.vector.tensor_tensor(lo[:, k % 2, 0:width], raw[:, k % raw.shape[1], 0:width],
                                    hi[:, k % 2, 0:width].bitcast(F32), ALU.subtract).then_inc(S["w_lo"], 1)

        def product3(out, w_hi, w_lo, x_hi, x_lo, start, stop):
            nc.tensor.matmul(out, w_hi, x_hi, start=start, stop=False)
            nc.tensor.matmul(out, w_hi, x_lo, start=False, stop=False)
            return nc.tensor.matmul(out, w_lo, x_hi, start=False, stop=stop)

        def dense_tile(pe, jobs, name, W, k, half, first_wait=None, it=None, x=None, first=0):
            b = bank_to_fill(pe, jobs, name, it)
            x_hi, x_lo = (u_hi, u_lo) if x is None else x
            w_hi, w_lo = (w[:, k % 2, 0:2048].rearrange("p (k c) -> p k c", c=256)[:, :, half * P:(half + 1) * P]
                          for w in W[1:])
            for c in range(DC):
                if first_wait is not None:
                    pe.wait_ge(first_wait, c + 1 + first)
                m = product3(ps[:, b, :], w_hi[:, c, :], w_lo[:, c, :], x_hi[:, c, :], x_lo[:, c, :],
                             c == 0, c == DC - 1)
            m.then_inc(full[b], 1)

        with nc.Fori(0, DEPTH) as layer:
            def w1_slab(k):
                return d["w1"][bass.ds(layer, 1), k].rearrange("a p c -> p (a c)")

            jobs = Banks()
            for name in ["sum", ("t", 0), ("t", 1), "ik_sum"] + [("t", t) for t in range(2, N_QK)]:
                jobs.plan(name)
            for s in range(N_V1):
                for tb in range(TB):
                    jobs.plan(("v", s, tb))

            WA = weight_room("a", 19912, 3)

            def last_of(k):
                return ("t", min(2 * k + 1, N_QK - 1)) if k < N_PROJ1 else ("v", k - S1_V, TB - 1)

            def split_a_hi(act, jobs, k):
                if k < S1_MERGE:
                    act.wait_ge(landed[k % 3], 16 * (k // 3 + 1))
                    if k >= 2:
                        b, n, _ = jobs.at[last_of(k - 2)]
                        act.wait_ge(full[b], n)
                    split_w_hi(act, WA, k, k + 1)

            def split_a_lo(dve, k):
                if k < S1_MERGE:
                    split_w_lo(dve, WA, k, k + 1)

            with nc.Block() as block:
                @block.sync
                def _(sy, jobs=jobs):
                    sy.dma_start(prm[:, 0:N_P1], d["prm1"][bass.ds(layer, 1)].rearrange("a p c -> p (a c)"))\
                      .then_inc(loaded, 16)
                    for k in range(S1_MERGE):
                        if k >= 3:
                            sy.wait_ge(S["w_lo"], k - 2)
                        sy.dma_start(WA[0][:, k % 3, :], w1_slab(k)[:, 0:2048]).then_inc(landed[k % 3], 16)

                @block.tensor
                def _(pe, jobs=jobs):
                    norm_sum(pe, jobs, "sum", four)

                    def tile(t):
                        if t % 2 == 0:
                            pe.wait_ge(S["w_lo"], t // 2 + 1)
                        dense_tile(pe, jobs, ("t", t), WA, t // 2, t % 2, S["u_lo"] if t == 0 else None)

                    tile(0)
                    tile(1)
                    b = bank_to_fill(pe, jobs, "ik_sum")
                    pe.wait_ge(S["ik_squared"], 1)
                    nc.tensor.matmul(ps[:, b, :], blk, iksq, start=True, stop=True).then_inc(full[b], 1)
                    for t in range(2, N_QK):
                        tile(t)
                    for s in range(N_V1):
                        k = S1_V + s
                        pe.wait_ge(S["w_lo"], k + 1)
                        w_hi, w_lo = (w[:, k % 2, :].rearrange("p (k c) -> p k c", c=256) for w in WA[1:])
                        for tb in range(TB):
                            b = bank_to_fill(pe, jobs, ("v", s, tb))
                            tok = slice(tb, L, TB) if s in (1, 2) else slice(tb * P, (tb + 1) * P)
                            for c in range(DC):
                                m = product3(ps[:, b, 0:256], u_hi[:, c, tok], u_lo[:, c, tok], w_hi[:, c, :], w_lo[:, c, :],
                                             c == 0, c == DC - 1)
                            m.then_inc(full[b], 1)

                @block.scalar
                def _(act, jobs=jobs):
                    norm_squares(act, False, four)
                    split_a_hi(act, jobs, 0)
                    split_a_hi(act, jobs, 1)
                    norm_root(act, jobs, "sum", rstd)
                    split_u_hi(act, four)

                    def swap(i, src):
                        if i < 2:
                            act.wait_ge(S["u_lo"], DC)
                        else:
                            act.wait_ge(S["roped"], i - 1)
                        for q in range(4):
                            o = q ^ 1
                            nc.scalar.activation(swp[32 * q:32 * q + 32, i % 2, :], src[32 * o:32 * o + 32, :],
                                                 ACT.Copy).then_inc(S["swapped"], 1)

                    act.wait_ge(*read_of(jobs, ("t", 0)))
                    nc.scalar.activation(iksq, ikn, ACT.Square).then_inc(S["ik_squared"], 1)
                    b = bank_filled(act, jobs, ("t", 1))
                    swap(0, ps[:, b, :])
                    split_a_hi(act, jobs, 2)
                    norm_root(act, jobs, "ik_sum", rstd)
                    act.wait_ge(S["ik_normed"], 1)
                    swap(1, ikn)
                    for t in range(2, N_QK):
                        b = bank_filled(act, jobs, ("t", t))
                        swap(t, ps[:, b, :])
                        if t % 2 == 1 or t == N_QK - 1:
                            split_a_hi(act, jobs, t // 2 + 2)
                    for s in range(N_V1):
                        for tb in range(TB):
                            b = bank_filled(act, jobs, ("v", s, tb))
                            if s < 3:
                                nc.scalar.activation(bv[:, tb, 256 * s:256 * s + 256], ps[:, b, 0:256], ACT.Copy)\
                                  .then_inc(read[b], 1)
                            else:
                                nc.scalar.activation(av[:, tb, :], ps[:, b, 0:HD], ACT.Copy)
                                nc.scalar.activation(cv[:, tb, :], ps[:, b, HD:3 * HD], ACT.Copy)
                                nc.scalar.activation(iw[:, tb, :], ps[:, b, 3 * HD:3 * HD + IDX_HEADS], ACT.Copy,
                                                     scale=IDX_HEADS ** -0.5).then_inc(read[b], 1)
                        split_a_hi(act, jobs, S1_V + s + 2)

                @block.gpsimd
                def _(pool):
                    split_u_lo(pool, four)

                @block.vector
                def _(dve, jobs=jobs):
                    own = Signal(dve_own)
                    split_a_lo(dve, 0)
                    split_a_lo(dve, 1)
                    dve.wait_ge(loaded, 16)
                    norm_inverse(dve, jobs, "sum", own, 1, rstd)
                    norm_apply(dve, P1_ATTN, rstd, four)
                    b = bank_filled(dve, jobs, ("t", 0))
                    dve.wait_ge(S["u_lo"], DC)
                    nc.vector.tensor_copy(ikn, ps[:, b, :]).then_inc(read[b], 1)

                    def rope(i, t, src, done):
                        dve.wait_ge(S["swapped"], 4 * (i + 1))
                        nc.vector.tensor_tensor(qk[:, t, :], src, cos, ALU.mult).then_inc(*done[:2])
                        dve.wait_ge(*own.up(nc.vector.tensor_tensor(swp[:, i % 2, :], swp[:, i % 2, :], sin, ALU.mult)))
                        dve.wait_ge(done[0], done[2])
                        nc.vector.tensor_tensor(qk[:, t, :], qk[:, t, :], swp[:, i % 2, :], ALU.add)\
                          .then_inc(S["roped"], 1)

                    def rope_bank(i, t):
                        b = bank_filled(dve, jobs, ("t", t))
                        rope(i, t, ps[:, b, :], (read[b], 1, jobs.at["t", t][1]))

                    rope_bank(0, 1)
                    split_a_lo(dve, 2)
                    b = bank_filled(dve, jobs, "ik_sum")
                    nc.vector.tensor_scalar(rstd, ps[:, b, :], 1.0 / HD, 1e-6, ALU.mult, ALU.add).then_inc(read[b], 1)
                    dve.wait_ge(S["root"], 2)
                    dve.wait_ge(*own.up(nc.vector.reciprocal(rstd, rstd)))
                    nc.vector.scalar_tensor_tensor(ikn, ikn, prm[:, P1_IK:P1_IK + 1], rstd, ALU.mult, ALU.mult)\
                      .then_inc(S["ik_normed"], 1)
                    dve.wait_ge(S["ik_normed"], 1)
                    own.n += 1
                    rope(1, T_IK, ikn, (dve_own, 1, own.n))
                    for t in range(2, N_QK):
                        rope_bank(t, t)
                        if t % 2 == 1 or t == N_QK - 1:
                            split_a_lo(dve, t // 2 + 2)
                    for s in range(N_V1):
                        split_a_lo(dve, S1_V + s + 2)
            close_block()

            b_units = [("B", j, r) for r in range(TB) for j in range(B_GROUP_HEADS)]
            c_units = [("C", hd, b) for b in range(TB) for hd in range(C_HEADS)]
            units = [u for i, b_unit in enumerate(b_units) for u in (b_unit, *c_units[2 * i:2 * i + 2])]
            units += [("A", hd, b) for b in range(TB) for hd in range(A_HEADS)]

            def unit_width(unit):
                br, hd, b = unit
                return 6 * P if br == "B" else min(b + 1, 2) * P if br == "C" else (b + 1) * P

            def steps():
                for k in range(len(units) + 5):
                    yield [k - lag if 0 <= k - lag < len(units) else None for lag in (0, 1, 3, 4, 5)]

            jobs = Banks()
            for b in range(1, TB):
                for hd in range(IDX_HEADS):
                    jobs.plan(("index", b, hd))
            for s0, s1, s2, s3, s4 in steps():
                if s0 is not None:
                    jobs.plan(("logits", s0, 0))
                    if units[s0][0] == "B":
                        jobs.plan(("logits", s0, 1))
                if s2 is not None:
                    jobs.plan(("pt", s2, 0))
                    if units[s2][0] == "B":
                        jobs.plan(("pt", s2, 1))
                if s3 is not None:
                    jobs.plan(("o", s3))

            def o_place(unit):
                br, hd, b = unit
                return {"A": 0, "B": 3, "C": 5}[br] + hd // 2, (slice(b, L, TB) if br == "B" else slice(b * P, (b + 1) * P))

            def half(hd):
                return slice(HD * (hd % 2), HD * (hd % 2) + HD)

            with nc.Block() as block:
                @block.sync
                def _(sy, jobs=jobs):
                    last_b = max(k for k, unit in enumerate(units) if unit[0] == "B")
                    bank, n, _ = jobs.at["logits", last_b, 1]
                    sy.wait_ge(full[bank], n)
                    fetch_ahead(sy, WC[0], d["w1"], S1_MERGE, SLOT)

                @block.tensor
                def _(pe, jobs=jobs):
                    for b in range(1, TB):
                        for hd in range(IDX_HEADS):
                            bank = bank_to_fill(pe, jobs, ("index", b, hd))
                            nc.tensor.matmul(ps[:, bank, 0:(b + 1) * P], qk[half(hd), T_IQ + hd // 2, b * P:(b + 1) * P],
                                             qk[half(hd), T_IK, 0:(b + 1) * P], start=True, stop=True)\
                              .then_inc(full[bank], 1)

                    def logits(k):
                        br, hd, b = units[k]
                        w = unit_width(units[k])
                        bank = bank_to_fill(pe, jobs, ("logits", k, 0))
                        if br == "A":
                            nc.tensor.matmul(ps[:, bank, 0:w], qk[half(hd), T_AQ + hd // 2, b * P:(b + 1) * P],
                                             qk[half(hd), T_AK, 0:w], start=True, stop=True).then_inc(full[bank], 1)
                        elif br == "C":
                            nc.tensor.matmul(ps[:, bank, 0:w], qk[half(hd), T_CQ + hd // 2, b * P:(b + 1) * P],
                                             qk[half(hd), T_CK + hd // 4, (b + 1) * P - w:(b + 1) * P],
                                             start=True, stop=True).then_inc(full[bank], 1)
                        else:
                            rows = slice(b, L, TB)
                            q = [qk[half(hd), T_BQ + (g * 4 + hd) // 2, rows] for g in range(3)]
                            kk = [qk[half(hd), T_BK + (g * 4 + hd) // 2, :] for g in range(3)]
                            nc.tensor.matmul(ps[:, bank, :], q[0], kk[0], start=True, stop=True).then_inc(full[bank], 1)
                            bank = bank_to_fill(pe, jobs, ("logits", k, 1))
                            for g in (1, 2):
                                m = nc.tensor.matmul(ps[:, bank, (g - 1) * P:g * P], q[g], kk[g][:, rows],
                                                     start=(g == 1), stop=(g == 2), skip_group_check=True)
                            m.then_inc(full[bank], 1)

                    def turn(k):
                        n = unit_width(units[k]) // P
                        pe.wait_ge(S["scaled"], k + 1)
                        for part in range(2 if n > 4 else 1):
                            bank = bank_to_fill(pe, jobs, ("pt", k, part))
                            cs = range(4 * part, min(4 * part + 4, n))
                            for c in cs:
                                m = nc.tensor.matmul(ps[:, bank, (c % 4) * P:(c % 4 + 1) * P], sc[:, k % 4, c * P:(c + 1) * P],
                                                     diag[:, k % 4, :], start=(c == cs[0]), stop=(c == cs[-1]),
                                                     skip_group_check=True)
                            m.then_inc(full[bank], 1)

                    def values(k):
                        br, hd, b = units[k]
                        n = unit_width(units[k]) // P
                        pe.wait_ge(*read_of(jobs, ("pt", k, 1 if n > 4 else 0)))
                        if n > 4:
                            pe.wait_ge(*read_of(jobs, ("pt", k, 0)))
                        bank = bank_to_fill(pe, jobs, ("o", k))
                        for c in range(n):
                            if br == "A":
                                v = av[:, c, :]
                            elif br == "C":
                                v = cv[:, b + 1 - n + c, hd // 4 * HD:(hd // 4 + 1) * HD]
                            elif c < 4:
                                v = bv[:, c, hd * HD:(hd + 1) * HD]
                            else:
                                v = bv[:, b, (4 * (c - 3) + hd) * HD:(4 * (c - 3) + hd + 1) * HD]
                            m = nc.tensor.matmul(ps[half(hd), bank, 0:P], v, pt[:, k % 2, c * P:(c + 1) * P],
                                                 start=(c == 0), stop=(c == n - 1))
                        m.then_inc(full[bank], 1)

                    for s0, s1, s2, s3, s4 in steps():
                        if s0 is not None:
                            logits(s0)
                        if s2 is not None:
                            turn(s2)
                        if s3 is not None:
                            values(s3)

                @block.scalar
                def _(act, jobs=jobs):
                    i = 0
                    for b in range(1, TB):
                        for hd in range(IDX_HEADS):
                            bank = bank_filled(act, jobs, ("index", b, hd))
                            if i >= 2:
                                act.wait_ge(S["iscored"], i - 1)
                            nc.scalar.activation(rel[:, i % 2, 0:(b + 1) * P], ps[:, bank, 0:(b + 1) * P], ACT.Relu,
                                                 scale=HD ** -0.5).then_inc(read[bank], 1)
                            i += 1
                    sinks = 0
                    for s0, s1, s2, s3, s4 in steps():
                        if s1 is not None:
                            k, w = s1, unit_width(units[s1])
                            if units[k][0] == "A":
                                act.wait_ge(*read_of(jobs, ("logits", k, 0)))
                            else:
                                act.wait_ge(S["row_min"], k + 1)
                            if units[k][0] == "C":
                                s = P1_SINK + units[k][1]
                                nc.scalar.activation(small[:, 16 + k % 4:17 + k % 4], small[:, k % 4:k % 4 + 1], ACT.Exp,
                                                     bias=prm[:, s:s + 1])
                            nc.scalar.activation(sc[:, k % 4, 0:w], sc[:, k % 4, 0:w], ACT.Exp,
                                                 bias=small[:, k % 4:k % 4 + 1], scale=-1.0,
                                                 accum_out=small[:, 4 + k % 4:5 + k % 4]).then_inc(S["exped"], 1)
                        if s4 is not None:
                            bank = bank_filled(act, jobs, ("o", s4))
                            br, hd, b = units[s4]
                            tile, cols = o_place(units[s4])
                            nc.scalar.activation(o_hi[half(hd), tile, cols], ps[half(hd), bank, 0:P], ACT.Copy)\
                              .then_inc(S["o_kept"], 1)
                        if s2 is not None:
                            k, n = s2, unit_width(units[s2]) // P
                            for part in range(2 if n > 4 else 1):
                                bank = bank_filled(act, jobs, ("pt", k, part))
                                if k >= 2:
                                    b, m, _ = jobs.at["o", k - 2]
                                    act.wait_ge(full[b], m)
                                lo, hi = 512 * part, min(512 * part + 512, n * P)
                                nc.scalar.activation(pt[:, k % 2, lo:hi], ps[:, bank, 0:hi - lo], ACT.Copy)\
                                  .then_inc(read[bank], 1)

                @block.gpsimd
                def _(pool, jobs=jobs):
                    for k, unit in enumerate(units):
                        pool.wait_ge(S["den_ready"], k + 1)
                        if k >= 4:
                            bank, m, _ = jobs.at["pt", k - 4, 1 if units[k - 4][0] == "B" else 0]
                            pool.wait_ge(full[bank], m)
                        nc.gpsimd.tensor_scalar(diag[:, k % 4, :], ident, small[:, 8 + k % 4:9 + k % 4], None,
                                                ALU.mult).then_inc(S["scaled"], 1)

                @block.vector
                def _(dve, jobs=jobs):
                    own = Signal(dve_own)
                    dve.wait_ge(*own.up(nc.vector.tensor_scalar(prm[:, P1_NSINK:P1_NSINK + C_HEADS],
                                                                prm[:, P1_SINK:P1_SINK + C_HEADS], -1.0, None, ALU.mult)))
                    i = 0
                    for b in range(1, TB):
                        w = (b + 1) * P
                        for hd in range(IDX_HEADS):
                            dve.wait_ge(*read_of(jobs, ("index", b, hd)))
                            if hd == 0:
                                nc.vector.tensor_scalar(score[:, b - 1, 0:w], rel[:, i % 2, 0:w], iw[:, b, hd:hd + 1], None,
                                                        ALU.mult).then_inc(S["iscored"], 1)
                            else:
                                dve.wait_ge(S["iscored"], i)
                                nc.vector.scalar_tensor_tensor(score[:, b - 1, 0:w], rel[:, i % 2, 0:w],
                                                               iw[:, b, hd:hd + 1], score[:, b - 1, 0:w],
                                                               ALU.mult, ALU.add).then_inc(S["iscored"], 1)
                            i += 1
                        dve.wait_ge(S["iscored"], i)
                        m = own.up(nc.vector.tensor_tensor(score[:, b - 1, b * P:w], score[:, b - 1, b * P:w], causal, ALU.add))
                        if b == TB - 1:
                            dve.wait_ge(*m)

                    def topk():
                        for b in range(1, TB):
                            row = score[:, b - 1, 0:(b + 1) * P]
                            for _ in range(TOPK // 8):
                                m = own.up(nc.vector.max(out=small[:, 32:40], in_=row))
                                yield
                                dve.wait_ge(*m)
                                m = own.up(nc.vector.match_replace(out=row, in_to_replace=small[:, 32:40], in_values=row,
                                                                   imm_value=TAKEN))
                                yield
                                dve.wait_ge(*m)
                            m = own.up(nc.vector.tensor_scalar(row, row, TAKEN / 2, NEG, ALU.is_gt, ALU.mult))
                            dve.wait_ge(*m)
                            yield

                    picks = topk()
                    for s0, s1, s2, s3, s4 in steps():
                        if s0 is not None:
                            k = s0
                            br, hd, b = units[k]
                            w = unit_width(units[k])
                            if br == "A":
                                for _ in picks:
                                    pass
                            mn = small[:, k % 4:k % 4 + 1]
                            if k >= 4:
                                bk, m, _ = jobs.at["pt", k - 4, 1 if units[k - 4][0] == "B" else 0]
                                dve.wait_ge(full[bk], m)
                            bank = bank_filled(dve, jobs, ("logits", k, 0))
                            if br == "B":
                                mask, w0 = cst[:, C1_DIL + b * L:C1_DIL + (b + 1) * L], L
                            elif br == "C":
                                mask, w0 = cst[:, C1_WIN + 256 - w:C1_WIN + 256], w
                            else:
                                mask, w0 = (causal if b == 0 else score[:, b - 1, 0:w]), w
                            part = small[:, 20 + 2 * (k % 2):22 + 2 * (k % 2)]
                            first = mn if br == "A" else part[:, 0:1]
                            t = nc.vector.tensor_tensor_reduce(out=sc[:, k % 4, 0:w0], in0=ps[:, bank, 0:w0], in1=mask,
                                                               scale=-(HD ** -0.5), scalar=-NEG, op0=ALU.add, op1=ALU.min,
                                                               accum_out=first)
                            t.then_inc(read[bank], 1)
                            dve.wait_ge(*read_of(jobs, ("logits", k, 0)))
                            if br == "B":
                                bank = bank_filled(dve, jobs, ("logits", k, 1))
                                mask = cst[:, C1_DIL16:C1_DIL16 + 256]
                                nc.vector.tensor_tensor_reduce(out=sc[:, k % 4, L:L + 256], in0=ps[:, bank, 0:256],
                                                               in1=mask, scale=-(HD ** -0.5), scalar=-NEG, op0=ALU.add,
                                                               op1=ALU.min, accum_out=part[:, 1:2]).then_inc(read[bank], 1)
                                dve.wait_ge(*read_of(jobs, ("logits", k, 1)))
                                nc.vector.tensor_tensor(mn, part[:, 0:1], part[:, 1:2], ALU.min).then_inc(S["row_min"], 1)
                            elif br == "C":
                                nc.vector.tensor_tensor(mn, part[:, 0:1], prm[:, P1_NSINK + hd:P1_NSINK + hd + 1], ALU.min)\
                                  .then_inc(S["row_min"], 1)
                        if s4 is not None:
                            k = s4
                            br, hd, b = units[k]
                            bank = bank_filled(dve, jobs, ("o", k))
                            tile, cols = o_place(units[k])
                            dve.wait_ge(S["o_kept"], k + 1)
                            nc.vector.tensor_tensor(o_lo[half(hd), tile, cols], ps[half(hd), bank, 0:P],
                                                    o_hi[half(hd), tile, cols].bitcast(F32), ALU.subtract).then_inc(read[bank], 1)
                        if s1 is not None:
                            k = s1
                            den = small[:, 4 + k % 4:5 + k % 4]
                            dve.wait_ge(S["exped"], k + 1)
                            if units[k][0] == "C":
                                dve.wait_ge(*own.up(nc.vector.tensor_tensor(den, den, small[:, 16 + k % 4:17 + k % 4], ALU.add)))
                            nc.vector.reciprocal(small[:, 8 + k % 4:9 + k % 4], den).then_inc(S["den_ready"], 1)
                        next(picks, None)
                        next(picks, None)
            close_block()

            m_hi, m_lo = place("m_hi", 26568, DC, L, dt=F32R), place("m_lo", 30664, DC, L, dt=F32R)
            gate, gtmp = place("gate", 34760, 3, L), place("gtmp", 36296, 3, L)
            BR = {0: (0, 3), 1: (3, 2), 2: (5, 4)}
            jobs = Banks(start=1)
            jobs.plan_body([(w, q, j) for q in range(2) for w in ("gate", "branch") for j in range(3)], DC // 2)
            for n in range(DC):
                jobs.plan(("wo", n))
            jobs.plan("sum")
            N_C = N_MERGE + N_WO

            def merge_last(j):
                return ("gate", j // 2, 1) if j % 2 == 0 else ("branch", j // 2, 2)

            with nc.Block() as block:
                @block.sync
                def _(sy, jobs=jobs):
                    def fetch(k, j):
                        sy.dma_start(WC[0][:, j, :], d["w1"][bass.ds(layer, 1), bass.ds(k, 1)].rearrange("a b p c -> p (a b c)"))\
                          .then_inc(landed[j], 16)

                    come_ahead(sy)
                    with sy.Fori(1, N_C // 2) as it:
                        for j in range(2):
                            sy.wait_ge(S["w_lo"], it * 2 + (j - 1))
                            fetch(it * 2 + (S1_MERGE + j), j)
                    sy.wait_ge(S["w_lo"], N_C)
                    fetch_ahead(sy, WF[0], d["w1"], S1_UP, 2048)

                @block.tensor
                def _(pe, jobs=jobs):
                    for b in range(8):
                        pe.sem_inc(full[b], 1)
                        pe.sem_inc(read[b], 1)
                    with pe.Fori(0, DC // 2) as it:
                        for q in range(2):
                            for j in range(3):
                                if j != 1:
                                    pe.wait_ge(S["w_lo"], it * 4 + (2 * q + (j == 2) + 1))
                                w_hi, w_lo = (w[:, int(j == 2), (j % 2) * 1024:(j % 2) * 1024 + 1024]
                                              .rearrange("p (k c) -> p k c", c=P) for w in WC[1:])
                                b = bank_to_fill(pe, jobs, ("gate", q, j), it)
                                for c in range(DC):
                                    m = product3(ps[:, b, :], w_hi[:, c, :], w_lo[:, c, :], u_hi[:, c, :], u_lo[:, c, :],
                                                 c == 0, c == DC - 1)
                                m.then_inc(full[b], 1)
                            w_hi, w_lo = (w[:, 1, 1024:MERGE_B].rearrange("p (k c) -> p k c", c=P) for w in WC[1:])
                            for j in range(3):
                                t0, n = BR[j]
                                b = bank_to_fill(pe, jobs, ("branch", q, j), it)
                                for c in range(n):
                                    m = product3(ps[:, b, :], w_hi[:, t0 + c, :], w_lo[:, t0 + c, :], o_hi[:, t0 + c, :],
                                                 o_lo[:, t0 + c, :], c == 0, c == n - 1)
                                m.then_inc(full[b], 1)
                    for n in range(DC):
                        if n % 2 == 0:
                            pe.wait_ge(S["w_lo"], N_MERGE + n // 2 + 1)
                        dense_tile(pe, jobs, ("wo", n), WC, n // 2, n % 2, S["m_lo"] if n == 0 else None, x=(m_hi, m_lo), first=1)
                    norm_sum(pe, jobs, "sum", four)

                @block.scalar
                def _(act, jobs=jobs):
                    for k in range(2):
                        act.wait_ge(landed[k], 16)
                        split_w_hi(act, WC, k, k + 1, SLOT)
                    with act.Fori(0, DC // 2) as it:
                        for q in range(2):
                            act.wait_ge(S["gated"], it * 2 + (q + 1))
                            for j in range(3):
                                b = bank_filled(act, jobs, ("gate", q, j), it)
                                nc.scalar.activation(gate[:, j, :], ps[:, b, :], ACT.Sigmoid).then_inc(read[b], 1)
                                if j == 1:
                                    act.wait_ge(landed[0], it * 32 + 16 * (q + 2))
                                    split_w_hi(act, WC, 0, None, SLOT)
                            act.wait_ge(S["gated"], it * 2 + (q + 2))
                            nc.scalar.activation(m_hi[:, bass.ds(it * 2 + q, 1), :].rearrange("p a c -> p (a c)"), gtmp[:, 0, :],
                                                 ACT.Copy).then_inc(S["m_hi"], 1)
                            act.wait_ge(landed[1], it * 32 + 16 * (q + 2))
                            split_w_hi(act, WC, 1, None, SLOT)
                    for k in range(2, N_WO):
                        act.wait_ge(landed[k % 2], 16 * ((N_MERGE + k) // 2 + 1))
                        b, n, _ = jobs.at["wo", 2 * (k - 2) + 1]
                        act.wait_ge(full[b], n)
                        split_w_hi(act, WC, k, None, SLOT)
                    norm_squares(act, True, four)
                    norm_root(act, jobs, "sum", rstd)

                @block.vector
                def _(dve, jobs=jobs):
                    dve.sem_inc(S["gated"], 1)
                    dve.sem_inc(S["m_lo"], 1)
                    for k in range(2):
                        split_w_lo(dve, WC, k, k + 1, SLOT)
                    with dve.Fori(0, DC // 2) as it:
                        for q in range(2):
                            for j in range(3):
                                if j == 1:
                                    b, n, per = jobs.at["gate", q, 1]
                                    split_w_lo(dve, WC, 0, it * 4 + (2 * q + 3), SLOT)
                                dve.wait_ge(*read_of(jobs, ("gate", q, j), it))
                                b = bank_filled(dve, jobs, ("branch", q, j), it)
                                if j == 0:
                                    dve.wait_ge(S["m_lo"], it * 2 + (q + 1))
                                nc.vector.tensor_tensor(gtmp[:, j, :], ps[:, b, :], gate[:, j, :], ALU.mult).then_inc(read[b], 1)
                            for j in range(2):
                                dve.wait_ge(*read_of(jobs, ("branch", q, j), it))
                            nc.vector.tensor_tensor(gtmp[:, 0, :], gtmp[:, 0, :], gtmp[:, 1, :], ALU.add).then_inc(dve_own, 1)
                            dve.wait_ge(*read_of(jobs, ("branch", q, 2), it))
                            dve.wait_ge(dve_own, it * 2 + (q + 1))
                            nc.vector.tensor_tensor(gtmp[:, 0, :], gtmp[:, 0, :], gtmp[:, 2, :], ALU.add).then_inc(S["gated"], 1)
                            n = it * 2 + (q + 1)
                            dve.wait_ge(S["m_hi"], n)
                            t = bass.ds(it * 2 + q, 1)
                            nc.vector.tensor_tensor(m_lo[:, t, :].rearrange("p a c -> p (a c)"), gtmp[:, 0, :],
                                                    m_hi[:, t, :].rearrange("p a c -> p (a c)").bitcast(F32), ALU.subtract)\
                              .then_inc(S["m_lo"], 1)
                            split_w_lo(dve, WC, 1, it * 4 + (2 * q + 4), SLOT)
                    own = Signal(dve_own)
                    own.n = DC
                    for n in range(DC):
                        b = bank_filled(dve, jobs, ("wo", n))
                        nc.vector.tensor_tensor(h[:, n, :], h[:, n, :], ps[:, b, :], ALU.add).then_inc(read[b], 1)
                        dve.wait_ge(*read_of(jobs, ("wo", n)))
                        dve.sem_inc(S["h_ready"], 1)
                        if n in (1, 3):
                            split_w_lo(dve, WC, n // 2, N_MERGE + n // 2 + 3, SLOT)
                    norm_inverse(dve, jobs, "sum", own, 1, rstd)
            close_block()

            HF = FF1 // 2
            hid_hi, hid_lo = place("hid_hi", 17352, HF, L, dt=F32R), place("hid_lo", 25544, HF, L, dt=F32R)
            hid = place("hid", 33736, 2, L)
            NS = HF
            jobs = Banks(start=1)
            before = list(jobs.fills)
            jobs.plan_body([("up", t) for t in range(HF)] + [("down", n) for n in range(DC)], 2)
            per_half = [(jobs.fills[b] - before[b]) // 2 for b in range(8)]

            with nc.Block() as block:
                @block.sync
                def _(sy, jobs=jobs):
                    def fetch(k, j):
                        sy.dma_start(WF[0][:, j, :], d["w1"][bass.ds(layer, 1), bass.ds(k, 1), :, 0:2048]
                                     .rearrange("a b p c -> p (a b c)")).then_inc(landed[j], 16)

                    come_ahead(sy)
                    with sy.Fori(1, NS) as it:
                        for j in range(2):
                            sy.wait_ge(S["w_lo"], it * 2 + (j - 1))
                            fetch(it * 2 + (S1_UP + j), j)

                @block.tensor
                def _(pe, jobs=jobs):
                    for b in range(8):
                        pe.sem_inc(full[b], 1)
                        pe.sem_inc(read[b], 1)
                    pe.sem_inc(S["slab_used"], 1)
                    with pe.Fori(0, 2) as hf:
                        for t in range(HF):
                            if t % 2 == 0:
                                pe.wait_ge(S["w_lo"], hf * NS + (t // 2 + 1))
                            dense_tile(pe, jobs, ("up", t), WF, t // 2, t % 2, S["u_lo"] if t == 0 else None, it=hf)
                        for k in range(HF // 2):
                            pe.wait_ge(S["w_lo"], hf * NS + (HF // 2 + k + 1))
                            w_hi, w_lo = (w[:, k % 2, :].rearrange("p (k c) -> p k c", c=D) for w in WF[1:])
                            for c in range(2):
                                t = 2 * k + c
                                pe.wait_ge(S["hidden_kept"], hf * HF + (t + 1))
                                for n in range(DC):
                                    b = jobs.at["down", n][0]
                                    if t == 0:
                                        bank_to_fill(pe, jobs, ("down", n), hf)
                                    f = slice(n * P, (n + 1) * P)
                                    m = product3(ps[:, b, :], w_hi[:, c, f], w_lo[:, c, f], hid_hi[:, t, :], hid_lo[:, t, :],
                                                 t == 0, t == HF - 1)
                                    if t == HF - 1:
                                        m.then_inc(full[b], 1)
                            if k < HF // 2 - 1:
                                m.then_inc(S["slab_used"], 1)

                def slab_done(eng, jobs, k, hf):
                    if k == -2:
                        eng.wait_ge(S["slab_used"], hf * (HF // 2 - 1) + 1)
                    elif k == -1:
                        for b in range(8):
                            eng.wait_ge(full[b], hf * per_half[b] + before[b])
                    elif k < HF // 2:
                        b, n, per = jobs.at["up", 2 * k + 1]
                        eng.wait_ge(full[b], hf * per + n)
                    else:
                        eng.wait_ge(S["slab_used"], hf * (HF // 2 - 1) + (k - HF // 2 + 2))

                @block.scalar
                def _(act, jobs=jobs):
                    for hf in range(2):
                        def split(k):
                            if k < NS:
                                act.wait_ge(landed[k % 2], hf * (8 * NS) + 16 * (k // 2 + 1))
                                slab_done(act, jobs, k - 2, hf)
                                split_w_hi(act, WF, k, None)

                        split(0)
                        if hf == 0:
                            split_u_hi(act, four)
                        split(1)
                        for t in range(HF):
                            b = bank_filled(act, jobs, ("up", t), hf)
                            act.wait_ge(S["hid_sq"], hf * HF + (t + 1))
                            nc.scalar.activation(hid[:, t % 2, :], ps[:, b, :], ACT.Relu).then_inc(read[b], 1)
                            act.wait_ge(S["relu_kept"], hf * HF + (t + 1))
                            nc.scalar.activation(hid_hi[:, t, :], hid[:, t % 2, :], ACT.Copy).then_inc(S["m_hi"], 1)
                            if t % 2 == 1:
                                split(t // 2 + 2)
                        for k in range(HF // 2 + 2, NS):
                            split(k)

                @block.gpsimd
                def _(pool):
                    with pool.Fori(0, 2) as hf:
                        for k in range(NS):
                            pool.wait_ge(S["w_hi"], hf * NS + (k + 1))
                            nc.gpsimd.tensor_tensor(WF[2][:, k % 2, :], WF[0][:, k % 2, :], WF[1][:, k % 2, :].bitcast(F32),
                                                    ALU.subtract).then_inc(S["w_lo"], 1)

                @block.vector
                def _(dve, jobs=jobs):
                    dve.sem_inc(S["hid_sq"], 2)
                    norm_apply(dve, P1_MLP, rstd, four, lo=True)
                    with dve.Fori(0, 2) as hf:
                        for t in range(HF):
                            dve.wait_ge(*read_of(jobs, ("up", t), hf))
                            x = hid[:, t % 2, :]
                            nc.vector.tensor_tensor(x, x, x, ALU.mult).then_inc(S["relu_kept"], 1)
                            dve.wait_ge(S["m_hi"], hf * HF + (t + 1))
                            nc.vector.tensor_tensor(hid_lo[:, t, :], x, hid_hi[:, t, :].bitcast(F32), ALU.subtract)\
                              .then_inc(S["hidden_kept"], 1)
                            dve.wait_ge(S["hidden_kept"], hf * HF + (t + 1))
                            dve.sem_inc(S["hid_sq"], 1)
                        for n in range(DC):
                            b = bank_filled(dve, jobs, ("down", n), hf)
                            nc.vector.tensor_tensor(h[:, n, :], h[:, n, :], ps[:, b, :], ALU.add).then_inc(read[b], 1)
            close_block()

        jobs = Banks()
        jobs.plan("sum")
        with nc.Block() as block:
            @block.sync
            def _(sy):
                for c in (slice(0, C1_ID), slice(C2_CAUSAL, N_C2)):
                    sy.dma_start(cst[:, c], d["cst2"][:, c]).then_inc(loaded, 16)
                sy.wait_ge(loaded, 32)

            @block.tensor
            def _(pe):
                norm_sum(pe, jobs, "sum", four)

            @block.scalar
            def _(act):
                norm_squares(act, False, four)
                norm_root(act, jobs, "sum", rstd)

            @block.vector
            def _(dve):
                norm_inverse(dve, jobs, "sum", Signal(dve_own), 1, rstd)
                norm_apply(dve, P1_FINAL, rstd, None, dst=h)
        close_block()

        IN2 = ROOM - 12288
        sbqk, sbv = place("sbqk", IN2, 4, L), place("sbv", IN2 + 2048, TB, SB_HEADS * HD)
        cq = place("cq", IN2 + 3072, 2, L)
        ckv = place("ckv", IN2 + 4096, L)[:, :]
        krs = place("krs", IN2 + 4608, L)[:, :]
        rw_in = place("rw_in", IN2 + 5120, 14, L)
        rr, rk, rv = (rw_in[:, PAIRS * i:PAIRS * (i + 1), :] for i in range(3))
        wdad, gd = rw_in[:, 12, :], rw_in[:, 13, :]
        mla_w = place("mla_w", IN2 - 2048, 2048)
        o2_hi, o2_lo = u_hi, u_lo
        WP = weight_room("p", 17352, 3)
        mq, mk = place("mq", 17352, MLA_HEADS, L), place("mk", 19400, MLA_HEADS, L)
        mv = place("mv", 21448, TB, MLA_HEADS * HD)
        sc2 = place("sc2", 22472, 4, L)
        pt2 = place("pt2", 24520, 2, L)
        msq = place("msq", 25544, 3, L)
        mrs = place("mrs", 27080, 2, L)
        diag2 = place("diag2", 33224, 4, P)
        lora = place("lora", 37832, 1024)[:, :]
        alpha, beta = place("alpha", 33736, PAIRS, L)[:, :, :], place("beta", 35784, PAIRS, L)[:, :, :]
        since = place("since", 11208, PAIRS, L)[:, :, :]
        before = place("before", 15304, PAIRS, L)[:, :, :]
        RW_W, RW_A, RW_KK, RW_P, RW_SCAN = 0, 1, 2, 3, 3 + PAIRS
        ZO = [0, 512, 896, 1152, 1280]
        zs = [place(f"zs{i}", 28104 + 1280 * i, 1280)[:, :] for i in range(2)]
        sp = [place(f"sp{i}", 30664 + 1280 * i, 1280)[:, :] for i in range(2)]

        def prm_col(c):
            return prm[:, c:c + 1]

        with nc.Fori(0, DEPTH) as layer:
            jobs = Banks()
            for t in range(N_T2):
                jobs.plan(("t", t))
            for tb in range(TB):
                jobs.plan(("v", tb))

            with nc.Block() as block:
                @block.sync
                def _(sy, jobs=jobs):
                    sy.dma_start(prm[:, 0:N_P2], d["prm2"][bass.ds(layer, 1)].rearrange("a p c -> p (a c)"))\
                      .then_inc(loaded, 16)
                    for k in range(S2_MLA):
                        if k >= 3:
                            sy.wait_ge(S["w_lo"], k - 2)
                        sy.dma_start(WP[0][:, k % 3, :],
                                     d["w2"][bass.ds(layer, 1), k, :, 0:2048].rearrange("a p c -> p (a c)"))\
                          .then_inc(landed[k % 3], 16)
                    sy.dma_start(mla_w[:, :], d["w2"][bass.ds(layer, 1), S2_MLA, :, 0:2048].rearrange("a p c -> p (a c)"))\
                      .then_inc(landed[3], 16)
                    sy.wait_ge(landed[3], 16)

                @block.tensor
                def _(pe, jobs=jobs):
                    for t in range(N_T2):
                        k = t // 2
                        if t % 2 == 0:
                            pe.wait_ge(S["w_lo"], k + 1)
                        dense_tile(pe, jobs, ("t", t), WP, k, t % 2, S["u_lo"] if t == 0 else None)
                    k = S2_V
                    pe.wait_ge(S["w_lo"], k + 1)
                    w_hi, w_lo = (w[:, k % 2, :].rearrange("p (k c) -> p k c", c=256) for w in WP[1:])
                    for tb in range(TB):
                        b = bank_to_fill(pe, jobs, ("v", tb))
                        for c in range(DC):
                            tok = slice(tb * P, (tb + 1) * P)
                            m = product3(ps[:, b, 0:256], u_hi[:, c, tok], u_lo[:, c, tok], w_hi[:, c, :], w_lo[:, c, :],
                                         c == 0, c == DC - 1)
                        m.then_inc(full[b], 1)

                @block.scalar
                def _(act, jobs=jobs):
                    def split(k):
                        if k < S2_MLA:
                            act.wait_ge(landed[k % 3], 16 * (k // 3 + 1))
                            if k >= 2:
                                b, n, _ = jobs.at["t", 2 * (k - 2) + 1]
                                act.wait_ge(full[b], n)
                            split_w_hi(act, WP, k, None)

                    for c in range(DC):
                        nc.scalar.activation(u_hi[:, c, :], h[:, c, :], ACT.Copy).then_inc(S["u_hi"], 1)
                        if c in (0, 3):
                            split(int(c == 3))
                    act.wait_ge(S["prm_ready"], 1)
                    for t in range(N_T2):
                        b = bank_filled(act, jobs, ("t", t))
                        if t < T2_RW:
                            dst = [sbqk[:, 0, :], sbqk[:, 1, :], sbqk[:, 2, :], sbqk[:, 3, :], cq[:, 0, :], cq[:, 1, :],
                                   ckv, krs][t]
                            nc.scalar.activation(dst, ps[:, b, :], ACT.Copy).then_inc(read[b], 1)
                        else:
                            i = t - T2_RW
                            nc.scalar.activation(rw_in[:, i, :], ps[:, b, :], ACT.Copy, scale=prm_col(P2_OMU + i))\
                              .then_inc(S["mixed"], 1)
                        if t % 2 == 1:
                            split(t // 2 + 2)
                    for tb in range(TB):
                        b = bank_filled(act, jobs, ("v", tb))
                        nc.scalar.activation(sbv[:, tb, :], ps[:, b, 0:256], ACT.Copy).then_inc(read[b], 1)

                @block.gpsimd
                def _(pool):
                    for c in range(DC):
                        pool.wait_ge(S["u_hi"], c + 1)
                        nc.gpsimd.tensor_tensor(u_lo[:, c, :], h[:, c, :], u_hi[:, c, :].bitcast(F32), ALU.subtract)\
                          .then_inc(S["u_lo"], 1)

                @block.vector
                def _(dve, jobs=jobs):
                    split_w_lo(dve, WP, 0, 1)
                    split_w_lo(dve, WP, 1, 2)
                    dve.wait_ge(loaded, 16)
                    nc.vector.tensor_scalar(prm[:, P2_OMU:P2_OMU + 14], prm[:, P2_MU:P2_MU + 14], -1.0, 1.0,
                                            ALU.mult, ALU.add).then_inc(S["prm_ready"], 1)
                    for k in range(2, T2_RW // 2 + 2):
                        split_w_lo(dve, WP, k, k + 1)
                    for t in range(T2_RW, N_T2):
                        i = t - T2_RW
                        b = bank_filled(dve, jobs, ("t", t))
                        dve.wait_ge(S["mixed"], i + 1)
                        nc.vector.scalar_tensor_tensor(rw_in[:, i, 1:L], ps[:, b, 0:L - 1], prm_col(P2_MU + i),
                                                       rw_in[:, i, 1:L], ALU.mult, ALU.add).then_inc(read[b], 1)
                        k = t // 2 + 2
                        if t % 2 == 1 and k < S2_MLA:
                            split_w_lo(dve, WP, k, k + 1)
            close_block()

            mla = [(hd, b) for b in range(TB) for hd in range(MLA_HEADS)]
            NM = len(mla)

            def steps2():
                for k in range(NM + 5):
                    m = [k - lag if 0 <= k - lag < NM else None for lag in (0, 1, 3, 4, 5)]
                    s = [(k - at) // 4 if (k - at) % 4 == 0 and 0 <= (k - at) // 4 < SB_HEADS else None
                         for at in (0, 1, 3, 4, 5, 6)]
                    yield m, s

            jobs = Banks()
            for name in ("cq_sum", "ckv_sum"):
                jobs.plan(name)
            for hd in range(MLA_HEADS):
                for name in ("qs", "q", "k"):
                    jobs.plan((name, hd))
            for tb in range(TB):
                jobs.plan(("mv", tb))
            for k0, (m, s) in enumerate(steps2()):
                if s[0] is not None:
                    for c in range(TB):
                        jobs.plan(("z", s[0], c))
                if s[2] is not None:
                    for c in range(TB):
                        jobs.plan(("later", s[2], c))
                if s[4] is not None:
                    jobs.plan(("sb", s[4]))
                if m[0] is not None:
                    jobs.plan(("logits", m[0]))
                if m[2] is not None:
                    jobs.plan(("pt", m[2]))
                if m[3] is not None:
                    jobs.plan(("o", m[3]))
                for name, at in (("w", RW_W), ("a", RW_A), ("kk", RW_KK)):
                    if k0 == at:
                        for p in range(PAIRS):
                            jobs.plan((name, p))

            def rw_pe(pe, jobs, step):
                if step == RW_W:
                    pe.wait_ge(loaded, 16)
                    pe.wait_ge(S["lora_in"], 1)
                for name, rows, at in (("w", slice(0, 64), RW_W), ("a", slice(64, 128), RW_A)):
                    if step == at:
                        for p in range(PAIRS):
                            b = bank_to_fill(pe, jobs, (name, p))
                            nc.tensor.matmul(ps[:, b, :], lora[rows, p * P:(p + 1) * P], wdad[rows, :], start=True, stop=True)\
                              .then_inc(full[b], 1)
                if step == RW_KK:
                    for p in range(PAIRS):
                        b = bank_to_fill(pe, jobs, ("kk", p))
                        pe.wait_ge(S["kk_sq"], p + 1)
                        nc.tensor.matmul(ps[:, b, :], blk, alpha[:, p, :], start=True, stop=True).then_inc(full[b], 1)

            def rw_act(act, jobs, step):
                for name, at, dst, bias in (("w", RW_W, before, P2_W0), ("a", RW_A, since, P2_A0)):
                    if step == at:
                        for p in range(PAIRS):
                            b = bank_filled(act, jobs, (name, p))
                            nc.scalar.activation(dst[:, p, :], ps[:, b, :], ACT.Sigmoid, bias=prm_col(bias + p))\
                              .then_inc(read[b], 1)
                if step == RW_A:
                    for p in range(PAIRS):
                        nc.scalar.activation(alpha[:, p, :], rk[:, p, :], ACT.Square, scale=prm_col(P2_KK + p))\
                          .then_inc(S["kk_sq"], 1)
                if step == RW_KK:
                    for p in range(PAIRS):
                        act.wait_ge(*read_of(jobs, ("kk", p)))
                        nc.scalar.activation(alpha[:, p, :], alpha[:, p, :], ACT.Sqrt).then_inc(S["kk_root"], 1)

            def rw_dve(dve, jobs, step, own):
                chain = lambda i: dve.wait_ge(*own.up(i))
                if step == RW_KK:
                    for p in range(PAIRS):
                        b = bank_filled(dve, jobs, ("kk", p))
                        nc.vector.tensor_scalar(alpha[:, p, :], ps[:, b, :], 1e-12, None, ALU.max).then_inc(read[b], 1)
                p = step - RW_P
                if 0 <= p < PAIRS:
                    x, a = alpha[:, p, :], since[:, p, :]
                    dve.wait_ge(S["kk_root"], p + 1)
                    dve.wait_ge(*read_of(jobs, ("a", p)))
                    chain(nc.vector.reciprocal(x, x))
                    chain(nc.vector.scalar_tensor_tensor(x, rk[:, p, :], prm_col(P2_KK + p), x, ALU.mult, ALU.mult))
                    chain(nc.vector.tensor_tensor(beta[:, p, :], x, a, ALU.mult))
                    chain(nc.vector.tensor_scalar(a, a, 1.0, prm_col(P2_KA + p), ALU.subtract, ALU.mult))
                    chain(nc.vector.scalar_tensor_tensor(rk[:, p, :], a, 1.0, rk[:, p, :], ALU.add, ALU.mult))
                p = step - RW_SCAN
                if 0 <= p < PAIRS:
                    dve.wait_ge(*read_of(jobs, ("w", p)))
                    chain(nc.vector.tensor_tensor_scan(since[:, p, :], cst[:, C2_RESET:C2_RESET + L], before[:, p, :], 0.0,
                                                       ALU.mult, ALU.add))
                    own.up(nc.vector.tensor_tensor(before[:, p, :], since[:, p, :], before[:, p, :], ALU.subtract))

            with nc.Block() as block:
                @block.sync
                def _(sy):
                    sy.dma_start(lora, d["w2"][bass.ds(layer, 1), S2_LORA, :, 0:1024].rearrange("a p c -> p (a c)"))\
                      .then_inc(loaded, 16)
                    sy.wait_ge(loaded, 16)

                @block.tensor
                def _(pe, jobs=jobs):
                    uq = mla_w[:, 0:1536].rearrange("p (k c) -> p k c", k=2)
                    ukv = mla_w[:, 1536:2048]
                    b = bank_to_fill(pe, jobs, "cq_sum")
                    pe.wait_ge(S["mla_squared"], 3)
                    nc.tensor.matmul(ps[:, b, :], ones, msq[:, 0, :], start=True, stop=False)
                    nc.tensor.matmul(ps[:, b, :], ones[0:64, :], msq[0:64, 1, :], start=False, stop=True).then_inc(full[b], 1)
                    b = bank_to_fill(pe, jobs, "ckv_sum")
                    nc.tensor.matmul(ps[:, b, :], ones, msq[:, 2, :], start=True, stop=True).then_inc(full[b], 1)
                    pe.wait_ge(S["mla_normed"], 3)
                    for hd in range(MLA_HEADS):
                        for name, c0 in (("qs", 384), ("q", 0)):
                            b = bank_to_fill(pe, jobs, (name, hd))
                            cols = slice(c0 + QW * hd, c0 + QW * hd + QW)
                            nc.tensor.matmul(ps[0:QW, b, :], uq[:, 0, cols], cq[:, 0, :], start=True, stop=False)
                            nc.tensor.matmul(ps[0:QW, b, :], uq[0:64, 1, cols], cq[0:64, 1, :], start=False, stop=True)\
                              .then_inc(full[b], 1)
                        b = bank_to_fill(pe, jobs, ("k", hd))
                        nc.tensor.matmul(ps[0:HD, b, :], ukv[:, HD * hd:HD * hd + HD], ckv, start=True, stop=True)\
                          .then_inc(full[b], 1)
                    for tb in range(TB):
                        b = bank_to_fill(pe, jobs, ("mv", tb))
                        nc.tensor.matmul(ps[:, b, 0:256], ckv[:, tb * P:(tb + 1) * P], ukv[:, 256:512], start=True, stop=True)\
                          .then_inc(full[b], 1)
                    for k0, (m, s) in enumerate(steps2()):
                        if s[0] is not None:
                            hd = s[0]
                            for c in range(TB):
                                b = bank_to_fill(pe, jobs, ("z", hd, c))
                                nc.tensor.matmul(ps[:, b, 0:L - c * P], sbqk[half(hd), 2 + hd // 2, c * P:(c + 1) * P],
                                                 sbqk[half(hd), hd // 2, c * P:L], start=True, stop=True).then_inc(full[b], 1)
                        if s[2] is not None:
                            hd = s[2]
                            pe.wait_ge(S["sb_masked"], hd + 1)
                            x = sp[hd % 2]
                            for c in range(TB):
                                b = bank_to_fill(pe, jobs, ("later", hd, c))
                                for c2 in range(c, TB):
                                    i = nc.tensor.matmul(ps[:, b, (c2 - c) * P:L - c * P],
                                                         cst[:, C2_TRI:C2_TRI + P] if c2 == c else ones,
                                                         x[:, ZO[c2]:ZO[c2 + 1]], start=(c2 == c), stop=(c2 == TB - 1),
                                                         skip_group_check=True)
                                i.then_inc(full[b], 1)
                        if s[4] is not None:
                            hd = s[4]
                            pe.wait_ge(S["sb_weight"], hd + 1)
                            b = bank_to_fill(pe, jobs, ("sb", hd))
                            for c in range(TB):
                                i = nc.tensor.matmul(ps[half(hd), b, c * P:L], sbv[:, c, hd * HD:(hd + 1) * HD],
                                                     zs[hd % 2][:, ZO[c]:ZO[c + 1]], start=(c == 0), stop=(c == TB - 1),
                                                     skip_group_check=True)
                            i.then_inc(full[b], 1)
                        if m[0] is not None:
                            k = m[0]
                            hd, tb = mla[k]
                            if k == 0:
                                pe.wait_ge(S["q_ready"], MLA_HEADS)
                                pe.wait_ge(S["k_ready"], MLA_HEADS)
                                for q in range(MLA_HEADS):
                                    pe.wait_ge(*read_of(jobs, ("k", q)))
                            b = bank_to_fill(pe, jobs, ("logits", k))
                            nc.tensor.matmul(ps[:, b, 0:(tb + 1) * P], mq[0:QW, hd, tb * P:(tb + 1) * P],
                                             mk[0:QW, hd, 0:(tb + 1) * P], start=True, stop=True).then_inc(full[b], 1)
                        if m[2] is not None:
                            k = m[2]
                            hd, tb = mla[k]
                            pe.wait_ge(S["scaled"], k + 1)
                            b = bank_to_fill(pe, jobs, ("pt", k))
                            for c in range(tb + 1):
                                i = nc.tensor.matmul(ps[:, b, c * P:(c + 1) * P], sc2[:, k % 4, c * P:(c + 1) * P],
                                                     diag2[:, k % 4, :], start=(c == 0), stop=(c == tb), skip_group_check=True)
                            i.then_inc(full[b], 1)
                        if m[3] is not None:
                            k = m[3]
                            hd, tb = mla[k]
                            pe.wait_ge(*read_of(jobs, ("pt", k)))
                            if k == 0:
                                for q in range(TB):
                                    pe.wait_ge(*read_of(jobs, ("mv", q)))
                            b = bank_to_fill(pe, jobs, ("o", k))
                            for c in range(tb + 1):
                                i = nc.tensor.matmul(ps[half(hd), b, 0:P], mv[:, c, hd * HD:(hd + 1) * HD],
                                                     pt2[:, k % 2, c * P:(c + 1) * P], start=(c == 0), stop=(c == tb))
                            i.then_inc(full[b], 1)
                        rw_pe(pe, jobs, k0)

                @block.scalar
                def _(act, jobs=jobs):
                    nc.scalar.activation(gd, gd, ACT.Sigmoid)
                    nc.scalar.activation(wdad[0:64, :], wdad[0:64, :], ACT.Tanh).then_inc(S["lora_in"], 1)
                    nc.scalar.activation(msq[:, 0, :], cq[:, 0, :], ACT.Square).then_inc(S["mla_squared"], 1)
                    nc.scalar.activation(msq[0:64, 1, :], cq[0:64, 1, :], ACT.Square).then_inc(S["mla_squared"], 1)
                    nc.scalar.activation(msq[:, 2, :], ckv, ACT.Square).then_inc(S["mla_squared"], 1)
                    for i, name in enumerate(("cq_sum", "ckv_sum")):
                        act.wait_ge(*read_of(jobs, name))
                        nc.scalar.activation(mrs[:, i, :], mrs[:, i, :], ACT.Sqrt).then_inc(S["root"], 1)
                    for hd in range(MLA_HEADS):
                        b = bank_filled(act, jobs, ("q", hd))
                        nc.scalar.activation(mq[0:QW, hd, :], ps[0:QW, b, :], ACT.Copy).then_inc(read[b], 1)
                        b = bank_filled(act, jobs, ("k", hd))
                        nc.scalar.activation(mk[0:HD, hd, :], ps[0:HD, b, :], ACT.Copy).then_inc(read[b], 1)
                    for tb in range(TB):
                        b = bank_filled(act, jobs, ("mv", tb))
                        nc.scalar.activation(mv[:, tb, :], ps[:, b, 0:256], ACT.Copy).then_inc(read[b], 1)
                    own = Signal(act_own)
                    for k0, (m, s) in enumerate(steps2()):
                        if m[1] is not None:
                            k = m[1]
                            w = (mla[k][1] + 1) * P
                            act.wait_ge(*read_of(jobs, ("logits", k)))
                            nc.scalar.activation(sc2[:, k % 4, 0:w], sc2[:, k % 4, 0:w], ACT.Exp, bias=small[:, k % 4:k % 4 + 1],
                                                 scale=-1.0, accum_out=small[:, 4 + k % 4:5 + k % 4]).then_inc(S["exped"], 1)
                        if s[0] is not None:
                            hd = s[0]
                            for c in range(TB):
                                act.wait_ge(*read_of(jobs, ("z", hd, c)))
                            x = sp[hd % 2]
                            act.wait_ge(*own.up(nc.scalar.activation(x, zs[hd % 2], ACT.Abs)))
                            act.wait_ge(*own.up(nc.scalar.activation(x, x, ACT.Exp, scale=-1.0)))
                            nc.scalar.activation(x, x, ACT.Ln, bias=1.0).then_inc(S["sb_abs"], 1)
                        if s[3] is not None:
                            hd = s[3]
                            act.wait_ge(S["sb_arg"], hd + 1)
                            nc.scalar.activation(zs[hd % 2], zs[hd % 2], ACT.Exp).then_inc(S["sb_weight"], 1)
                        if s[5] is not None:
                            hd = s[5]
                            b = bank_filled(act, jobs, ("sb", hd))
                            nc.scalar.activation(o2_hi[half(hd), hd // 2, :], ps[half(hd), b, :], ACT.Copy)\
                              .then_inc(S["o_kept"], 1)
                        if m[4] is not None:
                            k = m[4]
                            hd, tb = mla[k]
                            b = bank_filled(act, jobs, ("o", k))
                            nc.scalar.activation(o2_hi[half(hd), 2 + hd // 2, tb * P:(tb + 1) * P], ps[half(hd), b, 0:P],
                                                 ACT.Copy).then_inc(S["o_kept"], 1)
                        if m[2] is not None:
                            k = m[2]
                            w = (mla[k][1] + 1) * P
                            b = bank_filled(act, jobs, ("pt", k))
                            if k >= 2:
                                b2, n2, _ = jobs.at["o", k - 2]
                                act.wait_ge(full[b2], n2)
                            nc.scalar.activation(pt2[:, k % 2, 0:w], ps[:, b, 0:w], ACT.Copy).then_inc(read[b], 1)
                        rw_act(act, jobs, k0)

                @block.gpsimd
                def _(pool, jobs=jobs):
                    pool.wait_ge(S["kr_ready"], 1)
                    for hd in range(MLA_HEADS):
                        nc.gpsimd.tensor_copy(mk[64:96, hd, :], cq[64:96, 1, :]).then_inc(S["k_ready"], 1)
                    for k0, (m, s) in enumerate(steps2()):
                        if m[1] is not None:
                            k = m[1]
                            pool.wait_ge(S["den_ready"], k + 1)
                            if k >= 4:
                                b, n, _ = jobs.at["pt", k - 4]
                                pool.wait_ge(full[b], n)
                            nc.gpsimd.tensor_scalar(diag2[:, k % 4, :], ident, small[:, 8 + k % 4:9 + k % 4], None,
                                                    ALU.mult).then_inc(S["scaled"], 1)
                        if s[1] is not None:
                            hd = s[1]
                            pool.wait_ge(S["sb_soft"], hd + 1)
                            for c in range(TB):
                                x = sp[hd % 2][:, ZO[c]:ZO[c] + P]
                                i = nc.gpsimd.tensor_tensor(x, x, cst[:, C2_SBKEEP:C2_SBKEEP + P], ALU.mult)
                            i.then_inc(S["sb_masked"], 1)
                        if s[2] is not None:
                            hd = s[2]
                            for c in range(TB):
                                pool.wait_ge(*read_of(jobs, ("later", hd, c)))
                                x = zs[hd % 2][:, ZO[c]:ZO[c] + P]
                                i = nc.gpsimd.tensor_tensor(x, x, cst[:, C2_SBNEG:C2_SBNEG + P], ALU.add)
                            i.then_inc(S["sb_arg"], 1)

                @block.vector
                def _(dve, jobs=jobs):
                    own = Signal(dve_own)
                    outs = 0
                    cs = cst[64:96, C2_COS:C2_COS + L]
                    sn = cst[64:96, C2_SIN:C2_SIN + L]
                    for i, (name, n) in enumerate((("cq_sum", Q_LORA), ("ckv_sum", P))):
                        b = bank_filled(dve, jobs, name)
                        nc.vector.tensor_scalar(mrs[:, i, :], ps[:, b, :], 1.0 / n, 1e-6, ALU.mult, ALU.add).then_inc(read[b], 1)
                    dve.wait_ge(S["root"], 2)
                    dve.wait_ge(*own.up(nc.vector.reciprocal(mrs[:, :, :], mrs[:, :, :])))
                    for x, g, i in ((cq[:, 0, :], P2_QN, 0), (cq[0:64, 1, :], P2_QN + 1, 0), (ckv, P2_KVN, 1)):
                        n = x.shape[0]
                        nc.vector.scalar_tensor_tensor(x, x, prm[0:n, g:g + 1], mrs[0:n, i, :], ALU.mult, ALU.mult)\
                          .then_inc(S["mla_normed"], 1)
                    kr = cq[64:96, 1, :]
                    own.up(nc.vector.tensor_tensor(kr, kr, cs, ALU.mult))
                    dve.wait_ge(*own.up(nc.vector.tensor_tensor(krs[64:96, :], krs[64:96, :], sn, ALU.mult)))
                    nc.vector.tensor_tensor(kr, kr, krs[64:96, :], ALU.add).then_inc(S["kr_ready"], 1)
                    for hd in range(MLA_HEADS):
                        b = bank_filled(dve, jobs, ("qs", hd))
                        tmp = msq[64:96, hd % 2, :]
                        if hd == 0:
                            dve.wait_ge(S["mla_normed"], 3)
                        if hd >= 2:
                            dve.wait_ge(S["q_ready"], hd - 1)
                        nc.vector.tensor_tensor(tmp, ps[64:96, b, :], sn, ALU.mult).then_inc(read[b], 1)
                        dve.wait_ge(*read_of(jobs, ("q", hd)))
                        x = mq[64:96, hd, :]
                        dve.wait_ge(*own.up(nc.vector.tensor_tensor(x, x, cs, ALU.mult)))
                        dve.wait_ge(*read_of(jobs, ("qs", hd)))
                        nc.vector.tensor_tensor(x, x, tmp, ALU.add).then_inc(S["q_ready"], 1)
                    for k0, (m, s) in enumerate(steps2()):
                        if s[0] is not None:
                            hd = s[0]
                            if hd >= 2:
                                b, n, _ = jobs.at["sb", hd - 2]
                                dve.wait_ge(full[b], n)
                            for c in range(TB):
                                b = bank_filled(dve, jobs, ("z", hd, c))
                                nc.vector.tensor_scalar(zs[hd % 2][:, ZO[c]:ZO[c + 1]], ps[:, b, 0:L - c * P], HD ** -0.5, None,
                                                        ALU.mult).then_inc(read[b], 1)
                        if m[0] is not None:
                            k = m[0]
                            w = (mla[k][1] + 1) * P
                            if k >= 4:
                                b, n, _ = jobs.at["pt", k - 4]
                                dve.wait_ge(full[b], n)
                            b = bank_filled(dve, jobs, ("logits", k))
                            nc.vector.tensor_tensor_reduce(out=sc2[:, k % 4, 0:w], in0=ps[:, b, 0:w],
                                                           in1=cst[:, C2_CAUSAL + L - w:C2_CAUSAL + L],
                                                           scale=-(QW ** -0.5), scalar=-NEG, op0=ALU.add, op1=ALU.min,
                                                           accum_out=small[:, k % 4:k % 4 + 1]).then_inc(read[b], 1)
                        if s[1] is not None:
                            hd = s[1]
                            dve.wait_ge(S["sb_abs"], hd + 1)
                            nc.vector.scalar_tensor_tensor(sp[hd % 2], zs[hd % 2], 0.0, sp[hd % 2], ALU.max, ALU.add)\
                              .then_inc(S["sb_soft"], 1)
                        if s[2] is not None:
                            hd = s[2]
                            for c in range(TB):
                                b = bank_filled(dve, jobs, ("later", hd, c))
                                x = zs[hd % 2][:, ZO[c]:ZO[c + 1]]
                                nc.vector.tensor_tensor(x, x, ps[:, b, 0:L - c * P], ALU.subtract).then_inc(read[b], 1)
                        if m[1] is not None:
                            k = m[1]
                            dve.wait_ge(S["exped"], k + 1)
                            nc.vector.reciprocal(small[:, 8 + k % 4:9 + k % 4], small[:, 4 + k % 4:5 + k % 4])\
                              .then_inc(S["den_ready"], 1)
                        if s[5] is not None:
                            hd = s[5]
                            outs += 1
                            dve.wait_ge(S["o_kept"], outs)
                            b = bank_filled(dve, jobs, ("sb", hd))
                            nc.vector.tensor_tensor(o2_lo[half(hd), hd // 2, :], ps[half(hd), b, :],
                                                    o2_hi[half(hd), hd // 2, :].bitcast(F32), ALU.subtract).then_inc(read[b], 1)
                        if m[4] is not None:
                            k = m[4]
                            hd, tb = mla[k]
                            outs += 1
                            dve.wait_ge(S["o_kept"], outs)
                            b = bank_filled(dve, jobs, ("o", k))
                            x = (half(hd), 2 + hd // 2, slice(tb * P, (tb + 1) * P))
                            nc.vector.tensor_tensor(o2_lo[x], ps[half(hd), b, 0:P], o2_hi[x].bitcast(F32), ALU.subtract)\
                              .then_inc(read[b], 1)
                        rw_dve(dve, jobs, k0, own)
            close_block()

            y, bonus = place("y", 11208, PAIRS, L), place("bonus", 15304, PAIRS, L)
            w2t, w3t, w1t, w4t = (place(f"w{i}t", 25544 + 2048 * n, PAIRS, L)[:, :, :] for n, i in enumerate((2, 3, 1, 4)))
            both = lambda name, at0, at1, *shape: [place(f"{name}{i}", at, *shape) for i, at in enumerate((at0, at1))]
            xs = both("xs", IN2, 25544, PAIRS, 2 * P)
            x3 = both("x3", IN2 + 1024, 26568, 3, PAIRS * P)
            xt = both("xt", IN2 + 2560, 28104, PAIRS, 3 * P)
            m4 = both("m4", 29640, 31688, PAIRS, 4 * P)
            inv = [x[:, :] for x in both("inv", 39880, 38856, L)]
            rbuf, state, xbuf = (place(n, at, L)[:, :] for n, at in (("rbuf", 39368), ("state", IN2 + 4096), ("xbuf", IN2 + 4608)))
            dend = place("dend", 8840, PAIRS, NCH)[:, :, :]
            rs = place("rs", 17352, 16 * 512)[:, :]
            names = ("nd0", "no0", "ndt0", "q10", "nd1", "no1", "ndt1", "q11", "p2", "ip2", "p2t", "ip4", "wt", "et", "e", "mt")
            tmp = {n: rs[:, 512 * i:512 * (i + 1)] for i, n in enumerate(names)}
            tmp.update(im2=tmp["p2"], im4=tmp["p2t"], f1=tmp["ip2"], ft=tmp["ip4"], m2=tmp["wt"], m2t=tmp["et"],
                       m=tmp["p2t"], q2=tmp["ip4"])

            def T(name, c):
                return tmp[name + str(c % 2) if name in ("nd", "no", "ndt", "q1") else name]

            i4 = cst[:, C2_I4:C2_I4 + 512]

            def pr(x, p):
                return x[:, p * P:(p + 1) * P]

            SOLVE = [
                [("p2", "ndt", "nd", "act"), ("p2t", "nd", "ndt", "dve")],
                [("ip4", "p2t", "p2", "plus"), ("wt", "ip2", "q1", "act")],
                [("et", "ip4", "wt", "dve"), ("e", "wt", "ip4", "act")],
                [("m", "et", "no", "act"), ("mt", "no", "et", "dve")],
                [("m2", "mt", "m", "act"), ("m2t", "m", "mt", "dve")],
                [("im4", "m2t", "m2", "plus"), ("f1", "im2", "q2", "act")],
                [("ft", "im4", "f1", "act")],
                [("inv", "e", "ft", "dve")],
            ]
            AFTER = {"p2": ("ip2", ALU.add), "mt": ("q2", ALU.subtract), "m2": ("im2", ALU.add)}
            CHAIN = {0: "r", 1: "x", 2: "t", 3: "y"}
            FRONT = {4: (0,), 5: (1,), 6: (2,), 7: (3,)}

            jobs = Banks()
            for p in range(PAIRS):
                jobs.plan(("bonus", p))
            def plan_front(c, pairs):
                for p in pairs:
                    jobs.plan(("first", c, p))
                    jobs.plan(("second", c, p))

            plan_front(0, range(PAIRS))
            for c in range(NCH + 1):
                for s in range(len(SOLVE)):
                    if c < NCH:
                        for res, *_ in SOLVE[s]:
                            jobs.plan((res, c))
                    if c > 0 and s in CHAIN:
                        jobs.plan((CHAIN[s], c - 1))
                    if c + 1 < NCH and s in FRONT:
                        plan_front(c + 1, FRONT[s])
            for name in ("mean", "var", "g"):
                for p in range(PAIRS):
                    jobs.plan((name, p))

            def wait_operand(pe, jobs, c, x):
                if x in ("nd", "no", "ndt"):
                    pe.wait_ge(*read_of(jobs, ("second", c, PAIRS - 1)))
                elif x == "q1":
                    pe.wait_ge(S["nd_ready"], c + 1)
                elif x in ("ip2", "q2", "im2"):
                    pe.wait_ge(S["sq_plus"], 3 * c + ("ip2", "q2", "im2").index(x) + 1)
                else:
                    pe.wait_ge(*read_of(jobs, (x, c)))

            def chain_pe(pe, jobs, c, what):
                q = c % 2
                b = bank_to_fill(pe, jobs, (what, c))
                if what == "r":
                    pe.wait_ge(S["state_ready"], c + 1)
                    pe.wait_ge(*read_of(jobs, ("first", c, PAIRS - 1)))
                    pe.wait_ge(*read_of(jobs, ("second", c, PAIRS - 1)))
                    pe.wait_ge(S["solved"], PAIRS * (c + 1))
                if what == "x":
                    pe.wait_ge(*read_of(jobs, ("inv", c)))
                    pe.wait_ge(*read_of(jobs, ("r", c)))
                if what == "t":
                    pe.wait_ge(*read_of(jobs, ("x", c)))
                for p in range(PAIRS):
                    out = ps[:, b, p * P:(p + 1) * P]
                    bt, kt, vt = (xt[q][:, p, i * P:(i + 1) * P] for i in range(3))
                    al, rho = xs[q][:, p, 0:P], xs[q][:, p, P:2 * P]
                    mb, gt, mk2 = (m4[q][:, p, i * P:(i + 1) * P] for i in (1, 2, 3))
                    pairs = {"r": [(al, pr(state, p)), (gt, vt)],
                             "x": [(pr(inv[q], p), pr(rbuf, p))],
                             "t": [(bt, pr(xbuf, p)), (kt, vt)],
                             "y": [(pr(state, p), rho), (pr(xbuf, p), mb), (vt, mk2)]}[what]
                    for i, (lhs, rhs) in enumerate(pairs):
                        m = nc.tensor.matmul(out, lhs, rhs, start=(p == 0 and i == 0),
                                             stop=(p == PAIRS - 1 and i == len(pairs) - 1), skip_group_check=True)
                m.then_inc(full[b], 1)

            def expand(pool, c):
                for i, src in enumerate((beta, rk, rv)):
                    for hh in range(2):
                        dst = x3[c % 2][:, i, :].rearrange("p (a b) -> p a b", b=P)[:, :, 64 * hh:64 * hh + 64]
                        nc.gpsimd.tensor_scalar(dst, src[:, :, c * CH:(c + 1) * CH], cst[:, hh:hh + 1], None, ALU.mult)\
                          .then_inc(S["expanded"], 1)

            def expand_act(act, c):
                for src, at in ((alpha, 0), (rr, P)):
                    for hh in range(2):
                        nc.scalar.activation(xs[c % 2][:, :, at + 64 * hh:at + 64 * hh + 64], src[:, :, c * CH:(c + 1) * CH],
                                             ACT.Copy, scale=cst[:, hh:hh + 1]).then_inc(S["alpha_in"], 1)

            def front_pe(pe, jobs, c, pairs):
                pe.wait_ge(S["expanded"], 6 * (c + 1))
                pe.wait_ge(S["alpha_in"], 4 * (c + 1))
                q = c % 2
                for p in pairs:
                    b = bank_to_fill(pe, jobs, ("first", c, p))
                    bt, kt, vv = (pr(x3[q][:, i, :], p) for i in range(3))
                    nc.tensor.matmul(ps[:, b, 0:256], bt, xs[q][:, p, :], start=True, stop=False, skip_group_check=True)
                    nc.tensor.matmul(ps[:, b, 256:512], kt, xs[q][:, p, :], start=False, stop=True, skip_group_check=True)\
                      .then_inc(full[b], 1)
                    b = bank_to_fill(pe, jobs, ("second", c, p))
                    for i, v in enumerate((bt, kt, vv)):
                        nc.tensor.transpose(ps[:, b, i * P:(i + 1) * P], v, ident)
                    nc.tensor.matmul(ps[:, b, 384:512], xs[q][:, p, 0:P], bt, start=True, stop=True,
                                     skip_group_check=True).then_inc(full[b], 1)

            def front_dve(dve, jobs, c, pairs, own):
                for p in pairs:
                    b = bank_filled(dve, jobs, ("first", c, p))
                    own.up(nc.vector.tensor_tensor(pr(T("ndt", c), p), ps[:, b, 0:P], cst[:, C2_NDT:C2_NDT + P], ALU.mult))
                    nc.vector.tensor_tensor(m4[c % 2][:, p, :], ps[:, b, :], cst[:, C2_RW:C2_RW + 512], ALU.mult)\
                      .then_inc(read[b], 1)
                    b = bank_filled(dve, jobs, ("second", c, p))
                    own.up(nc.vector.tensor_tensor(pr(T("nd", c), p), ps[:, b, 384:512], cst[:, C2_ND:C2_ND + P], ALU.mult))
                    dve.wait_ge(*read_of(jobs, ("first", c, p)))
                    nc.vector.tensor_tensor(pr(T("no", c), p), ps[:, b, 384:512], cst[:, C2_NO:C2_NO + P], ALU.mult)\
                      .then_inc(S["solved"], 1)

            def front_act(act, jobs, c, pairs):
                for p in pairs:
                    b = bank_filled(act, jobs, ("second", c, p))
                    act.wait_ge(S["solved"], PAIRS * c + p + 1)
                    nc.scalar.activation(xt[c % 2][:, p, :], ps[:, b, 0:384], ACT.Copy).then_inc(read[b], 1)

            with nc.Block() as block:
                @block.sync
                def _(sy, jobs=jobs):
                    b, n, _ = jobs.at["inv", NCH - 1]
                    sy.wait_ge(full[b], n)
                    fetch_ahead(sy, W2[0], d["w2"], S2_WO, 2048)

                @block.tensor
                def _(pe, jobs=jobs):
                    for p in range(PAIRS):
                        b = bank_to_fill(pe, jobs, ("bonus", p))
                        pe.wait_ge(S["first_masked"], p + 1)
                        nc.tensor.matmul(ps[:, b, :], blk, w4t[:, p, :], start=True, stop=True).then_inc(full[b], 1)
                    front_pe(pe, jobs, 0, range(PAIRS))
                    for c in range(NCH + 1):
                        for s in range(len(SOLVE)):
                            if c < NCH:
                                for res, lhs, rhs, _ in SOLVE[s]:
                                    for x in (lhs, rhs):
                                        wait_operand(pe, jobs, c, x)
                                    b = bank_to_fill(pe, jobs, (res, c))
                                    for p in range(PAIRS):
                                        m = nc.tensor.matmul(ps[:, b, p * P:(p + 1) * P], pr(T(lhs, c), p), pr(T(rhs, c), p),
                                                             start=(p == 0), stop=(p == PAIRS - 1), skip_group_check=True)
                                    m.then_inc(full[b], 1)
                            if c > 0 and s in CHAIN:
                                chain_pe(pe, jobs, c - 1, CHAIN[s])
                            if c + 1 < NCH and s in FRONT:
                                front_pe(pe, jobs, c + 1, FRONT[s])
                    for name, src, sig in (("mean", y, None), ("var", w2t, "squared")):
                        for p in range(PAIRS):
                            b = bank_to_fill(pe, jobs, (name, p))
                            if sig is None:
                                pe.wait_ge(*read_of(jobs, ("y", NCH - 1)))
                            else:
                                pe.wait_ge(S[sig], p + 1)
                            nc.tensor.matmul(ps[:, b, :], blk, src[:, p, :], start=True, stop=True).then_inc(full[b], 1)
                    for p in range(PAIRS):
                        b = bank_to_fill(pe, jobs, ("g", p))
                        nc.tensor.matmul(ps[:, b, :], lora[:, 512 + p * P:512 + (p + 1) * P], gd, start=True, stop=True)\
                          .then_inc(full[b], 1)

                @block.scalar
                def _(act, jobs=jobs):
                    c = -float(np.exp(-0.5))
                    nc.scalar.activation(w2t, since, ACT.Exp, scale=c).then_inc(S["chunk_in"], 1)
                    nc.scalar.activation(w1t, before, ACT.Exp, scale=c).then_inc(S["chunk_in"], 1)
                    nc.scalar.activation(w3t, since, ACT.Exp, scale=-c).then_inc(S["chunk_in"], 1)
                    act.wait_ge(S["scaled_in"], 1)
                    expand_act(act, 0)
                    expand_act(act, 1)
                    front_act(act, jobs, 0, range(PAIRS))
                    for c in range(NCH + 1):
                        for s in range(len(SOLVE)):
                            if c < NCH:
                                for res, _, _, who in SOLVE[s]:
                                    if who == "act":
                                        b = bank_filled(act, jobs, (res, c))
                                        nc.scalar.activation(T(res, c), ps[:, b, :], ACT.Copy).then_inc(read[b], 1)
                            if c > 0 and s in CHAIN:
                                what = CHAIN[s]
                                if what in "rx":
                                    b = bank_filled(act, jobs, (what, c - 1))
                                    nc.scalar.activation(rbuf if what == "r" else xbuf, ps[:, b, :], ACT.Copy,
                                                         scale=-1.0 if what == "r" else 1.0).then_inc(read[b], 1)
                                if what == "y":
                                    b = bank_filled(act, jobs, (what, c - 1))
                                    if c + 1 < NCH:
                                        expand_act(act, c + 1)
                                    src = ps[:, b, :].rearrange("p (a b) -> p a b", b=P)
                                    t = slice((c - 1) * CH, c * CH)
                                    nc.scalar.activation(y[0:64, :, t], src[0:64, :, 0:64], ACT.Copy)
                                    nc.scalar.activation(y[64:128, :, t], src[64:128, :, 64:128], ACT.Copy).then_inc(read[b], 1)
                            if c + 1 < NCH and s in FRONT:
                                front_act(act, jobs, c + 1, FRONT[s])
                    for p in range(PAIRS):
                        act.wait_ge(*read_of(jobs, ("mean", p)))
                        nc.scalar.activation(w2t[:, p, :], w1t[:, p, :], ACT.Square).then_inc(S["squared"], 1)
                    for p in range(PAIRS):
                        act.wait_ge(*read_of(jobs, ("var", p)))
                        nc.scalar.activation(w3t[:, p, :], w3t[:, p, :], ACT.Sqrt).then_inc(S["root"], 1)
                    for p in range(PAIRS):
                        act.wait_ge(*read_of(jobs, ("g", p)))
                        nc.scalar.activation(o2_hi[:, 4 + p, :], w1t[:, p, :], ACT.Copy).then_inc(S["o_kept"], 1)

                @block.gpsimd
                def _(pool, jobs=jobs):
                    nc.gpsimd.memset(state, 0.0).then_inc(S["state_ready"], 1)
                    pool.wait_ge(S["scaled_in"], 2)
                    expand(pool, 0)
                    for c in range(NCH):
                        if c + 1 < NCH:
                            expand(pool, c + 1)
                        pool.wait_ge(S["solved"], PAIRS * (c + 1))
                        nc.gpsimd.tensor_tensor(T("q1", c), i4, T("ndt", c), ALU.subtract).then_inc(S["nd_ready"], 1)

                @block.vector
                def _(dve, jobs=jobs):
                    own = Signal(dve_own)
                    chain = lambda i: dve.wait_ge(*own.up(i))
                    for p in range(PAIRS):
                        nc.vector.scalar_tensor_tensor(w4t[:, p, :], rr[:, p, :], prm_col(P2_RK + p), rk[:, p, :],
                                                       ALU.mult, ALU.mult).then_inc(S["first_masked"], 1)
                    dve.wait_ge(S["chunk_in"], 1)
                    dve.wait_ge(S["first_masked"], PAIRS)
                    chain(nc.vector.tensor_copy(dend, w2t[:, :, CH - 1:L:CH]))
                    chain(nc.vector.tensor_tensor(rr, rr, w2t, ALU.mult))
                    dve.wait_ge(S["chunk_in"], 2)
                    nc.vector.tensor_tensor(alpha, alpha, w1t, ALU.mult).then_inc(S["scaled_in"], 1)
                    dve.wait_ge(S["chunk_in"], 3)
                    chain(nc.vector.tensor_tensor(beta, beta, w3t, ALU.mult))
                    dve.wait_ge(S["scaled_in"], 1)
                    nc.vector.tensor_tensor(rk, rk, w3t, ALU.mult).then_inc(S["scaled_in"], 1)
                    for p in range(PAIRS):
                        b = bank_filled(dve, jobs, ("bonus", p))
                        nc.vector.tensor_tensor(bonus[:, p, :], ps[:, b, :], rv[:, p, :], ALU.mult).then_inc(read[b], 1)
                    for p in range(PAIRS):
                        dve.wait_ge(*read_of(jobs, ("bonus", p)))
                    dve.wait_ge(S["scaled_in"], 2)
                    front_dve(dve, jobs, 0, range(PAIRS), own)
                    for c in range(NCH + 1):
                        for s in range(len(SOLVE)):
                            if c < NCH:
                                for res, _, _, who in SOLVE[s]:
                                    if who != "act":
                                        b = bank_filled(dve, jobs, (res, c))
                                        dst = inv[c % 2] if res == "inv" else T(res, c)
                                        if who == "plus":
                                            i = nc.vector.tensor_tensor(dst, ps[:, b, :], i4, ALU.add)
                                        else:
                                            i = nc.vector.tensor_copy(dst, ps[:, b, :])
                                        i.then_inc(read[b], 1)
                                for res, *_ in SOLVE[s]:
                                    if res in AFTER:
                                        dst, op = AFTER[res]
                                        dve.wait_ge(*read_of(jobs, (res, c)))
                                        nc.vector.tensor_tensor(tmp[dst], i4, tmp[res], op).then_inc(S["sq_plus"], 1)
                            if c > 0 and s in CHAIN and CHAIN[s] == "y":
                                b, n, _ = jobs.at["y", c - 1]
                                dve.wait_ge(full[b], n)
                                b = bank_filled(dve, jobs, ("t", c - 1))
                                nc.vector.tensor_tensor(state, state, ps[:, b, :], ALU.add).then_inc(read[b], 1)
                                dve.wait_ge(*read_of(jobs, ("t", c - 1)))
                                st = state.rearrange("p (a b) -> p a b", b=P)
                                nc.vector.tensor_tensor(st, st, dend[:, :, c - 1:c].to_broadcast([P, PAIRS, P]), ALU.mult)\
                                  .then_inc(S["state_ready"], 1)
                            if c + 1 < NCH and s in FRONT:
                                front_dve(dve, jobs, c + 1, FRONT[s], own)
                    for p in range(PAIRS):
                        b = bank_filled(dve, jobs, ("mean", p))
                        nc.vector.scalar_tensor_tensor(w1t[:, p, :], ps[:, b, :], -1.0 / HD, y[:, p, :], ALU.mult, ALU.add)\
                          .then_inc(read[b], 1)
                    for p in range(PAIRS):
                        b = bank_filled(dve, jobs, ("var", p))
                        nc.vector.tensor_scalar(w3t[:, p, :], ps[:, b, :], 1.0 / HD, 64e-5, ALU.mult, ALU.add).then_inc(read[b], 1)
                    dve.wait_ge(S["root"], PAIRS)
                    chain(nc.vector.reciprocal(w3t, w3t))
                    for p in range(PAIRS):
                        i = own.up(nc.vector.scalar_tensor_tensor(w1t[:, p, :], w1t[:, p, :], prm_col(P2_GNG + p), w3t[:, p, :],
                                                                  ALU.mult, ALU.mult))
                    dve.wait_ge(*i)
                    for p in range(PAIRS):
                        i = own.up(nc.vector.scalar_tensor_tensor(w1t[:, p, :], w1t[:, p, :], prm_col(P2_GNB + p), bonus[:, p, :],
                                                                  ALU.add, ALU.add))
                    dve.wait_ge(*i)
                    for p in range(PAIRS):
                        b = bank_filled(dve, jobs, ("g", p))
                        nc.vector.tensor_tensor(w1t[:, p, :], w1t[:, p, :], ps[:, b, :], ALU.mult).then_inc(read[b], 1)
                    for p in range(PAIRS):
                        dve.wait_ge(S["o_kept"], p + 1)
                        nc.vector.tensor_tensor(o2_lo[:, 4 + p, :], w1t[:, p, :], o2_hi[:, 4 + p, :].bitcast(F32), ALU.subtract)\
                          .then_inc(S["ln_out"], 1)
            close_block()

            hid2_hi, hid2_lo = place("hid2_hi", 17352, FF2, L, dt=F32R), place("hid2_lo", 28616, FF2, L, dt=F32R)
            cv2, ge = place("cv2", 52168, L)[:, :], place("ge", 52680, L)[:, :]
            nrm, nx = place("nrm", 17352, L)[:, :], place("nx", 17864, L)[:, :]
            lsq = place("lsq", 18376, DC, L)
            N_ALL = 4 + FF2 + FF2 // 2
            GU, GD = 4, 4 + FF2
            ROUNDS = 5
            jobs = Banks(start=1)
            for n in range(DC):
                jobs.plan(("wo", n))
            for name in ("mean1", "var1"):
                jobs.plan(name)
            jobs.plan_body([(w, j) for j in range(4) for w in ("conv", "up")], ROUNDS)
            for j in range(FF2 - 4 * ROUNDS):
                for w in ("conv", "up"):
                    jobs.plan((w, 4 + j))
            for n in range(DC):
                jobs.plan(("down", n))
            for name in ("mean2", "var2"):
                jobs.plan(name)

            def ln_pe(pe, name, squared):
                b = bank_to_fill(pe, jobs, name)
                for c in range(DC):
                    pe.wait_ge(S["squared" if squared else "h_ready"], (squared - 1 if squared else 0) + c + 1)
                    m = nc.tensor.matmul(ps[:, b, :], ones, (lsq if squared else h)[:, c, :], start=(c == 0), stop=(c == DC - 1))
                m.then_inc(full[b], 1)

            def ln_act(act, i):
                for c in range(DC):
                    act.wait_ge(S["centered"], DC * i + c + 1)
                    nc.scalar.activation(lsq[:, c, :], h[:, c, :], ACT.Square).then_inc(S["squared"], 1)
                act.wait_ge(*read_of(jobs, f"var{i + 1}"))
                nc.scalar.activation(nrm, nrm, ACT.Sqrt).then_inc(S["root"], 1)
                for c in range(DC):
                    act.wait_ge(S["normed"], DC * i + c + 1)
                    g = (P2_LN1B, P2_LN2B)[i] + c
                    nc.scalar.activation(h[:, c, :], h[:, c, :], ACT.Identity, bias=prm_col(g)).then_inc(S["ln_out"], 1)
                    if i == 0 and c > 0:
                        act.wait_ge(S["ln_out"], c)
                        nc.scalar.activation(u_hi[:, c - 1, :], h[:, c - 1, :], ACT.Copy).then_inc(S["u_hi"], 1)
                if i == 0:
                    act.wait_ge(S["ln_out"], DC)
                    nc.scalar.activation(u_hi[:, DC - 1, :], h[:, DC - 1, :], ACT.Copy).then_inc(S["u_hi"], 1)

            def ln_dve(dve, i, own):
                b = bank_filled(dve, jobs, f"mean{i + 1}")
                nc.vector.tensor_scalar(nx, ps[:, b, :], -1.0 / D, None, ALU.mult).then_inc(read[b], 1)
                dve.wait_ge(*read_of(jobs, f"mean{i + 1}"))
                for c in range(DC):
                    nc.vector.tensor_tensor(h[:, c, :], h[:, c, :], nx, ALU.add).then_inc(S["centered"], 1)
                b = bank_filled(dve, jobs, f"var{i + 1}")
                nc.vector.tensor_scalar(nrm, ps[:, b, :], 1.0 / D, 1e-5, ALU.mult, ALU.add).then_inc(read[b], 1)
                dve.wait_ge(S["root"], i + 1)
                dve.wait_ge(*own.up(nc.vector.reciprocal(nrm, nrm)))
                for c in range(DC):
                    g = (P2_LN1G, P2_LN2G)[i] + c
                    nc.vector.scalar_tensor_tensor(h[:, c, :], h[:, c, :], prm_col(g), nrm, ALU.mult, ALU.mult)\
                      .then_inc(S["normed"], 1)

            def at(x, k):
                if isinstance(k, int):
                    return x[:, k, :]
                return x[:, bass.ds(k, 1), :].rearrange("p a c -> p (a c)")

            def col(c, k):
                return prm[:, c + k:c + k + 1] if isinstance(k, int) else prm[:, bass.ds(k + c, 1)]

            with nc.Block() as block:
                @block.sync
                def _(sy, jobs=jobs):
                    def fetch(g, j):
                        sy.dma_start(W2[0][:, j, :],
                                     d["w2"][bass.ds(layer, 1), bass.ds(g, 1), :, 0:2048].rearrange("a b p c -> p (a b c)"))\
                          .then_inc(landed[j], 16)

                    come_ahead(sy)
                    with sy.Fori(1, N_ALL // 2) as it:
                        for j in range(2):
                            sy.wait_ge(S["w_lo"], it * 2 + (j - 1))
                            fetch(it * 2 + (S2_WO + j), j)
                    sy.wait_ge(S["w_lo"], N_ALL - 2)
                    fetch(S2_WO + N_ALL - 1, 0)

                @block.tensor
                def _(pe, jobs=jobs):
                    for b in range(8):
                        pe.sem_inc(full[b], 1)
                        pe.sem_inc(read[b], 1)
                    for n in range(DC):
                        if n % 2 == 0:
                            pe.wait_ge(S["w_lo"], n // 2 + 1)
                        dense_tile(pe, jobs, ("wo", n), W2, n // 2, n % 2, x=(o2_hi, o2_lo))
                    ln_pe(pe, "mean1", 0)
                    ln_pe(pe, "var1", 1)
                    pe.wait_ge(S["u_lo"], DC)
                    with pe.Fori(0, ROUNDS) as it:
                        for j in range(4):
                            pe.wait_ge(S["w_lo"], it * 4 + (GU + j + 1))
                            dense_tile(pe, jobs, ("conv", j), W2, j, 0, it=it)
                            dense_tile(pe, jobs, ("up", j), W2, j, 1, it=it)
                    for j in range(2):
                        pe.wait_ge(S["w_lo"], GU + 4 * ROUNDS + j + 1)
                        dense_tile(pe, jobs, ("conv", 4 + j), W2, j, 0)
                        dense_tile(pe, jobs, ("up", 4 + j), W2, j, 1)
                    for k in range(FF2 // 2):
                        pe.wait_ge(S["w_lo"], GD + k + 1)
                        w_hi, w_lo = (w[:, k % 2, :].rearrange("p (k c) -> p k c", c=D) for w in W2[1:])
                        for c in range(2):
                            t = 2 * k + c
                            pe.wait_ge(S["hidden_kept"], t + 2)
                            for n in range(DC):
                                b = jobs.at["down", n][0]
                                if t == 0:
                                    bank_to_fill(pe, jobs, ("down", n))
                                f = slice(n * P, (n + 1) * P)
                                m = product3(ps[:, b, :], w_hi[:, c, f], w_lo[:, c, f], hid2_hi[:, t, :], hid2_lo[:, t, :],
                                             t == 0, t == FF2 - 1)
                                if t == FF2 - 1:
                                    m.then_inc(full[b], 1)
                        if k < FF2 // 2 - 1:
                            m.then_inc(S["slab_used"], 1)
                    b = bank_to_fill(pe, jobs, "mean2")
                    for c in range(DC):
                        pe.wait_ge(*read_of(jobs, ("down", c)))
                        m = nc.tensor.matmul(ps[:, b, :], ones, h[:, c, :], start=(c == 0), stop=(c == DC - 1))
                    m.then_inc(full[b], 1)
                    ln_pe(pe, "var2", DC + 1)

                @block.scalar
                def _(act, jobs=jobs):
                    act.sem_inc(S["gelu"], 1)
                    for g in range(GU + 2):
                        act.wait_ge(landed[g % 2], 16 * (g // 2 + 1))
                        if g >= 2:
                            b, n, _ = jobs.at["wo", 2 * (g - 2) + 1]
                            act.wait_ge(full[b], n)
                        split_w_hi(act, W2, g, None)
                    ln_act(act, 0)

                    def pair(j, k, it, seq):
                        b = bank_filled(act, jobs, ("conv", j), it)
                        act.wait_ge(S["gelu"], seq + 1)
                        nc.scalar.activation(cv2, ps[:, b, :], ACT.Identity, bias=col(P2_CB, k),
                                             scale=col(P2_CW + 2 * FF2, k)).then_inc(S["mixed"], 1)
                        act.wait_ge(S["shifted"], seq + 1)
                        act.wait_ge(S["hidden_kept"], seq + 1)
                        nc.scalar.activation(ge, cv2, ACT.Gelu).then_inc(S["gelu"], 1)
                        act.wait_ge(*read_of(jobs, ("up", j), it))
                        nc.scalar.activation(at(hid2_hi, k), ge, ACT.Copy).then_inc(S["m_hi"], 1)
                        landings = (GU + j + 2) // 2 + 1
                        act.wait_ge(landed[j % 2], 16 * (2 * ROUNDS + landings - 2) if it is None else it * 32 + 16 * landings)
                        split_w_hi(act, W2, j, None)

                    with act.Fori(0, ROUNDS) as it:
                        for j in range(4):
                            pair(j, it * 4 + j, it, it * 4 + j)
                    for j in range(2):
                        pair(4 + j, 4 * ROUNDS + j, None, 4 * ROUNDS + j)
                    for g in range(GD + 2, N_ALL):
                        act.wait_ge(landed[g % 2], 16 * (g // 2 + 1))
                        act.wait_ge(S["slab_used"], g - GD - 1)
                        split_w_hi(act, W2, g, None)
                    ln_act(act, 1)

                @block.gpsimd
                def _(pool, jobs=jobs):
                    pool.sem_inc(S["hidden_kept"], 1)
                    for c in range(DC):
                        pool.wait_ge(S["u_hi"], c + 1)
                        nc.gpsimd.tensor_tensor(u_lo[:, c, :], h[:, c, :], u_hi[:, c, :].bitcast(F32), ALU.subtract)\
                          .then_inc(S["u_lo"], 1)
                    with pool.Fori(0, ROUNDS) as it:
                        for j in range(4):
                            k = it * 4 + j
                            pool.wait_ge(S["m_hi"], it * 4 + (j + 1))
                            nc.gpsimd.tensor_tensor(at(hid2_lo, k), ge, at(hid2_hi, k).bitcast(F32), ALU.subtract)\
                              .then_inc(S["hidden_kept"], 1)
                    for k in range(4 * ROUNDS, FF2):
                        pool.wait_ge(S["m_hi"], k + 1)
                        nc.gpsimd.tensor_tensor(hid2_lo[:, k, :], ge, hid2_hi[:, k, :].bitcast(F32), ALU.subtract)\
                          .then_inc(S["hidden_kept"], 1)

                @block.vector
                def _(dve, jobs=jobs):
                    own = Signal(dve_own)
                    split_w_lo(dve, W2, 0, 1)
                    split_w_lo(dve, W2, 1, 2)
                    for n in range(DC):
                        b = bank_filled(dve, jobs, ("wo", n))
                        nc.vector.scalar_tensor_tensor(h[:, n, :], h[:, n, :], ALPHA, ps[:, b, :], ALU.mult, ALU.add)\
                          .then_inc(read[b], 1)
                        dve.wait_ge(*read_of(jobs, ("wo", n)))
                        dve.sem_inc(S["h_ready"], 1)
                        if n % 2 == 1:
                            split_w_lo(dve, W2, n // 2, n // 2 + 3)
                    ln_dve(dve, 0, own)

                    def pair(j, k, it, seq):
                        x = cv2
                        b = bank_filled(dve, jobs, ("conv", j), it)
                        dve.wait_ge(S["mixed"], seq + 1)
                        nc.vector.scalar_tensor_tensor(x[:, 1:L], ps[:, b, 0:L - 1], col(P2_CW + FF2, k), x[:, 1:L],
                                                       ALU.mult, ALU.add).then_inc(dve_own, 1)
                        dve.wait_ge(dve_own, seq + 2)
                        nc.vector.scalar_tensor_tensor(x[:, 2:L], ps[:, b, 0:L - 2], col(P2_CW, k), x[:, 2:L],
                                                       ALU.mult, ALU.add).then_inc(read[b], 1)
                        dve.wait_ge(*read_of(jobs, ("conv", j), it))
                        dve.sem_inc(S["shifted"], 1)
                        b = bank_filled(dve, jobs, ("up", j), it)
                        dve.wait_ge(S["gelu"], seq + 2)
                        nc.vector.tensor_tensor(ge, ge, ps[:, b, :], ALU.mult).then_inc(read[b], 1)
                        split_w_lo(dve, W2, j, seq + GU + 3)

                    with dve.Fori(0, ROUNDS) as it:
                        for j in range(4):
                            pair(j, it * 4 + j, it, it * 4 + j)
                    for j in range(2):
                        pair(4 + j, 4 * ROUNDS + j, None, 4 * ROUNDS + j)
                    own.n += FF2
                    for g in range(GD + 2, N_ALL):
                        split_w_lo(dve, W2, g, g + 1)
                    for n in range(DC):
                        b = bank_filled(dve, jobs, ("down", n))
                        nc.vector.scalar_tensor_tensor(h[:, n, :], h[:, n, :], ALPHA, ps[:, b, :], ALU.mult, ALU.add)\
                          .then_inc(read[b], 1)
                    for n in range(DC):
                        dve.wait_ge(*read_of(jobs, ("down", n)))
                    ln_dve(dve, 1, own)
            close_block()

        with nc.Block() as block:
            @block.sync
            def _(sy):
                for c in range(DC):
                    sy.dma_start(d["out"][c], h[:, c, :]).then_inc(stored, 16)
                sy.wait_ge(stored, 16 * DC)


def _slabs(w, cols):
    w = w[:, cols]
    k, n = w.shape
    w = w.reshape(k // P, P, n // 256, 256).transpose(2, 1, 0, 3)
    return w.reshape(n // 256, P, (k // P) * 256)


def _padded(x, width=SLOT):
    out = np.zeros(x.shape[:-1] + (width,), x.dtype)
    out[..., :x.shape[-1]] = x
    return out


def _down_slabs(w):
    n = w.shape[0] // 256
    return w.reshape(n, 2, P, D).transpose(0, 2, 1, 3).reshape(n, P, 2 * D)


def _first_weights(w_in, w_a, w_b, w_c, w_o, w_up, w_down):
    o = W_OFF
    r = lambda name, n, at=0: list(range(o[name] + at, o[name] + at + n))
    qk = (r("ik", 64) * 2 + r("aq", 384) + r("ak", 64) * 2 + r("iq", 512) + r("bq", 768) + r("bk", 768) + r("cq", 512)
          + r("ck", 64) * 2 + r("ck", 64, 64) * 2)
    assert len(qk) == N_QK * P
    qk += [0] * P
    v = r("bv", 768) + r("av", 64) + r("cv", 128) + r("iw", 8)
    v += [0] * (1024 - len(v))
    out = [_padded(_slabs(w_in, qk)), _padded(_slabs(w_in, v))]
    for n in range(DC):
        cut = lambda w, c0: w[:, c0 + n * P:c0 + (n + 1) * P].reshape(-1, P, P).transpose(1, 0, 2).reshape(P, -1)
        g = [cut(w_in, o["gates"] + j * D) for j in range(3)]
        out.append(_padded(np.concatenate(g[:2], axis=1))[None])
        out.append(np.concatenate([g[2], cut(w_a, 0), cut(w_b, 0), cut(w_c, 0)], axis=1)[None])
    out.append(_padded(_slabs(w_o, list(range(D)))))
    for half in range(2):
        ff = range(half * 2 * D, (half + 1) * 2 * D)
        out.append(_padded(_slabs(w_up, list(ff))))
        out.append(_padded(_down_slabs(w_down[ff[0]:ff[-1] + 1])))
    return np.concatenate(out)


def _columns(v):
    return v.reshape(-1, P).T


def _first_constants():
    c = np.zeros((P, N_C1), np.float32)
    p = np.arange(P)
    c[:, C1_INV] = np.power(np.float32(10000.0), -(p % 32).astype(np.float32) / np.float32(32)).astype(np.float32)
    c[:, C1_SIGN] = np.where(p % 64 < 32, -1.0, 1.0)
    c[:, C1_ID:C1_ID + P] = np.eye(P)
    c[:, C1_ONE:C1_ONE + P] = 1.0
    c[:, C1_BLK:C1_BLK + P] = p[:, None] // 64 == p[None] // 64
    off = lambda on: np.where(on, 0.0, NEG)
    t, s = p[:, None], p[None]
    c[:, C1_CAUSAL:C1_CAUSAL + P] = off(s <= t)
    s2 = np.arange(2 * P)[None] - P
    c[:, C1_WIN:C1_WIN + 2 * P] = off((s2 <= t) & (s2 > t - 128))
    for r in range(4):
        back = 4 * t + r - np.arange(L)[None]
        c[:, C1_DIL + r * L:C1_DIL + (r + 1) * L] = off((back >= 0) & (back <= 128))
    c[:, C1_DIL16:C1_DIL16 + P] = off(s <= t)
    c[:, C1_DIL16 + P:C1_DIL16 + 2 * P] = off((s <= t) & ((t - s) % 4 == 0))
    return c


def _second_weights(w_in, w_uq, w_ukv, w2, a2, g2, w_o, w_up, w_down):
    sb, mla, rw = 0, 3 * SB_HEADS * HD, 3 * SB_HEADS * HD + Q_LORA + P + RD
    r = lambda at, n: list(range(at, at + n))
    wz = np.concatenate([w_in, np.zeros((D, 1), w_in.dtype)], axis=1)
    z = [w_in.shape[1]]
    kr = mla + Q_LORA + P
    cols = (r(sb, 512) + r(mla, Q_LORA) + r(kr, RD) + z * 32 + r(mla + Q_LORA, P)
            + z * 64 + r(kr + RD // 2, RD // 2) + r(kr, RD // 2) + z * 32 + r(rw, 14 * P))
    assert len(cols) == N_T2 * P
    out = [_padded(_slabs(wz, cols)), _padded(_slabs(wz, r(sb + 512, 256)))]
    swapped = [QW * hd + c for hd in range(MLA_HEADS) for c in r(0, NOPE) + r(NOPE + RD // 2, RD // 2) + r(NOPE, RD // 2)]
    uq = np.concatenate([w_uq, w_uq[:, swapped]], axis=1)
    uq = np.concatenate([uq, np.zeros((2 * P - Q_LORA, uq.shape[1]), uq.dtype)])
    uq = uq.reshape(2, P, -1).transpose(1, 0, 2).reshape(P, -1)
    keys = [2 * HD * hd + c for hd in range(MLA_HEADS) for c in range(HD)]
    ukv = w_ukv[:, keys + [c + HD for c in keys]]
    out.append(_padded(np.concatenate([uq, ukv], axis=1))[None])
    out.append(_padded(np.concatenate([np.concatenate([w2, a2]), g2], axis=1))[None])
    out.append(_padded(_slabs(w_o, r(0, D))))
    ff = FF2 * P
    out.append(_padded(_slabs(w_up, [c for n in range(FF2) for c in r(n * P, P) + r(ff + n * P, P)])))
    out.append(_padded(_down_slabs(w_down)))
    return np.concatenate(out)


def _second_constants():
    c = np.zeros((P, N_C2), np.float32)
    c[:, 2:C2_CAUSAL] = _first_constants()[:, 2:C2_CAUSAL]
    a, b = np.arange(P)[:, None], np.arange(P)[None]
    c[:HD, 0] = 1.0
    c[HD:, 1] = 1.0
    c[:, C2_CAUSAL + 3 * P:C2_CAUSAL + 4 * P] = np.where(b <= a, 0.0, NEG)
    c[:, C2_SBKEEP:C2_SBKEEP + P] = a < b
    c[:, C2_SBNEG:C2_SBNEG + P] = np.where(a < b, 0.0, NEG)
    c[:, C2_TRI:C2_TRI + P] = a >= b
    same = a // CH == b // CH
    for i, on in enumerate((a < b, a <= b) * 2):
        c[:, C2_RW + i * P:C2_RW + (i + 1) * P] = on & same
    near = a // 8 == b // 8
    c[:, C2_ND:C2_ND + P] = (b < a) & near
    c[:, C2_NO:C2_NO + P] = (b < a) & same & ~near
    c[:, C2_NDT:C2_NDT + 4 * P] = np.tile((a < b) & near, (1, 4))
    c[:, C2_I4:C2_I4 + 4 * P] = np.tile(np.eye(P), (1, 4))
    c[:, C2_RESET:C2_RESET + L] = np.arange(L) % CH != 0
    freq = (np.float32(1) / np.power(np.float32(10000), np.arange(0, RD, 2, dtype=np.float32) / np.float32(RD))).astype(np.float32)
    ang = (np.arange(L, dtype=np.float32)[None] * freq[:, None]).astype(np.float32).astype(np.float64)
    c[64:96, C2_COS:C2_COS + L] = np.tile(np.cos(ang), (2, 1))
    c[64:96, C2_SIN:C2_SIN + L] = np.concatenate([-np.sin(ang), np.sin(ang)])
    return c


def layout(x):
    f = lambda n: np.ascontiguousarray(np.asarray(x[n]))
    a = {}
    a["x"] = f("x")[0].T.reshape(DC, P, L)
    a["pos"] = np.broadcast_to(f("positions").astype(np.int32), (P, L))
    a["cst1"] = _first_constants()
    a["w1"] = np.stack([_first_weights(*(f(n)[l] for n in ("w_in", "w_a", "w_b", "w_c", "w_o", "w_up", "w_down")))
                        for l in range(DEPTH)])
    assert a["w1"].shape[1] == N_S1
    prm = np.zeros((DEPTH, P, N_P1), np.float32)
    for l in range(DEPTH):
        prm[l, :, P1_ATTN:P1_ATTN + 8] = _columns(f("attn_norm")[l])
        prm[l, :, P1_MLP:P1_MLP + 8] = _columns(f("mlp_norm")[l])
        prm[l, :, P1_IK] = np.tile(f("idx_k_norm")[l], 2)
        prm[l, :, P1_SINK:P1_SINK + 8] = f("sinks")[l][None]
        prm[l, :, P1_FINAL:P1_FINAL + 8] = _columns(f("final_norm"))
    a["prm1"] = prm
    a["cst2"] = _second_constants()
    names = ("w_in", "mla_w_uq", "mla_w_ukv", "rwkv_w2", "rwkv_a2", "rwkv_g2", "w_o", "ffn_w_up", "ffn_w_down")
    a["w2"] = np.stack([_second_weights(*(f(n + "_2")[l] for n in names)) for l in range(DEPTH)])
    assert a["w2"].shape[1] == N_S2
    prm = np.zeros((DEPTH, P, N_P2), np.float32)
    for l in range(DEPTH):
        for n, at in (("rwkv_mu", P2_MU), ("rwkv_w0", P2_W0), ("rwkv_a0", P2_A0), ("rwkv_k_k", P2_KK), ("rwkv_k_a", P2_KA),
                      ("rwkv_r_k", P2_RK), ("rwkv_gn_g", P2_GNG), ("rwkv_gn_b", P2_GNB), ("mla_kv_norm", P2_KVN),
                      ("ln1_g", P2_LN1G), ("ln1_b", P2_LN1B), ("ln2_g", P2_LN2G), ("ln2_b", P2_LN2B),
                      ("ffn_conv_w", P2_CW), ("ffn_conv_b", P2_CB)):
            v = _columns(f(n + "_2")[l].reshape(-1))
            prm[l, :, at:at + v.shape[1]] = v
        prm[l, :, P2_QN] = f("mla_q_norm_2")[l][0:P]
        prm[l, 0:Q_LORA - P, P2_QN + 1] = f("mla_q_norm_2")[l][P:]
    a["prm2"] = prm
    return {n: np.ascontiguousarray(v) for n, v in a.items()}


def kernel(**inputs):
    import concourse.bacc as bacc
    from concourse.bass_utils import run_bass_kernel_spmd

    nc = bacc.Bacc("TRN2", target_bir_lowering=False, num_devices=1)
    arrays, d = {}, {}
    for name, a in layout(inputs).items():
        arrays[f"in_{name}"] = a
        d[name] = nc.dram_tensor(f"in_{name}", a.shape, mybir.dt.from_np(a.dtype), kind="ExternalInput").ap()
    d["out"] = nc.dram_tensor("out", (DC, P, L), F32, kind="ExternalOutput").ap()
    build(nc, d)
    r = run_bass_kernel_spmd(nc, [arrays], core_ids=[0])
    out = r.results[0]["out"].reshape(D, L)
    return np.ascontiguousarray(out.T)[None]
```
